# Optimizing a Trainium2 kernel written in Bass

```python
import math
import jax, jax.numpy as jnp
from jax import lax
import numpy as np

D_MODEL = 1024
BATCH = 1
SEQ = 128
DEPTH = 1
DEC_BATCH = 1
DEC_SEQ = 512
PAST_LEN = 128

GRID_W = 64
GDN_H = 4
GDN_DK = 128
GDN_DV = 128
GDN_W = GDN_H * GDN_DV
HG_H = 4
HG_DK = 64
HG_DV = 64
HG_W = HG_H * HG_DV
F_MIN = 1e-30
RG_W = 256
RG_BLOCKS = 4
RG_BW = RG_W // RG_BLOCKS
RG_C = 8.0
MIX_W = GDN_W + HG_W + RG_W
CONV_K = 4
CONV_LEFT = 2
CHUNK = 64
N_EXPERTS = 16
N_GROUPS = 4
EXPERTS_PER_GROUP = N_EXPERTS // N_GROUPS
TOP_K = 2
D_FF = 512
EPS = 1e-6
IN_SIZES = (3 * GDN_W, GDN_W, 2 * GDN_H, 2 * GDN_H, HG_H * HG_DK, HG_W, HG_W, 2 * HG_H * HG_DK, RG_W, RG_W)
N_IN = sum(IN_SIZES)

kernel_name = 'hybrid_gdn_hgrn2_rglru_moe_diffusion_step'

def _rms(x, w):
    xf = x.astype(jnp.float32)
    y = xf * lax.rsqrt(jnp.mean(xf * xf, axis=-1, keepdims=True) + EPS)
    return (y * w.astype(jnp.float32)).astype(x.dtype)

def _l2norm(x):
    xf = x.astype(jnp.float32)
    return xf * lax.rsqrt(jnp.sum(xf * xf, axis=-1, keepdims=True) + EPS)

def _dwconv(x, w):
    return lax.conv_general_dilated(
        x, w[:, None, :].astype(x.dtype), window_strides=(1,),
        padding=[(CONV_LEFT, CONV_K - 1 - CONV_LEFT)],
        dimension_numbers=('NWC', 'WIO', 'NWC'), feature_group_count=x.shape[-1])

def _masked_exp(mask, diff):
    return jnp.where(mask, jnp.exp(jnp.where(mask, diff, 0.0)), 0.0)

def _gdn_step(S, inp):
    q, k, v, la, beta = inp
    incl = jnp.tril(jnp.ones((CHUNK, CHUNK), bool))
    g = jnp.cumsum(la, axis=-1)
    dec = _masked_exp(incl, g[..., :, None] - g[..., None, :])
    strict = jnp.where(jnp.eye(CHUNK, dtype=bool), 0.0, dec)
    lmat = beta[..., :, None] * jnp.einsum('bhid,bhjd->bhij', k, k) * strict
    m = jnp.eye(CHUNK, dtype=jnp.float32) + lmat
    eg = jnp.exp(g)
    rhs = jnp.concatenate([beta[..., None] * v, (beta * eg)[..., None] * k], axis=-1)
    sol = lax.linalg.triangular_solve(m, rhs, left_side=True, lower=True, unit_diagonal=True)
    u = sol[..., :GDN_DV] - jnp.einsum('bhck,bhkv->bhcv', sol[..., GDN_DV:], S)
    attn = jnp.einsum('bhik,bhjk->bhij', q, k) * dec
    o = jnp.einsum('bhck,bhkv->bhcv', q * eg[..., None], S) + jnp.einsum('bhij,bhjv->bhiv', attn, u)
    g_end = g[..., -1:]
    S_new = jnp.exp(g_end)[..., None] * S + jnp.einsum('bhck,bhcv->bhkv', k * jnp.exp(g_end - g)[..., None], u)
    return S_new, o

def _hgrn_step(S, inp):
    q, k, v, lf = inp
    incl = jnp.tril(jnp.ones((CHUNK, CHUNK), bool))[:, :, None]
    b = jnp.cumsum(lf, axis=2)
    dec = _masked_exp(incl, b[:, :, :, None, :] - b[:, :, None, :, :])
    attn = jnp.einsum('bhtd,bhjd,bhtjd->bhtj', q, k, dec)
    o = jnp.einsum('bhtd,bhdv->bhtv', q * jnp.exp(b), S) + jnp.einsum('bhtj,bhjv->bhtv', attn, v)
    b_end = b[:, :, -1:]
    S_new = jnp.exp(b_end[:, :, 0])[..., None] * S + jnp.einsum('bhjd,bhjv->bhdv', k * jnp.exp(b_end - b), v)
    return S_new, o

def _chunk_scan(step, s0, seqs):
    T = seqs[0].shape[2]
    n = T // CHUNK
    xs = tuple(jnp.moveaxis(s.reshape(s.shape[:2] + (n, CHUNK) + s.shape[3:]), 2, 0) for s in seqs)
    s_fin, o = lax.scan(step, s0.astype(jnp.float32), xs)
    o = jnp.moveaxis(o, 0, 2)
    return o.reshape(o.shape[:2] + (T, o.shape[-1])), s_fin

def _bidirectional(step, s0, fwd_seqs, bwd_seqs):
    o_f, s_f = _chunk_scan(step, s0[:, 0], fwd_seqs)
    o_b, s_b = _chunk_scan(step, s0[:, 1], tuple(jnp.flip(s, 2) for s in bwd_seqs))
    return o_f + jnp.flip(o_b, 2), jnp.stack([s_f, s_b], axis=1)

def _rglru(u, w_gate, b_gate, lam, h0):
    B, T, _ = u.shape
    xb = u.reshape(B, T, RG_BLOCKS, RG_BW)
    gates = jax.nn.sigmoid(jnp.einsum('btnk,gnkj->gbtnj', xb, w_gate.astype(jnp.float32)).reshape(2, B, T, RG_W)
                           + b_gate.astype(jnp.float32)[:, None, None, :])
    log_a = -RG_C * gates[0] * jax.nn.softplus(-lam.astype(jnp.float32))
    a = jnp.exp(log_a)
    bx = jnp.sqrt(jnp.maximum(-jnp.expm1(2.0 * log_a), 0.0)) * (gates[1] * u)

    def combine(l, r):
        return (l[0] * r[0], r[0] * l[1] + r[1])

    a_cum, b_cum = lax.associative_scan(combine, (a, bx), axis=1)
    h = a_cum * h0.astype(jnp.float32)[:, None, :] + b_cum
    return h, h[:, -1]

def _token_mixers(h, p, s_gdn, s_hg, s_rg, rows):
    B, T, _ = h.shape
    f32 = jnp.float32
    splits = np.cumsum(IN_SIZES)[:-1].tolist()
    qkv, g_gdn, a_gdn, b_gdn, q_hg, i_hg, g_hg, f_hg, x_rg, y_rg = jnp.split(h @ p['w_in'], splits, axis=-1)

    def heads(t, n):
        return t.reshape(B, T, n, -1).transpose(0, 2, 1, 3)

    qkv = jax.nn.silu(_dwconv(qkv, p['gdn_conv_w']))
    q, k, v = jnp.split(qkv, 3, axis=-1)
    q = _l2norm(heads(q, GDN_H)) * GDN_DK ** -0.5
    k = _l2norm(heads(k, GDN_H))
    v = heads(v, GDN_H).astype(f32)
    a = a_gdn.astype(f32).reshape(B, T, 2, GDN_H).transpose(2, 0, 3, 1)
    beta = jax.nn.sigmoid(b_gdn.astype(f32).reshape(B, T, 2, GDN_H).transpose(2, 0, 3, 1))
    log_alpha = (-jnp.exp(p['gdn_a_log'].astype(f32))[:, None, :, None]
                 * jax.nn.softplus(a + p['gdn_dt_bias'].astype(f32)[:, None, :, None]))
    o_a, st_a = _bidirectional(_gdn_step, s_gdn, (q, k, v, log_alpha[0], beta[0]), (q, k, v, log_alpha[1], beta[1]))
    o_a = _rms(o_a.astype(h.dtype), p['gdn_norm_w']) * jax.nn.silu(heads(g_gdn, GDN_H))
    o_a = o_a.transpose(0, 2, 1, 3).reshape(B, T, GDN_W)

    lb = p['hg_lb']
    zf = f_hg.astype(f32).reshape(B, T, 2, HG_H * HG_DK)
    f_gate = lb + (1.0 - lb) * jax.nn.sigmoid(zf)
    log_f = jnp.log(jnp.maximum(f_gate, F_MIN))
    k_f = (1.0 - lb) * jax.nn.sigmoid(-zf)

    def dirs(t):
        return t.reshape(B, T, 2, HG_H, HG_DK).transpose(2, 0, 3, 1, 4)

    log_f, k_f = dirs(log_f), dirs(k_f)
    qb = heads(q_hg, HG_H).astype(f32)
    ib = heads(i_hg, HG_H).astype(f32)
    o_b, st_b = _bidirectional(_hgrn_step, s_hg, (qb, k_f[0], ib, log_f[0]), (qb, k_f[1], ib, log_f[1]))
    o_b = _rms(o_b.astype(h.dtype), p['hg_norm_w']) * jax.nn.silu(heads(g_hg, HG_H))
    o_b = o_b.transpose(0, 2, 1, 3).reshape(B, T, HG_W)

    def to_scan_order(t):
        return t if rows is None else t.reshape(B, rows, GRID_W, -1).swapaxes(1, 2).reshape(B, T, -1)

    def from_scan_order(t):
        return t if rows is None else t.reshape(B, GRID_W, rows, -1).swapaxes(1, 2).reshape(B, T, -1)

    u = (_dwconv(to_scan_order(x_rg), p['rg_conv_w']) + p['rg_conv_b']).astype(f32)
    h_f, e_f = _rglru(u, p['rg_gate_w'][0], p['rg_gate_b'][0], p['rg_lambda'][0], s_rg[:, 0])
    h_b, e_b = _rglru(jnp.flip(u, 1), p['rg_gate_w'][1], p['rg_gate_b'][1], p['rg_lambda'][1], s_rg[:, 1])
    o_c = from_scan_order(h_f + jnp.flip(h_b, 1)).astype(h.dtype) * jax.nn.gelu(y_rg)
    st_c = jnp.stack([e_f, e_b], axis=1)

    out = jnp.concatenate([o_a, o_b, o_c], axis=-1) @ p['w_out']
    return out, (st_a, st_b, st_c)

def _moe(h, p):
    B, T, D = h.shape
    xt = h.reshape(B * T, D)
    logits = (xt @ p['router_w']).astype(jnp.float32) + p['router_b'].astype(jnp.float32)
    probs = jax.nn.softmax(logits, axis=-1)
    grouped = probs.reshape(-1, N_GROUPS, EXPERTS_PER_GROUP)
    group_score = jnp.sum(lax.top_k(grouped, TOP_K)[0], axis=-1)
    in_group = jnp.argmax(group_score, axis=-1)[:, None] == jnp.arange(N_GROUPS)
    masked = jnp.where(in_group[:, :, None], grouped, -1.0).reshape(-1, N_EXPERTS)
    top_p, top_i = lax.top_k(masked, TOP_K)
    top_w = top_p / jnp.sum(top_p, axis=-1, keepdims=True)
    gates = jnp.sum(jax.nn.one_hot(top_i, N_EXPERTS, dtype=jnp.float32) * top_w[..., None], axis=1)
    y = jnp.zeros((B * T, D), jnp.float32)
    for e in range(N_EXPERTS):
        hid = jax.nn.silu(xt @ p['moe_w_gate'][e]) * (xt @ p['moe_w_up'][e])
        y = y + gates[:, e:e + 1] * (hid @ p['moe_w_down'][e])
    return y.astype(h.dtype).reshape(B, T, D)

def _layer(x, mod, p, s_gdn, s_hg, s_rg, rows):
    sh1, sc1, gt1, sh2, sc2, gt2 = jnp.split(mod.astype(x.dtype), 6, axis=-1)
    h = _rms(x, p['norm1_w']) * (1 + sc1) + sh1
    o, states = _token_mixers(h, p, s_gdn, s_hg, s_rg, rows)
    x = x + gt1 * o
    h = _rms(x, p['norm2_w']) * (1 + sc2) + sh2
    x = x + gt2 * _moe(h, p)
    return x, states

def setup_inputs(seed: int = 0) -> dict:
    key = jax.random.key(seed)
    ks = iter(jax.random.split(key, 40))
    f32 = jnp.float32

    def nrm(shape, s):
        return jax.random.normal(next(ks), shape, f32) * s

    x_prompt = nrm((BATCH, SEQ, D_MODEL), 1.0)
    x_sample = nrm((DEC_BATCH, DEC_SEQ, D_MODEL), 1.0)
    state_gdn = nrm((DEC_BATCH, DEPTH, 2, GDN_H, GDN_DK, GDN_DV), 0.1)
    state_hgrn = nrm((DEC_BATCH, DEPTH, 2, HG_H, HG_DK, HG_DV), 0.3)
    state_rglru = nrm((DEC_BATCH, DEPTH, 2, RG_W), 0.5)
    c = nrm((DEC_BATCH, D_MODEL), 1.0)
    c_ctx = nrm((D_MODEL,), 1.0)
    ada_w = nrm((DEPTH, D_MODEL, 6 * D_MODEL), 0.5 * D_MODEL ** -0.5)
    ada_b = nrm((DEPTH, 6 * D_MODEL), 0.02)
    norm1_w = 1.0 + nrm((DEPTH, D_MODEL), 0.05)
    norm2_w = 1.0 + nrm((DEPTH, D_MODEL), 0.05)
    final_norm_w = 1.0 + nrm((D_MODEL,), 0.05)
    w_in = nrm((DEPTH, D_MODEL, N_IN), D_MODEL ** -0.5)
    gdn_conv_w = nrm((DEPTH, CONV_K, 3 * GDN_W), 0.5)
    gdn_a_log = jnp.log(jax.random.uniform(next(ks), (DEPTH, 2, GDN_H), f32, 1.0, 16.0))
    dt = jnp.exp(jax.random.uniform(next(ks), (DEPTH, 2, GDN_H), f32, math.log(1e-3), math.log(1e-1)))
    gdn_dt_bias = dt + jnp.log(-jnp.expm1(-dt))
    gdn_norm_w = 1.0 + nrm((DEPTH, GDN_DV), 0.05)
    hg_lb_logits = nrm((DEPTH, 2, HG_H * HG_DK), 0.5)
    hg_norm_w = 1.0 + nrm((DEPTH, HG_DV), 0.05)
    rg_conv_w = nrm((DEPTH, CONV_K, RG_W), 0.5)
    rg_conv_b = nrm((DEPTH, RG_W), 0.02)
    rg_gate_w = nrm((DEPTH, 2, 2, RG_BLOCKS, RG_BW, RG_BW), RG_BW ** -0.5)
    rg_gate_b = nrm((DEPTH, 2, 2, RG_W), 0.02)
    a0 = jax.random.uniform(next(ks), (DEPTH, 2, RG_W), f32, 0.9, 0.999)
    rg_lambda = jnp.log(a0) - jnp.log1p(-a0)
    w_out = nrm((DEPTH, MIX_W, D_MODEL), MIX_W ** -0.5)
    router_w = nrm((D_MODEL, N_EXPERTS), D_MODEL ** -0.5)
    router_b = nrm((N_EXPERTS,), 0.01)
    moe_w_gate = nrm((DEPTH, N_EXPERTS, D_MODEL, D_FF), D_MODEL ** -0.5)
    moe_w_up = nrm((DEPTH, N_EXPERTS, D_MODEL, D_FF), D_MODEL ** -0.5)
    moe_w_down = nrm((DEPTH, N_EXPERTS, D_FF, D_MODEL), D_FF ** -0.5)
    return {
        'x_prompt': x_prompt, 'x_sample': x_sample,
        'state_gdn': state_gdn, 'state_hgrn': state_hgrn, 'state_rglru': state_rglru,
        'c': c, 'c_ctx': c_ctx,
        'ada_w': ada_w, 'ada_b': ada_b,
        'norm1_w': norm1_w, 'norm2_w': norm2_w, 'final_norm_w': final_norm_w,
        'w_in': w_in,
        'gdn_conv_w': gdn_conv_w, 'gdn_a_log': gdn_a_log, 'gdn_dt_bias': gdn_dt_bias, 'gdn_norm_w': gdn_norm_w,
        'hg_lb_logits': hg_lb_logits, 'hg_norm_w': hg_norm_w,
        'rg_conv_w': rg_conv_w, 'rg_conv_b': rg_conv_b, 'rg_gate_w': rg_gate_w, 'rg_gate_b': rg_gate_b,
        'rg_lambda': rg_lambda,
        'w_out': w_out,
        'router_w': router_w, 'router_b': router_b,
        'moe_w_gate': moe_w_gate, 'moe_w_up': moe_w_up, 'moe_w_down': moe_w_down,
    }

def reference(x_prompt, x_sample, state_gdn, state_hgrn, state_rglru, c, c_ctx, ada_w, ada_b, norm1_w, norm2_w,
              final_norm_w, w_in, gdn_conv_w, gdn_a_log, gdn_dt_bias, gdn_norm_w, hg_lb_logits, hg_norm_w,
              rg_conv_w, rg_conv_b, rg_gate_w, rg_gate_b, rg_lambda, w_out, router_w, router_b,
              moe_w_gate, moe_w_up, moe_w_down):
    rows = x_sample.shape[1] // GRID_W
    bp = x_prompt.shape[0]
    lb_soft = jax.nn.softmax(hg_lb_logits.astype(jnp.float32), axis=0)
    hg_lb = jnp.cumsum(lb_soft, axis=0) - lb_soft[:1]
    zero_gdn = jnp.zeros((bp, 2, GDN_H, GDN_DK, GDN_DV), jnp.float32)
    zero_hg = jnp.zeros((bp, 2, HG_H, HG_DK, HG_DV), jnp.float32)
    zero_rg = jnp.zeros((bp, 2, RG_W), jnp.float32)
    xp, xs = x_prompt, x_sample
    new_gdn, new_hg, new_rg = [], [], []
    for l in range(DEPTH):
        p = {
            'w_in': w_in[l], 'gdn_conv_w': gdn_conv_w[l], 'gdn_a_log': gdn_a_log[l],
            'gdn_dt_bias': gdn_dt_bias[l], 'gdn_norm_w': gdn_norm_w[l],
            'hg_lb': hg_lb[l], 'hg_norm_w': hg_norm_w[l],
            'rg_conv_w': rg_conv_w[l], 'rg_conv_b': rg_conv_b[l], 'rg_gate_w': rg_gate_w[l],
            'rg_gate_b': rg_gate_b[l], 'rg_lambda': rg_lambda[l],
            'w_out': w_out[l], 'norm1_w': norm1_w[l], 'norm2_w': norm2_w[l],
            'router_w': router_w, 'router_b': router_b,
            'moe_w_gate': moe_w_gate[l], 'moe_w_up': moe_w_up[l], 'moe_w_down': moe_w_down[l],
        }
        mod_ctx = (jax.nn.silu(c_ctx) @ ada_w[l] + ada_b[l])[None, None, :]
        mod_lat = (jax.nn.silu(c) @ ada_w[l] + ada_b[l])[:, None, :]
        xp, (sg, sh, sr) = _layer(xp, mod_ctx, p, zero_gdn, zero_hg, zero_rg, None)
        xs, _ = _layer(xs, mod_lat, p, state_gdn[:, l], state_hgrn[:, l], state_rglru[:, l], rows)
        new_gdn.append(sg)
        new_hg.append(sh)
        new_rg.append(sr)
    y_prompt = _rms(xp, final_norm_w)
    y_sample = _rms(xs, final_norm_w)
    new_state_gdn = jnp.stack(new_gdn, axis=1)
    new_state_hgrn = jnp.stack(new_hg, axis=1)
    new_state_rglru = jnp.stack(new_rg, axis=1)
    return (y_prompt, y_sample, new_state_gdn, new_state_hgrn, new_state_rglru)


_drawn_inputs = setup_inputs


def setup_inputs(seed=0):
    import zlib

    import numpy as np

    out = dict(_drawn_inputs(seed))
    spreads = {}
    factors = {'state_hgrn': 8.0,
     'state_rglru': 3.455,
     'hg_norm_w': 3.679,
     'rg_gate_b': 6.333,
     'router_b': 3.89,
     'gdn_norm_w': 4.796}
    for name, (base, spread) in spreads.items():
        noise = np.random.default_rng([zlib.crc32(name.encode()), seed]).standard_normal(out[name].shape)
        drawn = base * np.exp(spread * noise) if base else spread * noise
        out[name] = __import__('jax').numpy.asarray(drawn.astype(out[name].dtype))
    for name, factor in factors.items():
        out[name] = (out[name] * factor).astype(out[name].dtype)
    return out
```

```python
from contextlib import ExitStack

import numpy as np
import concourse.bass as bass
from concourse import mybir

F32 = mybir.dt.float32
I32 = mybir.dt.int32
U32 = mybir.dt.uint32
ACT = mybir.ActivationFunctionType
ALU = mybir.AluOpType
AX = mybir.AxisListType

P = 128
D = 1024
KD = D // P
CTX, LAT = 128, 512
T = CTX + LAT
NT = T // P
GH = 4
HH, HK = 4, 64
NE = 16
FF = 512
EPS = 1e-6
RG_C = 8.0
F_MIN = 1e-30
LNSPLIT = 2.0 ** -60
GRID_W, ROWS = 64, LAT // 64
PADW = 2 + CTX + 2 + LAT + 1
CONVW = PADW - 3
SEG = ((0, CTX, 0), (CTX, T, 1))
FWD = (0, 1, 2, 3, 4)
BWD = (0, 4, 3, 2, 1)
LEVELS = (1, 2, 4, 8, 16, 32, 64)
O_QKV, O_G, O_AB, O_HQ, O_HF1, O_RG = 0, 1536, 2048, 2064, 3088, 3344
RING = 3
SLAB = 8 * 512
MULT, ADD, SUB, MAX, MIN = ALU.mult, ALU.add, ALU.subtract, ALU.max, ALU.min


def slab_plan():
    s = [(("ada", i), 512) for i in range(12)]
    s += [(("rg", 0), 512), (("hq", 0), 512), (("hg", 0), 512), (("hf", 0), 256)]
    s += [(("gdn", i), 512) for i in range(4)]
    s += [(("out", i), 512) for i in range(2)]
    for e in range(NE):
        s += [(("gate", e), 512), (("up", e), 512), (("down", e), 512)]
    return s


def job_plan():
    j = [("stage", 0)]
    j += [("xt", t) for t in range(NT)]
    j += [("ada", i) for i in range(12)] + [("modT", 0)]
    j += [("rms", 0)]
    j += [("rgx", b) for b in range(2)] + [("rgy", b) for b in range(2)]
    j += [("rgg", n) for n in range(8)]
    j += [("hq", b) for b in range(2)] + [("hi", n) for n in range(2)]
    j += [("hgate", n) for n in range(2)] + [("hf", n) for n in range(4)]
    j += [("lev", l, t) for l in range(8) for t in range(NT)]
    j += [("kdt", t) for t in range(NT)]
    for s in range(NT):
        j += [("ho", s), ("hs", s)]
    j += [("hmix", t) for t in range(NT)]
    j += [("qkv", b) for b in range(12)] + [("gg", t) for t in range(NT)] + [("ab", 0)]
    j += [("ss", b) for b in range(8)] + [("rows", t) for t in range(NT)] + [("gcol", 0)]
    for s in range(NT):
        j += [("gb", s), ("kk", s), ("kq", s)]
        for l in range(7):
            j += [("t1", s, l)] + [("dx", s, l)] * (0 < l < 6) + [("dxt", s, l)]
        j += [("ks", s), ("u", s), ("o", s), ("ds", s)]
    j += [("gmix", t) for t in range(NT)]
    j += [("out", n) for n in range(KD)]
    j += [("rms", 1), ("router", 0)]
    for e in range(NE):
        for f in range(4):
            j += [("gate", e, f), ("up", e, f)]
        j += [("down", e, t) for t in range(NT)]
    j += [("yT", t) for t in range(NT)]
    j += [("rms", 2)] + [("fin", t) for t in range(NT)]
    return j


def layer_program(nc, I, O, stop=None):
    ctx = ExitStack()
    with ctx:
        def sb(name, *shape, dt=F32):
            return ctx.enter_context(nc.sbuf_tensor(name, [P, *shape], dt))

        def sem(name):
            return ctx.enter_context(nc.semaphore(name))

        ps = ctx.enter_context(nc.psum_tensor("ps", [P, 4, 1024], F32))
        ring = sb("ring", RING, SLAB)
        xT = sb("xT", KD, T)
        hT = sb("hT", KD, T)
        mixBC = sb("mixBC", 4, T)
        ident = sb("ident", P)
        ones = sb("ones", P)
        tri = sb("tri", 2, P)
        lmask = sb("lmask", 2, 7, P)
        vi = sb("vi", 2, P, dt=I32)
        vf = sb("vf", 2, P)
        b_end = sb("b_end", NT, 4)
        stA = sb("stA", P)
        stB = sb("stB", P)
        vecA = sb("vecA", 88)
        vecB = sb("vecB", 80)
        cs = sb("cs", KD, 2)
        modT = sb("modT", 48, 2)
        scl1 = sb("scl1", KD, 2)
        scl2 = sb("scl2", KD, 2)
        wab = sb("wab", KD, 16)
        rw = sb("rw", KD, NE)
        rbias = sb("rbias", NE)
        alog = sb("alog", 8)
        dtb = sb("dtb", 8)
        rb = sb("rb", T)
        small = sb("small", 64)
        stateB = sb("stateB", 2, 2, 2, HK)
        ARENA = 23040
        arena = sb("arena", ARENA)

        def carve(at, *shape):
            n = int(np.prod(shape))
            assert at + n <= ARENA, (at, n)
            v = arena[:, at:at + n]
            if len(shape) > 1:
                names = "abcdef"[:len(shape)]
                v = v.rearrange("p (%s) -> p %s" % (" ".join(names), " ".join(names)),
                                **dict(zip(names, shape)))
            return v

        SQ_AT, WG_AT = 11264, 20480
        sq = carve(SQ_AT, KD, T)
        xrow = carve(0, NT, D)
        modrow = carve(NT * D, 6 * D)
        c_x = carve(0, 2, PADW)
        c_u = carve(1300, 2, CONVW)
        c_yg = carve(2600, 2, T)
        c_g = carve(3900, 2, 2, 2, T)
        c_a = carve(9100, 4, T)
        c_t = carve(11700, 4, T)
        c_h = carve(14300, 4, T)
        c_wg = carve(WG_AT, 8, P)
        b_q = carve(0, 2, T)
        b_v = carve(1280, NT, 256)
        b_g = carve(2560, NT, 256)
        b_o = carve(3840, NT, 256)
        b_f = carve(5120, 4, T)
        b_k = carve(7680, 4, T)
        b_b = carve(10240, 4, T)
        b_Z = [carve(12800, 4, T), carve(15360, 4, T)]
        b_at = carve(17920, NT, 8, P)
        a_qk = carve(0, 8, T)
        a_K = carve(5120, NT, 512)
        a_V = carve(7680, NT, 512)
        a_g = carve(10240, NT, 512)
        a_o = carve(12800, NT, 512)
        a_S = carve(15360, 2, 8, P)
        a_X = carve(17408, 8, P)
        a_XT = carve(18432, 8, P)
        a_AT = carve(19456, 8, P)
        a_CT = [carve(20480, 8, P), carve(21504, 8, P)]
        a_pad = carve(17408, 2, PADW)
        a_cv = carve(17408 + 2 * PADW, 2, CONVW)
        a_rn = carve(17408, 8, T)
        a_sm = carve(22530, 420)

        def smallcol(at, *shape):
            n = int(np.prod(shape))
            v = a_sm[:, at:at + n]
            if len(shape) > 1:
                v = v.rearrange("p (a b) -> p a b", a=shape[0])
            return v

        a_la = smallcol(0, NT, 8)
        a_z = smallcol(40, NT, 8)
        a_w = smallcol(80, NT, 8)
        a_beta = smallcol(120, NT, 8)
        a_gc = smallcol(160, NT, 8)
        a_beg = smallcol(200, NT, 8)
        s_beta = smallcol(240, NT, 8)
        s_gc = smallcol(280, NT, 8)
        s_beg = smallcol(320, NT, 8)
        a_nea = smallcol(360, 8)
        a_ge = smallcol(368, NT, 8)
        a_r = smallcol(40, 20)
        hTf = hT[:, :, :].rearrange("p k t -> p (k t)")

        def temp(n):
            return hTf[:, 1024 * n:1024 * (n + 1)].rearrange("p (a b) -> p a b", a=8)

        a_T1, a_dec, a_qe, a_Kd, a_U = (temp(n) for n in range(5))
        mixA = hT[:, 0:4, :]
        m_y = carve(0, NT, D)
        m_hid = carve(5120, 2, 4, T)
        m_sg = carve(16640, 2, T)
        m_out = carve(18000, 2, D)
        m_tmp = carve(10240, 8, P)
        m_p = carve(20100, NT, NE)
        m_gate = carve(20200, NT, NE)
        m_rank = carve(20300, NT, NE)
        m_gt = carve(20400, NT, NE)
        m_col = carve(20500, 16)
        m_gs = carve(20520, NT, 4)
        m_gr = carve(20540, NT, 4)
        m_gg = carve(20560, NT, 4)

        PLAN = job_plan()
        JOB = {name: n for n, name in enumerate(PLAN)}
        pair_full = [sem(f"pair_full{i}") for i in range(4)]
        pair_free = [sem(f"pair_free{i}") for i in range(4)]

        def pair(name):
            return JOB[name] % 4

        def bank(name):
            return ps[:, pair(name), :]

        def full_after(name):
            return pair_full[pair(name)], JOB[name] // 4 + 1

        def free_before(name):
            return pair_free[pair(name)], JOB[name] // 4

        def free_after(name):
            return pair_free[pair(name)], JOB[name] // 4 + 1

        s_a_conv = sem("a_conv")
        s_a_ct = sem("a_ct")
        s_a_d = sem("a_d")
        s_a_dec = sem("a_dec")
        s_a_eg = sem("a_eg")
        s_a_la = sem("a_la")
        s_a_ln = sem("a_ln")
        s_a_norm = sem("a_norm")
        s_a_oall = sem("a_oall")
        s_a_on = sem("a_on")
        s_a_orn = sem("a_orn")
        s_a_osq = sem("a_osq")
        s_a_oss = sem("a_oss")
        s_a_pad = sem("a_pad")
        s_a_rhs = sem("a_rhs")
        s_a_rn = sem("a_rn")
        s_a_silu = sem("a_silu")
        s_a_sq = sem("a_sq")
        s_a_state = sem("a_state")
        s_a_x0 = sem("a_x0")
        s_a_z = sem("a_z")
        s_b_d = sem("b_d")
        s_b_e = sem("b_e")
        s_b_k = sem("b_k")
        s_b_kd = sem("b_kd")
        s_b_ln = sem("b_ln")
        s_b_m = sem("b_m")
        s_b_oall = sem("b_oall")
        s_b_on = sem("b_on")
        s_b_r = sem("b_r")
        s_b_sq = sem("b_sq")
        s_b_ss = sem("b_ss")
        s_b_state = sem("b_state")
        s_b_z = sem("b_z")
        s_c_a = sem("c_a")
        s_c_done = sem("c_done")
        s_c_fin = sem("c_fin")
        s_c_lam = sem("c_lam")
        s_c_ln = sem("c_ln")
        s_c_mix = sem("c_mix")
        s_c_nc8 = sem("c_nc8")
        s_c_pad = sem("c_pad")
        s_c_sqrt = sem("c_sqrt")
        s_c_y = sem("c_y")
        s_conv_c = sem("conv_c")
        s_cs = sem("cs")
        s_eps = sem("eps")
        s_fin_h = sem("fin_h")
        s_h = sem("h")
        s_hid = sem("hid")
        s_hraw = sem("hraw")
        s_ident = sem("ident")
        s_iota = sem("iota")
        s_m_sg = sem("m_sg")
        s_mod = sem("mod")
        s_r_exp = sem("r_exp")
        s_r_max = sem("r_max")
        s_rb = sem("rb")
        s_sb_in = sem("sb_in")
        s_sg_in = sem("sg_in")
        s_small_in = sem("small_in")
        s_sq = sem("sq")
        s_st_in = sem("st_in")
        s_state_stored = sem("state_stored")
        s_wg_in = sem("wg_in")
        s_wg_zero = sem("wg_zero")
        s_x2 = sem("x2")
        s_x_in = sem("x_in")
        s_y_stored = [sem(f"y_stored{i}") for i in range(2)]

        class Chain:

            def __init__(self, eng, name):
                self.eng, self.sem, self.n = eng, sem(name), 0

            def __call__(self, ins):
                ins.then_inc(self.sem, 1)
                self.n += 1

            def sync(self):
                self.eng.wait_ge(self.sem, self.n)

        SLABS = slab_plan()
        SLAB_N = {name: n for n, (name, _) in enumerate(SLABS)}
        slab_full = [sem(f"slab_full{i}") for i in range(RING)]
        LAST = {}
        for i in range(12):
            LAST[("ada", i)] = ("ada", i)
        LAST[("rg", 0)] = ("rgy", 1)
        LAST[("hq", 0)] = ("hi", 1)
        LAST[("hg", 0)] = ("hf", 1)
        LAST[("hf", 0)] = ("hf", 3)
        for i in range(3):
            LAST[("gdn", i)] = ("qkv", 4 * i + 3)
        LAST[("gdn", 3)] = ("gg", NT - 1)
        for i in range(2):
            LAST[("out", i)] = ("out", 4 * i + 3)
        for e in range(NE):
            LAST[("gate", e)] = ("gate", e, 3)
            LAST[("up", e)] = ("up", e, 3)
            LAST[("down", e)] = ("down", e, NT - 1)

        def slab(name, width=512):
            n = SLAB_N[name] % RING
            return ring[:, n, 0:8 * width].rearrange("p (k n) -> p k n", k=8)

        def slab_after(name):
            n = SLAB_N[name]
            return slab_full[n % RING], 16 * (n // RING + 1)

        win = I["w_in"][0].rearrange("(k p) n -> p k n", p=P)

        def slab_source(name):
            kind, i = name
            if kind == "ada":
                return I["ada_w"][0].rearrange("(k p) n -> p k n", p=P)[:, :, 512 * i:512 * i + 512]
            if kind in ("rg", "hq", "hg", "hf", "gdn"):
                at = {"rg": O_RG, "hq": O_HQ, "hg": O_HQ + 512, "hf": O_HQ + 1024, "gdn": 512 * i}[kind]
                return win[:, :, at:at + (256 if kind == "hf" else 512)]
            if kind == "out":
                return I["w_out"][0].rearrange("(k p) n -> p k n", p=P)[:, :, 512 * i:512 * i + 512]
            if kind == "down":
                return I["moe_w_down"][0, i].rearrange("(k p) n -> p k n", p=P)
            return I["moe_w_" + kind][0, i].rearrange("(k p) n -> p k n", p=P)

        def segs(name):
            b = bank(name)
            return ((0, CTX, b[:, 0:CTX], 0), (CTX, T, b[:, 512:1024], 1))

        def wide(v, at, n):
            v = v.unsqueeze(at)
            shape = list(v.shape)
            shape[at] = n
            return v.to_broadcast(shape)

        vb = vecB
        block = ctx.enter_context(nc.Block())

        @block.sync
        def _(sp):
            sp.dma_start(xrow[:, 0, :], I["x_prompt"][0]).then_inc(s_x_in, 16)
            sp.dma_start(xrow[:, 1:NT, :], I["x_sample"][0].rearrange("(t p) d -> p t d", p=P)).then_inc(s_x_in, 16)
            for n, (name, width) in enumerate(SLABS):
                if n >= RING:
                    sp.wait_ge(*full_after(LAST[SLABS[n - RING][0]]))
                if name[0] == "down":
                    dst = ring[:, n % RING, :].rearrange("p (k n) -> p k n", k=4)
                else:
                    dst = slab(name, width)
                sp.dma_start(dst, slab_source(name)).then_inc(slab_full[n % RING], 16)
            for t in range(NT):
                sp.wait_ge(*free_after(("fin", t)))
                dst = O["y_prompt"][0] if t == 0 else O["y_sample"][0, (t - 1) * P:t * P, :]
                sp.dma_start(dst, m_out[:, t % 2, :]).then_inc(s_y_stored[t % 2], 16)
            sp.wait_ge(s_y_stored[0], 48)
            sp.wait_ge(s_y_stored[1], 32)
            sp.wait_ge(s_state_stored, 16 * 3)

        @block.tensor
        def _(pe):
            mm = nc.tensor.matmul

            def tr(out, in_, n=P):
                return nc.tensor.transpose(out, in_, ident[0:n, 0:n])

            def project(name, w, cols, rhs=None):
                rhs = rhs or (lambda k: hT[:, k, :])
                pe.wait_ge(*free_before(name))
                for a, b, out, g in segs(name):
                    for k in range(KD):
                        last = mm(out, w[:, k, cols], rhs(k)[:, a:b], start=(k == 0), stop=(k == KD - 1))
                last.then_inc(pair_full[pair(name)], 1)

            pe.wait_ge(s_ident, 1)
            pe.wait_ge(s_st_in, 16 * 16)
            b = bank(("stage", 0))
            tr(b[:, 0:88], stA[0:88, :], 88)
            tr(b[:, 512:592], stB[0:80, :], 80).then_inc(pair_full[pair(("stage", 0))], 1)
            pe.wait_ge(s_x_in, 32)
            for t in range(NT):
                name = ("xt", t)
                pe.wait_ge(*free_before(name))
                for k in range(KD):
                    last = tr(bank(name)[:, P * k:P * k + P], xrow[:, t, P * k:P * k + P])
                last.then_inc(pair_full[pair(name)], 1)
            pe.wait_ge(s_cs, 2)
            for i in range(12):
                name = ("ada", i)
                pe.wait_ge(*slab_after(name))
                pe.wait_ge(*free_before(name))
                for k in range(KD):
                    last = mm(bank(name)[0:2, 0:512], cs[:, k, :], slab(name)[:, k, :],
                              start=(k == 0), stop=(k == KD - 1))
                last.then_inc(pair_full[pair(name)], 1)
            pe.wait_ge(*free_after(("ada", 11)))
            pe.wait_ge(*free_after(("ada", 10)))
            pe.wait_ge(*free_after(("ada", 9)))
            name = ("modT", 0)
            pe.wait_ge(*free_before(name))
            for c in range(48):
                last = tr(bank(name)[:, 2 * c:2 * c + 2], modrow[0:2, P * c:P * c + P], 2)
            last.then_inc(pair_full[pair(name)], 1)

            def rms_sums(n):
                name = ("rms", n)
                pe.wait_ge(*free_before(name))
                for k in range(KD):
                    pe.wait_ge(s_sq, KD * n + k + 1)
                    for a, b, out, g in segs(name):
                        last = mm(out, ones[:, :], sq[:, k, a:b], start=(k == 0), stop=(k == KD - 1))
                last.then_inc(pair_full[pair(name)], 1)

            rms_sums(0)
            pe.wait_ge(s_h, 16)
            w = slab(("rg", 0))
            pe.wait_ge(*slab_after(("rg", 0)))
            for b in range(2):
                project(("rgx", b), w, slice(P * b, P * b + P))
            for b in range(2):
                project(("rgy", b), w, slice(256 + P * b, 256 + P * b + P))
            pe.wait_ge(s_conv_c, 2)
            pe.wait_ge(s_wg_in, 16 * 16)
            for n in range(8):
                name = ("rgg", n)
                pe.wait_ge(*free_before(name))
                for a, b, out, g in segs(name):
                    last = mm(out, c_wg[:, n, :], c_u[:, n % 2, a + 2 * g:b + 2 * g], start=True, stop=True)
                last.then_inc(pair_full[pair(name)], 1)
            w = slab(("hq", 0))
            pe.wait_ge(*slab_after(("hq", 0)))
            for b in range(2):
                project(("hq", b), w, slice(P * b, P * b + P))

            def token_rows(kind, w, col, width, per, tiles=NT):
                for n in range((tiles + per - 1) // per):
                    name = (kind, n)
                    pe.wait_ge(*free_before(name))
                    for t in range(n * per, min(tiles, n * per + per)):
                        out = bank(name)[:, (t - n * per) * width:(t - n * per + 1) * width]
                        for k in range(KD):
                            last = mm(out, hT[:, k, P * t:P * t + P], w[:, k, col:col + width],
                                      start=(k == 0), stop=(k == KD - 1))
                    last.then_inc(pair_full[pair(name)], 1)

            token_rows("hi", w, 256, 256, 4)
            w = slab(("hg", 0))
            pe.wait_ge(*slab_after(("hg", 0)))
            token_rows("hgate", w, 0, 256, 4)
            for n in range(2):
                project(("hf", n), w, slice(256 + P * n, 256 + P * n + P))
            w = slab(("hf", 0), 256)
            pe.wait_ge(*slab_after(("hf", 0)))
            for n in range(2):
                project(("hf", 2 + n), w, slice(P * n, P * n + P))

            HALVES = [(half, dp) for half in range(2) for dp in range(4)]

            def half(v, h, dp, t):
                return v[64 * h:64 * h + 64, dp, P * t:P * t + P]

            pe.wait_ge(s_b_k, 1)
            for l in range(8):
                if l:
                    pe.wait_ge(s_b_z, l)
                for t in range(NT):
                    name = ("lev", l, t)
                    pe.wait_ge(*free_before(name))
                    for h, dp in HALVES:
                        lhs = half(b_Z[l % 2] if l else b_k, h, dp, t)
                        rhs = half(b_Z[l % 2], h, dp, t) if l else half(b_q, h, dp % 2, t)
                        last = mm(bank(name)[:, 512 * h + P * dp:512 * h + P * dp + P], lhs, rhs, start=True, stop=True)
                    last.then_inc(pair_full[pair(name)], 1)
            pe.wait_ge(s_b_kd, 1)
            for t in range(NT):
                name = ("kdt", t)
                pe.wait_ge(*free_before(name))
                for dp in range(4):
                    last = tr(bank(name)[:, P * dp:P * dp + P], b_Z[1][:, dp, P * t:P * t + P])
                last.then_inc(pair_full[pair(name)], 1)
            b_kdr = b_k.rearrange("p a t -> p (a t)").rearrange("p (t c n) -> p t c n", t=NT, c=4)
            for s in range(NT):
                seg = min(s, 1)
                name = ("ho", s)
                if s == 0:
                    pe.wait_ge(*free_after(("kdt", NT - 1)))
                    pe.wait_ge(*free_after(("lev", 7, NT - 1)))
                if s == 0:
                    pe.wait_ge(s_b_state, 1)
                else:
                    pe.wait_ge(*free_after(("hs", s - 1)))
                pe.wait_ge(*free_before(name))
                for h, dp in HALVES:
                    t = (FWD, BWD)[dp // 2][s]
                    out = bank(name)[:, 512 * h + 64 * dp:512 * h + 64 * dp + 64]
                    v = P * (dp % 2) + 64 * h
                    mm(out, half(b_Z[0], h, dp, t), stateB[64 * h:64 * h + 64, seg, dp // 2, dp % 2, :],
                       start=True, stop=False)
                    last = mm(out, b_at[:, t, 4 * h + dp, :], b_v[:, t, v:v + 64], start=False, stop=True)
                last.then_inc(pair_full[pair(name)], 1)
                name = ("hs", s)
                pe.wait_ge(*free_before(name))
                for dp in range(4):
                    t = (FWD, BWD)[dp // 2][s]
                    last = mm(bank(name)[:, P * dp:P * dp + P], b_kdr[:, t, dp, :],
                              b_v[:, t, P * (dp % 2):P * (dp % 2) + P], start=True, stop=True)
                last.then_inc(pair_full[pair(name)], 1)
            pe.wait_ge(s_b_on, 1)
            for t in range(NT):
                name = ("hmix", t)
                pe.wait_ge(*free_before(name))
                for p in range(2):
                    last = tr(bank(name)[:, P * p:P * p + P], b_o[:, t, P * p:P * p + P])
                last.then_inc(pair_full[pair(name)], 1)
            for b in range(12):
                if b % 4 == 0:
                    pe.wait_ge(*slab_after(("gdn", b // 4)))
                project(("qkv", b), slab(("gdn", b // 4)), slice(P * (b % 4), P * (b % 4) + P))
            pe.wait_ge(*slab_after(("gdn", 3)))
            token_rows("gg", slab(("gdn", 3)), 0, 512, 1)
            pe.wait_ge(s_small_in, 16 * 5)
            token_rows("ab", wab, 0, 16, NT)
            for b in range(8):
                name = ("ss", b)
                pe.wait_ge(s_a_sq, b + 1)
                pe.wait_ge(*free_before(name))
                for a, e, out, g in segs(name):
                    last = mm(out, ones[:, :], a_K.rearrange("p a b -> p (a b)")
                              .rearrange("p (n t) -> p n t", t=T)[:, b % 4, a:e], start=True, stop=True)
                last.then_inc(pair_full[pair(name)], 1)
            pe.wait_ge(s_a_norm, 1)
            for t in range(NT):
                name = ("rows", t)
                pe.wait_ge(*free_before(name))
                vT = a_o.rearrange("p a b -> p (a b)").rearrange("p (n t) -> p n t", t=T)
                for h in range(GH):
                    tr(bank(name)[:, P * h:P * h + P], a_qk[:, 4 + h, P * t:P * t + P])
                for h in range(GH):
                    last = tr(bank(name)[:, 512 + P * h:512 + P * h + P], vT[:, h, P * t:P * t + P])
                last.then_inc(pair_full[pair(name)], 1)
            name = ("gcol", 0)
            pe.wait_ge(s_a_la, 1)
            pe.wait_ge(*free_before(name))
            for t in range(NT):
                for d in range(2):
                    c = 8 * t + 4 * d
                    last = mm(bank(name)[:, c:c + 4], tri[:, d, :], a_la[:, t, 4 * d:4 * d + 4],
                              start=True, stop=True)
            last.then_inc(pair_full[pair(name)], 1)

            def eight(name, lhs, rhs):
                pe.wait_ge(*free_before(name))
                for dh in range(8):
                    last = mm(bank(name)[:, P * dh:P * dh + P], lhs(dh), rhs(dh), start=True, stop=True)
                last.then_inc(pair_full[pair(name)], 1)

            def cut(v, base):
                return lambda s: lambda dh: v[:, base + dh % 4, P * (FWD, BWD)[dh // 4][s]:P * (FWD, BWD)[dh // 4][s] + P]

            kT, qT = cut(a_qk, 4), cut(a_qk, 0)
            for s in range(NT):
                seg = min(s, 1)
                tile = lambda dh: (FWD, BWD)[dh // 4][s]
                eight(("gb", s), lambda dh: a_la[:, tile(dh), dh:dh + 1].to_broadcast([P, P]),
                      lambda dh: tri[:, dh // 4, :])
                eight(("kk", s), kT(s), kT(s))
                eight(("kq", s), kT(s), qT(s))
                for l in range(7):
                    pe.wait_ge(s_a_ct, 7 * s + l + 1)
                    if l:
                        pe.wait_ge(*free_after(("dxt", s, l - 1)))
                        if l > 1:
                            pe.wait_ge(*free_after(("dx", s, l - 1)))
                        else:
                            pe.wait_ge(s_a_x0, s + 1)
                    ct = a_CT[l % 2]
                    eight(("t1", s, l), lambda dh: ct[:, dh, :],
                          (lambda dh: a_X[:, dh, :]) if l else (lambda dh: ident[:, :]))
                    pe.wait_ge(*free_after(("t1", s, l)))
                    if 0 < l < 6:
                        eight(("dx", s, l), lambda dh: a_XT[:, dh, :], lambda dh: a_T1[:, dh, :])
                    eight(("dxt", s, l), lambda dh: a_T1[:, dh, :],
                          (lambda dh: a_XT[:, dh, :]) if l else (lambda dh: ident[:, :]))
                if s == 0:
                    pe.wait_ge(s_a_state, 1)
                else:
                    pe.wait_ge(*free_after(("ds", s - 1)))
                    pe.wait_ge(s_sg_in, 16)
                eight(("ks", s), kT(s), lambda dh: a_S[:, seg, dh, :])
                pe.wait_ge(s_a_rhs, s + 1)
                pe.wait_ge(*free_after(("dxt", s, 6)))
                eight(("u", s), lambda dh: a_XT[:, dh, :], lambda dh: a_CT[0][:, dh, :])
                pe.wait_ge(*free_after(("u", s)))
                pe.wait_ge(*free_after(("kq", s)))
                name = ("o", s)
                pe.wait_ge(*free_before(name))
                for dh in range(8):
                    out = bank(name)[:, P * dh:P * dh + P]
                    mm(out, a_qe[:, dh, :], a_S[:, seg, dh, :], start=True, stop=False)
                    last = mm(out, a_dec[:, dh, :], a_U[:, dh, :], start=False, stop=True)
                last.then_inc(pair_full[pair(name)], 1)
                eight(("ds", s), lambda dh: a_Kd[:, dh, :], lambda dh: a_U[:, dh, :])
            pe.wait_ge(s_a_on, 1)
            for t in range(NT):
                name = ("gmix", t)
                pe.wait_ge(*free_before(name))
                for h in range(GH):
                    last = tr(bank(name)[:, P * h:P * h + P], a_o[:, t, P * h:P * h + P])
                last.then_inc(pair_full[pair(name)], 1)
            for t in range(NT):
                pe.wait_ge(*free_after(("gmix", t)))
                pe.wait_ge(*free_after(("hmix", t)))
            pe.wait_ge(s_c_mix, 4)
            for n in range(KD):
                if n % 4 == 0:
                    pe.wait_ge(*slab_after(("out", n // 4)))
                project(("out", n), slab(("out", n // 4)), slice(P * (n % 4), P * (n % 4) + P),
                        rhs=lambda k: mixA[:, k, :] if k < 4 else mixBC[:, k - 4, :])
            rms_sums(1)
            pe.wait_ge(s_h, 32)
            token_rows("router", rw, 0, NE, NT)
            for e in range(NE):
                for f in range(4):
                    for kind in ("gate", "up"):
                        if f == 0:
                            pe.wait_ge(*slab_after((kind, e)))
                        project((kind, e, f), slab((kind, e)), slice(P * f, P * f + P))
                wd = ring[:, SLAB_N[("down", e)] % RING, :].rearrange("p (k n) -> p k n", k=4)
                pe.wait_ge(*slab_after(("down", e)))
                pe.wait_ge(s_hid, 8 * (e + 1))
                for t in range(NT):
                    name = ("down", e, t)
                    pe.wait_ge(*free_before(name))
                    for n in range(2):
                        for f in range(4):
                            last = mm(bank(name)[:, 512 * n:512 * n + 512], m_hid[:, e % 2, f, P * t:P * t + P],
                                      wd[:, f, 512 * n:512 * n + 512], start=(f == 0), stop=(f == 3))
                    last.then_inc(pair_full[pair(name)], 1)
            for t in range(NT):
                name = ("yT", t)
                pe.wait_ge(*free_after(("down", NE - 1, t)))
                pe.wait_ge(*free_before(name))
                for k in range(KD):
                    last = tr(bank(name)[:, P * k:P * k + P], m_y[:, t, P * k:P * k + P])
                last.then_inc(pair_full[pair(name)], 1)
            rms_sums(2)
            pe.wait_ge(s_fin_h, KD)
            for t in range(NT):
                name = ("fin", t)
                pe.wait_ge(*free_before(name))
                for k in range(KD):
                    last = tr(bank(name)[:, P * k:P * k + P], hT[:, k, P * t:P * t + P])
                last.then_inc(pair_full[pair(name)], 1)

        @block.scalar
        def _(act):
            A = nc.scalar.activation
            ch = Chain(act, "act_chain")
            dma = act.dma_start

            def rowsof(v, n):
                return v.rearrange("(n p) -> n p", p=P)

            st = s_st_in
            dma(stA[0:48, :], rowsof(I["ada_b"][0], 48)).then_inc(st, 16)
            dma(stA[48:56, :], rowsof(I["norm1_w"][0], 8)).then_inc(st, 16)
            dma(stA[56:64, :], rowsof(I["norm2_w"][0], 8)).then_inc(st, 16)
            dma(stA[64:72, :], rowsof(I["final_norm_w"], 8)).then_inc(st, 16)
            dma(stA[72:80, :], rowsof(I["c"][0], 8)).then_inc(st, 16)
            dma(stA[80:88, :], rowsof(I["c_ctx"], 8)).then_inc(st, 16)
            dma(stB[0:48, :], I["gdn_conv_w"][0].rearrange("j (n p) -> (j n) p", p=P)).then_inc(st, 16)
            dma(stB[48:56, :], I["rg_conv_w"][0].rearrange("j (n p) -> (j n) p", p=P)).then_inc(st, 16)
            dma(stB[56:58, :], rowsof(I["rg_conv_b"][0], 2)).then_inc(st, 16)
            dma(stB[58:66, :], I["rg_gate_b"][0].rearrange("d g (n p) -> (d g n) p", p=P)).then_inc(st, 16)
            dma(stB[66:70, :], I["rg_lambda"][0].rearrange("d (n p) -> (d n) p", p=P)).then_inc(st, 16)
            dma(stB[70:74, :], I["state_rglru"][0, 0].rearrange("d (n p) -> (d n) p", p=P)).then_inc(st, 16)
            dma(stB[74:78, :], I["hg_lb_logits"][0].rearrange("d (n p) -> (d n) p", p=P)).then_inc(st, 16)
            dma(stB[78:79, :], I["gdn_norm_w"]).then_inc(st, 16)
            for i in range(2):
                dma(stB[79:80, 64 * i:64 * i + 64], I["hg_norm_w"]).then_inc(st, 16)
            sm = s_small_in
            dma(wab[:, :, :], win[:, :, O_AB:O_AB + 16]).then_inc(sm, 16)
            dma(rw[:, :, :], I["router_w"].rearrange("(k p) e -> p k e", p=P)).then_inc(sm, 16)
            dma(rbias[:, :], I["router_b"].partition_broadcast(P)).then_inc(sm, 16)
            dma(alog[:, :], I["gdn_a_log"][0].rearrange("d h -> (d h)").partition_broadcast(P)).then_inc(sm, 16)
            dma(dtb[:, :], I["gdn_dt_bias"][0].rearrange("d h -> (d h)").partition_broadcast(P)).then_inc(sm, 16)
            dma(stateB[:, 1, :, :, :].rearrange("p d q v -> p (d q) v"),
                I["state_hgrn"][0, 0].rearrange("d (q e) k v -> (e k) (d q) v", e=2)).then_inc(s_sb_in, 16)
            act.wait_ge(s_wg_zero, 1)
            for n in range(8):
                for i in range(2):
                    dma(c_wg[64 * i:64 * i + 64, n, 64 * i:64 * i + 64],
                        I["rg_gate_w"][0, n // 4, n // 2 % 2, 2 * (n % 2) + i]).then_inc(s_wg_in, 16)

            act.wait_ge(*free_after(("stage", 0)))
            A(cs[:, :, 1], vecA[:, 72:80], ACT.Silu).then_inc(s_cs, 1)
            A(cs[:, :, 0], vecA[:, 80:88], ACT.Silu).then_inc(s_cs, 1)

            for i in range(12):
                act.wait_ge(*full_after(("ada", i)))
                A(modrow[0:2, 512 * i:512 * i + 512], bank(("ada", i))[0:2, 0:512], ACT.Copy).then_inc(pair_free[pair(("ada", i))], 1)

            def rms(n, scl, shift, sqfrom):
                sqfrom()
                for k in range(KD):
                    A(sq[:, k, :], xT[:, k, :], ACT.Square).then_inc(s_sq, 1)
                name = ("rms", n)
                act.wait_ge(*full_after(name))
                for a, b, out, g in segs(name):
                    ins = A(rb[:, a:b], out, ACT.Ln, scale=1.0 / D, bias=small[:, 0:1])
                    ch(ins) if g == 0 else ins.then_inc(pair_free[pair(name)], 1)
                act.wait_ge(*free_after(name))
                ch.sync()
                A(rb[:, :], rb[:, :], ACT.Exp, scale=-0.5).then_inc(s_rb, 1)
                if scl is not None:
                    for k in range(KD):
                        act.wait_ge(s_hraw, KD * n + k + 1)
                        for a, b, _, g in segs(name):
                            A(hT[:, k, a:b], hT[:, k, a:b], ACT.Identity, scale=scl[:, k, g:g + 1],
                                   bias=modT[:, shift + k, g:g + 1]).then_inc(s_h, 1)

            act.wait_ge(s_eps, 1)
            act.wait_ge(s_mod, 1)

            def silu_out(b):
                act.wait_ge(s_a_conv, b + 1)
                vT = a_o.rearrange("p a b -> p (a b)").rearrange("p (n t) -> p n t", t=T)
                dst = a_qk[:, b, :] if b < 8 else vT[:, b - 8, :]
                for a, e, g in SEG:
                    A(dst[:, a:e], a_cv[:, b % 2, a + 2 * g:e + 2 * g], ACT.Silu).then_inc(s_a_silu, 1)

            def l2_ln(b):
                name = ("ss", b)
                act.wait_ge(*full_after(name))
                for a, e, out, g in segs(name):
                    ins = A(a_rn[:, b, a:e], out, ACT.Ln, bias=small[:, 0:1])
                    ch(ins) if g == 0 else ins.then_inc(pair_free[pair(name)], 1)

            def x_ready():
                for t in range(NT):
                    act.wait_ge(*free_after(("xt", t)))

            rms(0, scl1, 0, x_ready)
            act.wait_ge(s_c_pad, 1)
            act.wait_ge(s_h, 16)
            for b in range(2):
                name = ("rgx", b)
                act.wait_ge(*full_after(name))
                lo, hi = bank(name)[:, 0:CTX], bank(name)[:, 512:1024]
                ch(A(c_x[:, b, 2:2 + CTX], lo, ACT.Copy))
                A(c_x[:, b, 4 + CTX:4 + T].rearrange("p (c r) -> p r c", r=ROWS),
                       hi.rearrange("p (r c) -> p r c", c=GRID_W), ACT.Copy).then_inc(pair_free[pair(name)], 1)
            for b in range(2):
                name = ("rgy", b)
                act.wait_ge(*full_after(name))
                lo, hi = bank(name)[:, 0:CTX], bank(name)[:, 512:1024]
                ch(A(c_yg[:, b, 0:CTX], lo, ACT.Gelu_apprx_tanh))
                A(c_yg[:, b, CTX:T].rearrange("p (c r) -> p r c", r=ROWS),
                       hi.rearrange("p (r c) -> p r c", c=GRID_W), ACT.Gelu_apprx_tanh).then_inc(pair_free[pair(name)], 1)
            act.wait_ge(s_c_lam, 1)
            ch(A(small[:, 8:12], small[:, 4:8], ACT.Exp))
            ch.sync()
            ch(A(small[:, 44:48], small[:, 44:48], ACT.Exp))
            A(small[:, 8:12], small[:, 8:12], ACT.Ln, bias=small[:, 1:2]).then_inc(s_c_ln, 1)
            for n in range(8):
                name = ("rgg", n)
                act.wait_ge(*full_after(name))
                for a, b, out, g in segs(name):
                    ins = A(c_g[:, n // 4, n // 2 % 2, n % 2, a:b], out, ACT.Sigmoid, bias=vb[:, 58 + n:59 + n])
                    ch(ins) if g == 0 else ins.then_inc(pair_free[pair(name)], 1)
            for n in (0, 1, 4, 5):
                act.wait_ge(*free_after(("rgg", n)))
            ch.sync()
            act.wait_ge(s_c_nc8, 1)
            for db in range(4):
                A(c_a[:, db, :], c_g[:, db // 2, 0, db % 2, :], ACT.Exp, scale=small[:, 12 + db:13 + db]).then_inc(s_c_a, 1)
            for db in range(4):
                A(c_t[:, db, :], c_g[:, db // 2, 0, db % 2, :], ACT.Tanh, scale=small[:, 12 + db:13 + db]).then_inc(s_c_a, 1)
            act.wait_ge(s_c_y, 1)
            A(c_t[:, :, :], c_h[:, :, :], ACT.Sqrt).then_inc(s_c_sqrt, 1)
            act.wait_ge(s_c_fin, 1)
            dma(O["new_rg"][0, 0].rearrange("d (n p) -> p (d n)", p=P), small[:, 20:24],
                allow_slow_non_contiguous=True).then_inc(s_state_stored, 16)
            act.wait_ge(s_c_done, 1)
            for b in range(2):
                name = ("hq", b)
                act.wait_ge(*full_after(name))
                for a, e, out, g in segs(name):
                    ins = A(b_q[:, b, a:e], out, ACT.Copy)
                    ch(ins) if g == 0 else ins.then_inc(pair_free[pair(name)], 1)
            for n in range(2):
                name = ("hi", n)
                act.wait_ge(*full_after(name))
                A(b_v[:, 4 * n:min(NT, 4 * n + 4), :], bank(name)[:, 0:256 * (4 if n == 0 else 1)]
                       .rearrange("p (t c) -> p t c", c=256), ACT.Copy).then_inc(pair_free[pair(name)], 1)
            for n in range(2):
                name = ("hgate", n)
                act.wait_ge(*full_after(name))
                A(b_g[:, 4 * n:min(NT, 4 * n + 4), :], bank(name)[:, 0:256 * (4 if n == 0 else 1)]
                       .rearrange("p (t c) -> p t c", c=256), ACT.Silu).then_inc(pair_free[pair(name)], 1)
            for n in range(4):
                name = ("hf", n)
                act.wait_ge(*full_after(name))
                for a, e, out, g in segs(name):
                    ch(A(b_f[:, n, a:e], out, ACT.Sigmoid))
                    ins = A(b_k[:, n, a:e], out, ACT.Sigmoid, scale=-1.0)
                    ch(ins) if g == 0 else ins.then_inc(pair_free[pair(name)], 1)
            act.wait_ge(s_b_m, 1)
            ch(A(b_f[:, :, :], b_f[:, :, :], ACT.Ln))
            A(b_Z[0][:, :, :], b_Z[0][:, :, :], ACT.Ln, scale=1.0 / LNSPLIT).then_inc(s_b_ln, 1)
            for l in range(7):
                act.wait_ge(s_b_d, l + 1)
                A(b_f[:, :, :], b_f[:, :, :], ACT.Exp).then_inc(s_b_e, 1)
            act.wait_ge(s_b_z, 7)
            A(b_f[:, :, :], b_b[:, :, :], ACT.Exp).then_inc(s_b_e, 1)
            act.wait_ge(s_b_d, 8)
            A(b_Z[1][:, :, :], b_Z[1][:, :, :], ACT.Exp).then_inc(s_b_e, 1)
            act.wait_ge(s_b_kd, 1)
            b_kdr = b_k.rearrange("p a t -> p (a t)").rearrange("p (t c) -> p t c", t=NT)
            for t in range(NT):
                act.wait_ge(*full_after(("kdt", t)))
                A(b_kdr[:, t, :], bank(("kdt", t))[:, 0:512], ACT.Copy).then_inc(pair_free[pair(("kdt", t))], 1)
            act.wait_ge(*free_after(("hs", 0)))
            dma(O["new_hgrn"][0, 0].rearrange("d (q e) k v -> (e k) (d q) v", e=2),
                stateB[:, 0, :, :, :].rearrange("p d q v -> p (d q) v")).then_inc(s_state_stored, 16)
            act.wait_ge(s_b_oall, 1)
            A(b_f[:, 0:2, :].rearrange("p a t -> p (a t)"), b_o[:, :, :].rearrange("p a t -> p (a t)"),
                   ACT.Square).then_inc(s_b_sq, 1)
            act.wait_ge(s_b_ss, 1)
            ch(A(small[:, 24:44], small[:, 24:44], ACT.Ln, scale=1.0 / HK, bias=small[:, 0:1]))
            ch.sync()
            A(small[:, 24:44], small[:, 24:44], ACT.Exp, scale=-0.5).then_inc(s_b_r, 1)
            for t in range(NT):
                act.wait_ge(*full_after(("hmix", t)))
                A(mixBC[:, 0:2, P * t:P * t + P], bank(("hmix", t))[:, 0:256].rearrange("p (a t) -> p a t", a=2),
                       ACT.Copy, scale=vb[:, 79:80]).then_inc(pair_free[pair(("hmix", t))], 1)
            act.wait_ge(s_a_pad, 1)
            for b in range(12):
                name = ("qkv", b)
                act.wait_ge(*full_after(name))
                if b >= 2:
                    act.wait_ge(s_a_conv, b - 1)
                for a, e, out, g in segs(name):
                    ins = A(a_pad[:, b % 2, 2 + a + 2 * g:2 + e + 2 * g], out, ACT.Copy)
                    ch(ins) if g == 0 else ins.then_inc(pair_free[pair(name)], 1)
                if b >= 1:
                    silu_out(b - 1)
            silu_out(11)
            for t in range(NT):
                act.wait_ge(*full_after(("gg", t)))
                A(a_g[:, t, :], bank(("gg", t))[:, 0:512], ACT.Silu).then_inc(pair_free[pair(("gg", t))], 1)
            sqs = a_K.rearrange("p a b -> p (a b)").rearrange("p (n t) -> p n t", t=T)
            act.wait_ge(s_a_silu, 24)
            for b in range(8):
                if b >= 4:
                    act.wait_ge(*full_after(("ss", b - 4)))
                A(sqs[:, b % 4, :], a_qk[:, b, :], ACT.Square).then_inc(s_a_sq, 1)
                if b >= 3:
                    l2_ln(b - 3)
            for b in range(5, 8):
                l2_ln(b)
            act.wait_ge(*free_after(("ss", 7)))
            act.wait_ge(*free_after(("ss", 6)))
            act.wait_ge(*free_after(("ss", 5)))
            act.wait_ge(*free_after(("ss", 4)))
            ch.sync()
            A(a_rn[:, :, :], a_rn[:, :, :], ACT.Exp, scale=-0.5).then_inc(s_a_rn, 1)
            act.wait_ge(s_a_z, 1)
            ch(A(a_w[:, :, :], a_w[:, :, :], ACT.Exp))
            ch(A(a_nea[:, :], alog[:, :], ACT.Exp))
            ch.sync()
            ch(A(a_beta[:, :, :], a_beta[:, :, :], ACT.Sigmoid))
            A(a_w[:, :, :], a_w[:, :, :], ACT.Ln, bias=small[:, 1:2]).then_inc(s_a_ln, 1)
            for t in range(NT):
                act.wait_ge(*full_after(("rows", t)))
                ch(A(a_K[:, t, :], bank(("rows", t))[:, 0:512], ACT.Copy))
                A(a_V[:, t, :], bank(("rows", t))[:, 512:1024], ACT.Copy).then_inc(pair_free[pair(("rows", t))], 1)
            act.wait_ge(*free_after(("gcol", 0)))
            A(a_beg[:, :, :], a_gc[:, :, :], ACT.Exp).then_inc(s_a_eg, 1)
            for s in range(NT):
                name = ("gb", s)
                act.wait_ge(*full_after(name))
                if s:
                    act.wait_ge(*full_after(("o", s - 1)))
                act.wait_ge(s_a_d, s + 1)
                A(a_dec[:, :, :], a_dec[:, :, :], ACT.Exp).then_inc(s_a_dec, 1)
                A(a_qe[:, :, :], bank(name).rearrange("p (a b) -> p a b", a=8), ACT.Exp).then_inc(pair_free[pair(name)], 1)
                act.wait_ge(*full_after(("u", s)))
                if s:
                    act.wait_ge(*full_after(("ds", s - 1)))
                A(a_U[:, :, :], bank(("u", s)).rearrange("p (a b) -> p a b", a=8), ACT.Copy).then_inc(pair_free[pair(("u", s))], 1)
                if s == 0:
                    act.wait_ge(*free_after(("ds", 0)))
                    dma(O["new_gdn"][0, 0].rearrange("d h k v -> k (d h) v"), a_S[:, 0, :, :]).then_inc(s_state_stored, 16)
            act.wait_ge(s_a_oall, 1)
            A(a_K[:, :, :], a_o[:, :, :], ACT.Square).then_inc(s_a_osq, 1)
            act.wait_ge(s_a_oss, 1)
            ch(A(a_r[:, :], a_r[:, :], ACT.Ln, scale=1.0 / P, bias=small[:, 0:1]))
            ch.sync()
            A(a_r[:, :], a_r[:, :], ACT.Exp, scale=-0.5).then_inc(s_a_orn, 1)
            for t in range(NT):
                act.wait_ge(*full_after(("gmix", t)))
                A(mixA[:, :, P * t:P * t + P], bank(("gmix", t))[:, 0:512].rearrange("p (a t) -> p a t", a=4),
                       ACT.Copy, scale=vb[:, 78:79]).then_inc(pair_free[pair(("gmix", t))], 1)

            def x1_ready():
                act.wait_ge(s_state_stored, 48)
                for n in range(KD):
                    act.wait_ge(*free_after(("out", n)))

            rms(1, scl2, 24, x1_ready)
            act.wait_ge(s_r_max, 1)
            A(m_p[:, :, :], m_p[:, :, :], ACT.Exp).then_inc(s_r_exp, 1)
            for e in range(NE):
                for f in range(4):
                    name = ("gate", e, f)
                    act.wait_ge(*full_after(name))
                    n = 4 * e + f
                    if n >= 2:
                        act.wait_ge(s_hid, 2 * (n - 1))
                    for a, b, out, g in segs(name):
                        ins = A(m_sg[:, f % 2, a:b], out, ACT.Silu)
                        ins.then_inc(s_m_sg, 1) if g == 0 else ins.then_inc(pair_free[pair(name)], 1)

            def x2_ready():
                for t in range(NT):
                    act.wait_ge(s_x2, t + 1)

            rms(2, None, None, x2_ready)
            for t in range(NT):
                name = ("fin", t)
                act.wait_ge(*full_after(name))
                if t >= 2:
                    act.wait_ge(s_y_stored[t % 2], 16 * (t // 2))
                ch(A(m_out[:, t % 2, 0:512], bank(name)[:, 0:512], ACT.Copy))
                A(m_out[:, t % 2, 512:1024], bank(name)[:, 512:1024], ACT.Copy).then_inc(pair_free[pair(name)], 1)

        @block.gpsimd
        def _(pool):
            ch = Chain(pool, "pool_chain")
            ch(nc.gpsimd.memset(ident[:, :], 0.0))
            ch.sync()
            nc.gpsimd.affine_select(out=ident[:, :], in_=ident[:, :], compare_op=ALU.not_equal, fill=1.0,
                                         base=0, pattern=[[-1, P]], channel_multiplier=1).then_inc(s_ident, 1)
            ch(nc.gpsimd.memset(ones[:, :], 1.0))
            ch.sync()
            for d, sign in ((0, 1), (1, -1)):
                ch(nc.gpsimd.affine_select(out=tri[:, d, :], in_=ones[:, :], compare_op=ALU.is_ge, fill=0.0,
                                           base=0, pattern=[[sign, P]], channel_multiplier=-sign))
            ch(nc.gpsimd.iota(vi[:, 0, :], pattern=[[1, P]], base=0, channel_multiplier=0))
            nc.gpsimd.iota(vi[:, 1, :], pattern=[[0, P]], base=0, channel_multiplier=1).then_inc(s_iota, 1)
            nc.gpsimd.memset(c_wg[:, :, :], 0.0).then_inc(s_wg_zero, 1)
            pool.wait_ge(*full_after(("modT", 0)))
            nc.gpsimd.memset(c_x[:, :, :], 0.0).then_inc(s_c_pad, 1)
            pool.wait_ge(*full_after(("hmix", NT - 1)))
            nc.gpsimd.memset(a_pad[:, :, :], 0.0).then_inc(s_a_pad, 1)
            nc.gpsimd.memset(a_S[:, 0, :, :], 0.0).then_inc(s_a_state, 1)
            pool.dma_start(a_S[:, 1, :, :], I["state_gdn"][0, 0].rearrange("d h k v -> k (d h) v")).then_inc(s_sg_in, 16)
            for s in range(NT):
                pool.wait_ge(*free_after(("kk", s)))
                for l in range(7):
                    if l >= 2:
                        pool.wait_ge(*full_after(("t1", s, l - 2)))
                    elif s and l == 0:
                        pool.wait_ge(*full_after(("u", s - 1)))
                    for d in range(2):
                        ins = nc.gpsimd.tensor_tensor(out=a_CT[l % 2][:, 4 * d:4 * d + 4, :], in0=a_AT[:, 4 * d:4 * d + 4, :],
                                                      in1=wide(lmask[:, d, l, :], 1, 4), op=MULT)
                        ch(ins) if d == 0 else ins.then_inc(s_a_ct, 1)

        @block.vector
        def _(dve):
            ch = Chain(dve, "dve_chain")
            V = nc.vector
            TT, TS, STT = V.tensor_tensor, V.tensor_scalar, V.scalar_tensor_tensor

            def link(ins):
                ch(ins)
                ch.sync()

            ch(V.memset(small[:, 0:1], EPS))
            V.memset(small[:, 1:2], 1.0).then_inc(s_eps, 1)
            ch(V.memset(stateB[:, 0, :, :, :], 0.0))
            dve.wait_ge(s_iota, 1)
            link(TT(out=vi[:, 0, :], in0=vi[:, 0, :], in1=vi[:, 1, :], op=ALU.bitwise_xor))
            link(V.tensor_copy(vf[:, 0, :], vi[:, 0, :]))
            for l, w in enumerate(LEVELS):
                link(TS(vf[:, 1, :], vf[:, 0, :], float(w), None, ALU.is_ge))
                link(STT(out=vf[:, 1, :], in0=vf[:, 0, :], scalar=float(2 * w), in1=vf[:, 1, :], op0=ALU.is_lt, op1=MULT))
                for d in range(2):
                    link(TT(out=lmask[:, d, l, :], in0=vf[:, 1, :], in1=tri[:, d, :], op=MULT))
            dve.wait_ge(*full_after(("stage", 0)))
            ch(V.tensor_copy(vecA[:, :], bank(("stage", 0))[:, 0:88]))
            V.tensor_copy(vecB[:, :], bank(("stage", 0))[:, 512:592]).then_inc(pair_free[pair(("stage", 0))], 1)
            for t in range(NT):
                name = ("xt", t)
                dve.wait_ge(*full_after(name))
                V.tensor_copy(xT[:, :, P * t:P * t + P], bank(name).rearrange("p (a b) -> p a b", a=KD)).then_inc(pair_free[pair(name)], 1)
            name = ("modT", 0)
            dve.wait_ge(*full_after(name))
            dve.wait_ge(*free_after(("stage", 0)))
            TT(out=modT[:, :, :], in0=bank(name)[:, 0:96].rearrange("p (a b) -> p a b", b=2),
                    in1=wide(vecA[:, 0:48], 2, 2), op=ADD).then_inc(pair_free[pair(name)], 1)
            dve.wait_ge(*free_after(name))
            ch(STT(out=scl1[:, :, :], in0=modT[:, 8:16, :], scalar=1.0, in1=wide(vecA[:, 48:56], 2, 2), op0=ADD, op1=MULT))
            STT(out=scl2[:, :, :], in0=modT[:, 32:40, :], scalar=1.0, in1=wide(vecA[:, 56:64], 2, 2), op0=ADD, op1=MULT).then_inc(s_mod, 1)

            def scale_x(n):
                dve.wait_ge(s_rb, n + 1)
                for k in range(KD):
                    TT(out=hT[:, k, :], in0=xT[:, k, :], in1=rb[:, :], op=MULT).then_inc(s_hraw, 1)

            for t in range(NT):
                dve.wait_ge(*free_after(("xt", t)))
            ch(STT(out=small[:, 4:8], in0=vb[:, 66:70], scalar=-1.0, in1=vb[:, 66:70], op0=MULT, op1=MIN))
            ch(TT(out=small[:, 44:48], in0=vb[:, 74:78], in1=vb[:, 74:78], op=SUB))
            TS(small[:, 16:20], vb[:, 66:70], -1.0, 0.0, MULT, MAX).then_inc(s_c_lam, 1)
            scale_x(0)
            for b in range(2):
                dve.wait_ge(*free_after(("rgx", b)))
                link(TS(c_u[:, b, :], c_x[:, b, 0:CONVW], vb[:, 48 + b:49 + b], vb[:, 56 + b:57 + b], MULT, ADD))
                for j in range(1, 4):
                    ins = STT(out=c_u[:, b, :], in0=c_x[:, b, j:j + CONVW], scalar=vb[:, 48 + 2 * j + b:49 + 2 * j + b],
                              in1=c_u[:, b, :], op0=MULT, op1=ADD)
                    link(ins) if j < 3 else ins.then_inc(s_conv_c, 1)
            dve.wait_ge(s_conv_c, 2)
            dve.wait_ge(s_c_ln, 1)
            link(TT(out=small[:, 8:12], in0=small[:, 8:12], in1=small[:, 16:20], op=ADD))
            TS(small[:, 12:16], small[:, 8:12], -RG_C, None, MULT).then_inc(s_c_nc8, 1)
            link(V.reciprocal(small[:, 48:52], small[:, 44:48]))
            link(TT(out=small[:, 48:52], in0=small[:, 48:52], in1=small[:, 44:48], op=MULT))
            link(TT(out=small[:, 48:52], in0=small[:, 48:52], in1=small[:, 48:52], op=SUB))
            link(TS(small[:, 52:56], small[:, 48:52], -1.0, 1.0, MULT, ADD))
            dve.wait_ge(s_c_a, 8)
            link(TT(out=c_h[:, :, :], in0=c_a[:, :, :], in1=c_a[:, :, :], op=MULT))
            link(STT(out=c_h[:, :, :], in0=c_h[:, :, :], scalar=1.0, in1=c_t[:, :, :], op0=ADD, op1=MULT))
            TS(c_h[:, :, :], c_h[:, :, :], -1.0, 0.0, MULT, MAX).then_inc(s_c_y, 1)
            for d in range(2):
                for a, e, g in SEG:
                    ch(TT(out=c_g[:, d, 1, :, a:e], in0=c_g[:, d, 1, :, a:e], in1=c_u[:, :, a + 2 * g:e + 2 * g], op=MULT))
            ch.sync()
            dve.wait_ge(s_c_sqrt, 1)
            for d in range(2):
                ch(TT(out=c_t[:, 2 * d:2 * d + 2, :], in0=c_t[:, 2 * d:2 * d + 2, :], in1=c_g[:, d, 1, :, :], op=MULT))
            ch.sync()
            for db in range(4):
                for a, e, g in SEG:
                    way = slice(None, None, -1) if db // 2 else slice(None)
                    ch(V.tensor_tensor_scan(c_h[:, db, a:e][:, way], c_a[:, db, a:e][:, way], c_t[:, db, a:e][:, way],
                                            vb[:, 70 + db:71 + db] if g else 0.0, MULT, ADD))
            ch.sync()
            ch(V.tensor_copy(small[:, 20:22], c_h[:, 0:2, CTX - 1]))
            V.tensor_copy(small[:, 22:24], c_h[:, 2:4, 0]).then_inc(s_c_fin, 1)
            ch.sync()
            dve.wait_ge(s_c_fin, 1)
            link(TT(out=c_h[:, 0:2, :], in0=c_h[:, 0:2, :], in1=c_h[:, 2:4, :], op=ADD))
            for b in range(2):
                TT(out=mixBC[:, 2 + b, 0:CTX], in0=c_h[:, b, 0:CTX], in1=c_yg[:, b, 0:CTX], op=MULT).then_inc(s_c_mix, 1)
                ins = TT(out=mixBC[:, 2 + b, CTX:T].rearrange("p (r c) -> p c r", c=GRID_W),
                         in0=c_h[:, b, CTX:T].rearrange("p (c r) -> p c r", r=ROWS),
                         in1=c_yg[:, b, CTX:T].rearrange("p (c r) -> p c r", r=ROWS), op=MULT)
                ins.then_inc(s_c_mix, 1)
            dve.wait_ge(s_c_mix, 4)
            V.memset(b_o[:, :, :], 0.0).then_inc(s_c_done, 1)
            dve.wait_ge(*free_after(("hf", 3)))
            for dp in range(4):
                ch(TS(b_f[:, dp, :], b_f[:, dp, :], small[:, 52 + dp:53 + dp], small[:, 48 + dp:49 + dp], MULT, ADD))
                ins = TS(b_k[:, dp, :], b_k[:, dp, :], small[:, 52 + dp:53 + dp], None, MULT)
                ch(ins) if dp < 3 else ins.then_inc(s_b_k, 1)
            dve.wait_ge(s_b_k, 1)
            ch.sync()
            link(TS(b_Z[0][:, :, :], b_f[:, :, :], F_MIN, LNSPLIT, MAX, MIN))
            TS(b_f[:, :, :], b_f[:, :, :], LNSPLIT, None, MAX).then_inc(s_b_m, 1)
            dve.wait_ge(s_b_ln, 1)
            link(TT(out=b_f[:, :, :], in0=b_f[:, :, :], in1=b_Z[0][:, :, :], op=ADD))
            for dp in range(4):
                way = slice(None, None, -1) if dp // 2 else slice(None)
                for t in range(NT):
                    ch(V.tensor_tensor_scan(b_b[:, dp, P * t:P * t + P][:, way], ones[:, :],
                                            b_f[:, dp, P * t:P * t + P][:, way], 0.0, MULT, ADD))
            ch.sync()

            def blocks(v, d, w):
                v = v[:, 2 * d:2 * d + 2, :] if v.shape[1] == 4 else v
                return v.rearrange("p a t -> p (a t)").rearrange("p (n w) -> p n w", w=w)

            def level_out(L):
                for t in range(NT):
                    name = ("lev", L, t)
                    dve.wait_ge(*full_after(name))
                    src = bank(name).rearrange("p (e d q i) -> p e d q i", e=2, d=2, q=2)
                    dst = b_at[:, t, :, :].rearrange("p (e d q) i -> p e d q i", e=2, d=2)
                    if L == 0:
                        TT(out=b_at[:, t, :, :], in0=bank(name).rearrange("p (a i) -> p a i", a=8),
                                in1=wide(ident[:, :], 1, 8), op=MULT).then_inc(pair_free[pair(name)], 1)
                    else:
                        dve.wait_ge(*free_after(("lev", L - 1, t)))
                        msk = wide(lmask[:, :, L - 1, :].bitcast(I32), 2, 2)
                        ch(V.copy_predicated(dst[:, 0], msk, src[:, 0]))
                        V.copy_predicated(dst[:, 1], msk, src[:, 1]).then_inc(pair_free[pair(name)], 1)

            for l, s in enumerate(LEVELS):
                w, n = 2 * s, 2 * T // (2 * s)
                L = l + 1
                for d in range(2):
                    b, E = blocks(b_b, d, w), blocks(b_f, d, w)
                    mid = b[:, :, s - 1:s] if d == 0 else b[:, :, s:s + 1]
                    mid = mid.to_broadcast([P, n, s])
                    lo, hi = b[:, :, 0:s], b[:, :, s:w]
                    ch(TT(out=E[:, :, 0:s], in0=mid if d == 0 else lo, in1=lo if d == 0 else mid, op=SUB))
                    ins = TT(out=E[:, :, s:w], in0=hi if d == 0 else mid, in1=mid if d == 0 else hi, op=SUB)
                    ch(ins) if d == 0 else ins.then_inc(s_b_d, 1)
                level_out(l)
                dve.wait_ge(s_b_e, L)
                if L >= 3:
                    dve.wait_ge(*full_after(("lev", L - 2, NT - 1)))
                for d in range(2):
                    E, Z, q, k = (blocks(v, d, w) for v in (b_f, b_Z[L % 2], b_q, b_k))
                    left, right = (k, q) if d == 0 else (q, k)
                    ch(TT(out=Z[:, :, 0:s], in0=left[:, :, 0:s], in1=E[:, :, 0:s], op=MULT))
                    ins = TT(out=Z[:, :, s:w], in0=right[:, :, s:w], in1=E[:, :, s:w], op=MULT)
                    ch(ins) if d == 0 else ins.then_inc(s_b_z, 1)
                ch.sync()
                dve.wait_ge(s_b_z, L)
            level_out(7)
            dve.wait_ge(s_b_e, 8)
            for d in range(2):
                ch(TT(out=b_Z[0][:, 2 * d:2 * d + 2, :], in0=b_q[:, :, :], in1=b_f[:, 2 * d:2 * d + 2, :], op=MULT))
            ends = b_f.rearrange("p q (t c) -> p t q c", c=P)
            ch(V.tensor_copy(b_end[:, :, 0:2], ends[:, :, 0:2, P - 1]))
            ch(V.tensor_copy(b_end[:, 0:1, 2:4], ends[:, 0:1, 2:4, 0]))
            ch(V.tensor_copy(b_end[:, 1:NT, 2:4], ends[:, 1:NT, 2:4, 0][:, ::-1]))
            for d in range(2):
                b, Z = blocks(b_b, d, P), blocks(b_Z[1], d, P)
                end = (b[:, :, P - 1:P] if d == 0 else b[:, :, 0:1]).to_broadcast([P, 2 * NT, P])
                ins = TT(out=Z, in0=end, in1=b, op=SUB)
                ch(ins) if d == 0 else ins.then_inc(s_b_d, 1)
            ch.sync()
            dve.wait_ge(s_b_e, 9)
            TT(out=b_Z[1][:, :, :], in0=b_Z[1][:, :, :], in1=b_k[:, :, :], op=MULT).then_inc(s_b_kd, 1)
            dve.wait_ge(s_sb_in, 16)
            V.memset(small[:, 57:58], 0.0).then_inc(s_b_state, 1)
            ch.sync()
            for s in range(NT):
                name = ("ho", s)
                dve.wait_ge(*full_after(name))
                for d in range(2):
                    o = b_o[:, (FWD, BWD)[d][s], :].rearrange("p (q e v) -> p e q v", q=2, e=2)
                    src = bank(name).rearrange("p (e x) -> p e x", e=2)[:, :, P * d:P * d + P]
                    ins = TT(out=o, in0=src.rearrange("p e (q v) -> p e q v", q=2), in1=o, op=ADD)
                    if d == 0:
                        link(ins)
                    else:
                        ins.then_inc(pair_free[pair(name)], 1)
                name = ("hs", s)
                dve.wait_ge(*full_after(name))
                S = stateB[:, min(s, 1), :, :, :].rearrange("p d q v -> p (d q) v")
                link(TT(out=S, in0=S, in1=wide(b_end[:, s, :], 2, HK), op=MULT))
                src = bank(name)[:, 0:512].rearrange("p (c v) -> p c v", c=4)
                ch(TT(out=S[0:64], in0=src[0:64, :, 0:64], in1=S[0:64], op=ADD))
                TT(out=S[64:128], in0=src[64:128, :, 64:128], in1=S[64:128], op=ADD).then_inc(pair_free[pair(name)], 1)
                dve.wait_ge(*free_after(name))
                dve.wait_ge(*free_after(("ho", s)))
                ch.sync()
            V.memset(small[:, 58:59], 0.0).then_inc(s_b_oall, 1)
            dve.wait_ge(s_b_sq, 1)
            V.tensor_reduce(small[:, 24:44], b_f[:, 0:2, :].rearrange("p a t -> p (a t)")
                                 .rearrange("p (n v) -> p n v", v=HK), AX.X, ADD).then_inc(s_b_ss, 1)
            dve.wait_ge(s_b_r, 1)
            o = b_o.rearrange("p t c -> p (t c)").rearrange("p (n v) -> p n v", v=HK)
            link(TT(out=o, in0=o, in1=wide(small[:, 24:44], 2, HK), op=MULT))
            TT(out=b_o[:, :, :], in0=b_o[:, :, :], in1=b_g[:, :, :], op=MULT).then_inc(s_b_on, 1)
            for b in range(12):
                dve.wait_ge(*free_after(("qkv", b)))
                if b >= 2:
                    dve.wait_ge(s_a_silu, 2 * (b - 1))
                link(TS(a_cv[:, b % 2, :], a_pad[:, b % 2, 0:CONVW], vb[:, b:b + 1], None, MULT))
                for j in range(1, 4):
                    ins = STT(out=a_cv[:, b % 2, :], in0=a_pad[:, b % 2, j:j + CONVW], scalar=vb[:, 12 * j + b:12 * j + b + 1],
                              in1=a_cv[:, b % 2, :], op0=MULT, op1=ADD)
                    link(ins) if j < 3 else ins.then_inc(s_a_conv, 1)
            name = ("ab", 0)
            dve.wait_ge(*full_after(name))
            dve.wait_ge(s_small_in, 16 * 5)
            ab = bank(name)[:, 0:16 * NT].rearrange("p (t c) -> p t c", c=16)
            ch(TT(out=a_z[:, :, :], in0=ab[:, :, 0:8], in1=wide(dtb[:, :], 1, NT), op=ADD))
            V.tensor_copy(a_beta[:, :, :], ab[:, :, 8:16]).then_inc(pair_free[pair(name)], 1)
            dve.wait_ge(*free_after(name))
            ch.sync()
            link(STT(out=a_w[:, :, :], in0=a_z[:, :, :], scalar=-1.0, in1=a_z[:, :, :], op0=MULT, op1=MIN))
            TS(a_z[:, :, :], a_z[:, :, :], 0.0, None, MAX).then_inc(s_a_z, 1)
            dve.wait_ge(s_a_rn, 1)
            ch(STT(out=a_qk[:, 0:4, :], in0=a_qk[:, 0:4, :], scalar=float(P) ** -0.5, in1=a_rn[:, 0:4, :], op0=MULT, op1=MULT))
            TT(out=a_qk[:, 4:8, :], in0=a_qk[:, 4:8, :], in1=a_rn[:, 4:8, :], op=MULT).then_inc(s_a_norm, 1)
            dve.wait_ge(s_a_ln, 1)
            dve.wait_ge(s_a_z, 1)
            link(TT(out=a_w[:, :, :], in0=a_w[:, :, :], in1=a_z[:, :, :], op=ADD))
            STT(out=a_la[:, :, :], in0=a_w[:, :, :], scalar=-1.0, in1=wide(a_nea[:, :], 1, NT), op0=MULT, op1=MULT).then_inc(s_a_la, 1)
            name = ("gcol", 0)
            dve.wait_ge(*full_after(name))
            V.tensor_copy(a_gc[:, :, :], bank(name)[:, 0:8 * NT].rearrange("p (t c) -> p t c", c=8)).then_inc(pair_free[pair(name)], 1)
            dve.wait_ge(s_a_eg, 1)
            link(TT(out=a_beg[:, :, :], in0=a_beg[:, :, :], in1=a_beta[:, :, :], op=MULT))
            for dst, src in ((s_beta, a_beta), (s_gc, a_gc), (s_beg, a_beg)):
                ch(V.tensor_copy(dst[:, :, 0:4], src[:, :, 0:4]))
                ch(V.tensor_copy(dst[:, 0:1, 4:8], src[:, 0:1, 4:8]))
                ch(V.tensor_copy(dst[:, 1:NT, 4:8], src[:, 1:NT, 4:8][:, ::-1]))
            ch.sync()
            dve.wait_ge(*free_after(("rows", NT - 1)))
            ch(V.memset(a_o[:, :, :], 0.0))
            eight = lambda v: v.rearrange("p (a b) -> p a b", a=8)
            for s in range(NT):
                tile = lambda d: (FWD, BWD)[d][s]
                name = ("gb", s)
                dve.wait_ge(*full_after(name))
                if s:
                    dve.wait_ge(*full_after(("ds", s - 1)))
                link(TT(out=a_dec[:, :, :], in0=eight(bank(name)), in1=wide(s_gc[:, s, :], 2, P), op=SUB))
                TS(a_dec[:, :, :], a_dec[:, :, :], 0.0, None, MIN).then_inc(s_a_d, 1)
                dve.wait_ge(s_a_dec, s + 1)
                dve.wait_ge(*free_after(name))
                for d in range(2):
                    last = P - 1 if d == 0 else 0
                    h = slice(4 * d, 4 * d + 4)
                    ch(TT(out=a_Kd[:, h, :], in0=a_K[:, tile(d), :].rearrange("p (h c) -> p h c", h=4),
                          in1=a_dec[:, h, last:last + 1].to_broadcast([P, 4, P]), op=MULT))
                    ch(V.tensor_copy(a_ge[:, s, h], a_qe[:, h, last]))
                ch.sync()
                for d in range(2):
                    h = slice(4 * d, 4 * d + 4)
                    ch(TT(out=a_qe[:, h, :], in0=a_qe[:, h, :], in1=a_qk[:, 0:4, P * tile(d):P * tile(d) + P], op=MULT))
                    ch(TT(out=a_dec[:, h, :], in0=a_dec[:, h, :], in1=wide(tri[:, d, :], 1, 4), op=MULT))
                ch.sync()
                if s:
                    dve.wait_ge(s_a_ct, 7 * s)
                name = ("kk", s)
                dve.wait_ge(*full_after(name))
                TT(out=a_AT[:, :, :], in0=eight(bank(name)), in1=a_dec[:, :, :], op=MULT).then_inc(pair_free[pair(name)], 1)
                name = ("kq", s)
                dve.wait_ge(*full_after(name))
                TT(out=a_dec[:, :, :], in0=eight(bank(name)), in1=a_dec[:, :, :], op=MULT).then_inc(pair_free[pair(name)], 1)
                for l in range(7):
                    name = ("t1", s, l)
                    dve.wait_ge(*full_after(name))
                    TT(out=a_T1[:, :, :], in0=eight(bank(name)), in1=wide(s_beta[:, s, :], 2, P), op=MULT).then_inc(pair_free[pair(name)], 1)
                    if l == 0:
                        dve.wait_ge(*free_after(name))
                        TT(out=a_X[:, :, :], in0=wide(ident[:, :], 1, 8), in1=a_T1[:, :, :], op=SUB).then_inc(s_a_x0, 1)
                        dve.wait_ge(s_a_x0, s + 1)
                    elif l < 6:
                        name = ("dx", s, l)
                        dve.wait_ge(*full_after(name))
                        if l > 1:
                            dve.wait_ge(*free_after(("dx", s, l - 1)))
                        TT(out=a_X[:, :, :], in0=a_X[:, :, :], in1=eight(bank(name)), op=SUB).then_inc(pair_free[pair(name)], 1)
                    name = ("dxt", s, l)
                    dve.wait_ge(*full_after(name))
                    if l:
                        dve.wait_ge(*free_after(("dxt", s, l - 1)))
                    xt0 = a_XT[:, :, :] if l else wide(ident[:, :], 1, 8)
                    TT(out=a_XT[:, :, :], in0=xt0, in1=eight(bank(name)), op=SUB).then_inc(pair_free[pair(name)], 1)
                name = ("ks", s)
                dve.wait_ge(*full_after(name))
                TT(out=a_CT[1][:, :, :], in0=eight(bank(name)), in1=wide(s_beg[:, s, :], 2, P), op=MULT).then_inc(pair_free[pair(name)], 1)
                for d in range(2):
                    h = slice(4 * d, 4 * d + 4)
                    ch(TT(out=a_CT[0][:, h, :], in0=a_V[:, tile(d), :].rearrange("p (h c) -> p h c", h=4),
                          in1=wide(s_beta[:, s, h], 2, P), op=MULT))
                ch.sync()
                dve.wait_ge(*free_after(name))
                TT(out=a_CT[0][:, :, :], in0=a_CT[0][:, :, :], in1=a_CT[1][:, :, :], op=SUB).then_inc(s_a_rhs, 1)
                dve.wait_ge(s_a_rhs, s + 1)
                name = ("o", s)
                dve.wait_ge(*full_after(name))
                for d in range(2):
                    o = a_o[:, tile(d), :]
                    ins = TT(out=o, in0=bank(name)[:, 512 * d:512 * d + 512], in1=o, op=ADD)
                    if d == 0:
                        link(ins)
                    else:
                        ins.then_inc(pair_free[pair(name)], 1)
                name = ("ds", s)
                dve.wait_ge(*full_after(name))
                S = a_S[:, min(s, 1), :, :]
                if s == 1:
                    dve.wait_ge(s_sg_in, 16)
                if s == 0:
                    dve.wait_ge(s_a_state, 1)
                link(TT(out=S, in0=S, in1=wide(a_ge[:, s, :], 2, P), op=MULT))
                TT(out=S, in0=S, in1=eight(bank(name)), op=ADD).then_inc(pair_free[pair(name)], 1)
                dve.wait_ge(*free_after(name))
                dve.wait_ge(*free_after(("o", s)))
            V.memset(small[:, 59:60], 0.0).then_inc(s_a_oall, 1)
            dve.wait_ge(s_a_osq, 1)
            V.tensor_reduce(a_r[:, :], a_K.rearrange("p t (h v) -> p (t h) v", h=4), AX.X, ADD).then_inc(s_a_oss, 1)
            dve.wait_ge(s_a_orn, 1)
            o = a_o.rearrange("p t (h v) -> p (t h) v", h=4)
            link(TT(out=o, in0=o, in1=wide(a_r[:, :], 2, P), op=MULT))
            TT(out=a_o[:, :, :], in0=a_o[:, :, :], in1=a_g[:, :, :], op=MULT).then_inc(s_a_on, 1)
            for n in range(KD):
                name = ("out", n)
                dve.wait_ge(*full_after(name))
                for a, e, out, g in segs(name):
                    ins = STT(out=xT[:, n, a:e], in0=out, scalar=modT[:, 16 + n, g:g + 1], in1=xT[:, n, a:e],
                              op0=MULT, op1=ADD)
                    ch(ins) if g == 0 else ins.then_inc(pair_free[pair(name)], 1)
            for n in range(KD):
                dve.wait_ge(*free_after(("out", n)))
            scale_x(1)
            name = ("router", 0)
            dve.wait_ge(*full_after(name))
            link(TT(out=m_p[:, :, :], in0=bank(name)[:, 0:NT * NE].rearrange("p (t e) -> p t e", e=NE),
                    in1=wide(rbias[:, :], 1, NT), op=ADD))
            link(V.tensor_reduce(m_col[:, 0:NT], m_p[:, :, :], AX.X, MAX))
            V.memset(m_gg[:, :, :], 0.0).then_inc(pair_free[pair(name)], 1)
            TT(out=m_p[:, :, :], in0=m_p[:, :, :], in1=wide(m_col[:, 0:NT], 2, NE), op=SUB).then_inc(s_r_max, 1)
            dve.wait_ge(s_r_exp, 1)
            link(V.tensor_reduce(m_col[:, 0:NT], m_p[:, :, :], AX.X, ADD))
            link(V.reciprocal(m_col[:, 8:8 + NT], m_col[:, 0:NT]))
            link(TT(out=m_p[:, :, :], in0=m_p[:, :, :], in1=wide(m_col[:, 8:8 + NT], 2, NE), op=MULT))

            def rank4(values, rank, tmp):
                for i in range(4):
                    ch(V.memset(rank[:, :, i:i + 1], float(i)))
                ch.sync()
                for off in range(1, 4):
                    n = 4 - off
                    link(TT(out=tmp[:, :, 0:n], in0=values[:, :, off:4], in1=values[:, :, 0:n], op=ALU.is_gt))
                    link(TT(out=rank[:, :, 0:n], in0=rank[:, :, 0:n], in1=tmp[:, :, 0:n], op=ADD))
                    link(TT(out=rank[:, :, off:4], in0=rank[:, :, off:4], in1=tmp[:, :, 0:n], op=SUB))

            fours = lambda v: v.rearrange("p t e -> p (t e)").rearrange("p (n e) -> p n e", e=4)
            rank4(fours(m_p), fours(m_rank), fours(m_gt))
            link(STT(out=m_gate[:, :, :], in0=m_rank[:, :, :], scalar=2.0, in1=m_p[:, :, :], op0=ALU.is_lt, op1=MULT))
            link(V.tensor_reduce(m_gs.rearrange("p t g -> p (t g)"), fours(m_gate), AX.X, ADD))
            dve.wait_ge(*free_after(("router", 0)))
            rank4(m_gs, m_gr, m_gg)
            link(TS(m_gr[:, :, :], m_gr[:, :, :], 1.0, None, ALU.is_lt))
            link(TT(out=fours(m_gate), in0=fours(m_gate), in1=wide(m_gr.rearrange("p t g -> p (t g)"), 2, 4), op=MULT))
            link(V.tensor_reduce(m_col[:, 0:NT], m_gate[:, :, :], AX.X, ADD))
            link(V.reciprocal(m_col[:, 8:8 + NT], m_col[:, 0:NT]))
            link(TT(out=m_gate[:, :, :], in0=m_gate[:, :, :], in1=wide(m_col[:, 8:8 + NT], 2, NE), op=MULT))
            link(V.memset(m_y[:, :, :], 0.0))
            for e in range(NE):
                for f in range(4):
                    if e >= 2 and f == 0:
                        dve.wait_ge(*full_after(("down", e - 2, NT - 1)))
                    dve.wait_ge(*free_after(("gate", e, f)))
                    name = ("up", e, f)
                    dve.wait_ge(*full_after(name))
                    for a, b, out, g in segs(name):
                        ins = TT(out=m_hid[:, e % 2, f, a:b], in0=out, in1=m_sg[:, f % 2, a:b], op=MULT)
                        ins.then_inc(s_hid, 1)
                    dve.wait_ge(s_hid, 8 * e + 2 * f + 2)
                    V.memset(small[:, 60:61], 0.0).then_inc(pair_free[pair(name)], 1)
                for t in range(NT):
                    name = ("down", e, t)
                    dve.wait_ge(*full_after(name))
                    if e:
                        dve.wait_ge(*free_after(("down", e - 1, t)))
                    STT(out=m_y[:, t, :], in0=bank(name), scalar=m_gate[:, t, e:e + 1], in1=m_y[:, t, :],
                             op0=MULT, op1=ADD).then_inc(pair_free[pair(name)], 1)
            for t in range(NT):
                name = ("yT", t)
                dve.wait_ge(*full_after(name))
                g = min(t, 1)
                TT(out=m_tmp[:, :, :], in0=eight(bank(name)), in1=wide(modT[:, 40:48, g], 2, P), op=MULT).then_inc(pair_free[pair(name)], 1)
                dve.wait_ge(*free_after(name))
                TT(out=xT[:, :, P * t:P * t + P], in0=xT[:, :, P * t:P * t + P], in1=m_tmp[:, :, :], op=ADD).then_inc(s_x2, 1)
                dve.wait_ge(s_x2, t + 1)
            dve.wait_ge(s_rb, 3)
            for k in range(KD):
                STT(out=hT[:, k, :], in0=xT[:, k, :], scalar=vecA[:, 64 + k:65 + k], in1=rb[:, :],
                         op0=MULT, op1=MULT).then_inc(s_fin_h, 1)


def build(nc, inputs):
    arrays, I = {}, {}
    for name, a in inputs.items():
        a = np.ascontiguousarray(a)
        arrays[f"in_{name}"] = a
        I[name] = nc.dram_tensor(f"in_{name}", a.shape, mybir.dt.from_np(a.dtype), kind="ExternalInput").ap()
    O = {}
    for name, shape in OUTS.items():
        O[name] = nc.dram_tensor(f"out_{name}", shape, F32, kind="ExternalOutput").ap()
    layer_program(nc, I, O)
    return arrays


OUTS = {"y_prompt": (1, CTX, D), "y_sample": (1, LAT, D), "new_gdn": (1, 1, 2, GH, P, P),
        "new_hgrn": (1, 1, 2, HH, HK, HK), "new_rg": (1, 1, 2, 256)}


def kernel(**inputs):
    import concourse.bacc as _bacc
    from concourse.bass_utils import run_bass_kernel_spmd as _run

    nc = _bacc.Bacc("TRN2", target_bir_lowering=False, num_devices=1)
    arrays = build(nc, inputs)
    r = _run(nc, [arrays], core_ids=[0])
    return tuple(r.results[0][f"out_{name}"] for name in OUTS)
```

```python
from contextlib import ExitStack

import numpy as np
import concourse.bass as bass
from concourse import mybir

F32 = mybir.dt.float32
I32 = mybir.dt.int32
U32 = mybir.dt.uint32
ACT = mybir.ActivationFunctionType
ALU = mybir.AluOpType
AX = mybir.AxisListType

P = 128
D = 1024
KD = D // P
CTX, LAT = 128, 512
T = CTX + LAT
NT = T // P
GH = 4
HH, HK = 4, 64
NE = 16
FF = 512
EPS = 1e-6
RG_C = 8.0
F_MIN = 1e-30
LNSPLIT = 2.0 ** -60
GRID_W, ROWS = 64, LAT // 64
PADW = 2 + CTX + 2 + LAT + 1
CONVW = PADW - 3
SEG = ((0, CTX, 0), (CTX, T, 1))
FWD = (0, 1, 2, 3, 4)
BWD = (0, 4, 3, 2, 1)
LEVELS = (1, 2, 4, 8, 16, 32, 64)
O_QKV, O_G, O_AB, O_HQ, O_HF1, O_RG = 0, 1536, 2048, 2064, 3088, 3344
RING = 3
MAX_OVER = (2 * T - 1) // P
NB = NE + MAX_OVER
XG, GU, HD, DN = range(4)
MSLOTS = 6
SLAB = 8 * 512
MULT, ADD, SUB, MAX, MIN = ALU.mult, ALU.add, ALU.subtract, ALU.max, ALU.min


def slab_plan():
    s = [(("ada", i), 512) for i in range(12)]
    s += [(("rg", 0), 512), (("hq", 0), 512), (("hg", 0), 512), (("hf", 0), 256)]
    s += [(("gdn", i), 512) for i in range(4)]
    s += [(("out", i), 512) for i in range(2)]
    return s


def job_plan():
    j = [("stage", 0)]
    j += [("xt", t) for t in range(NT)]
    j += [("ada", i) for i in range(12)] + [("modT", 0)]
    j += [("rms", 0)]
    j += [("rgx", b) for b in range(2)] + [("rgy", b) for b in range(2)]
    j += [("rgg", n) for n in range(8)]
    j += [("hq", b) for b in range(2)] + [("hi", n) for n in range(2)]
    j += [("hgate", n) for n in range(2)] + [("hf", n) for n in range(4)]
    j += [("lev", l, t) for l in range(8) for t in range(NT)]
    j += [("kdt", t) for t in range(NT)]
    for s in range(NT):
        j += [("ho", s), ("hs", s)]
    j += [("hmix", t) for t in range(NT)]
    j += [("qkv", b) for b in range(12)] + [("gg", t) for t in range(NT)] + [("ab", 0)]
    j += [("ss", b) for b in range(8)] + [("rows", t) for t in range(NT)] + [("gcol", 0)]
    for s in range(NT):
        j += [("gb", s), ("kk", s), ("kq", s)]
        for l in range(7):
            j += [("t1", s, l)] + [("dx", s, l)] * (0 < l < 6) + [("dxt", s, l)]
        j += [("ks", s), ("u", s), ("o", s), ("ds", s)]
    j += [("gmix", t) for t in range(NT)]
    j += [("out", n) for n in range(KD)]
    j += [("rms", 1), ("router", 0)]
    j += [("h2row", t) for t in range(NT)] + [("pos", 0), ("slots", 0)]
    return j


def final_plan():
    return [("yT", t) for t in range(NT)] + [("rms", 2)] + [("fin", t) for t in range(NT)]


def layer_program(nc, I, O, stop=None):
    ctx = ExitStack()
    with ctx:
        def sb(name, *shape, dt=F32):
            return ctx.enter_context(nc.sbuf_tensor(name, [P, *shape], dt))

        def sem(name):
            return ctx.enter_context(nc.semaphore(name))

        ps = ctx.enter_context(nc.psum_tensor("ps", [P, 4, 1024], F32))
        ring = sb("ring", RING, SLAB)
        xT = sb("xT", KD, T)
        hT = sb("hT", KD, T)
        mixBC = sb("mixBC", 4, T)
        ident = sb("ident", P)
        ones = sb("ones", P)
        tri = sb("tri", 2, P)
        lmask = sb("lmask", 2, 7, P)
        vi = sb("vi", 2, P, dt=I32)
        vf = sb("vf", 2, P)
        b_end = sb("b_end", NT, 4)
        stA = sb("stA", P)
        stB = sb("stB", P)
        vecA = sb("vecA", 88)
        vecB = sb("vecB", 80)
        cs = sb("cs", KD, 2)
        modT = sb("modT", 48, 2)
        scl1 = sb("scl1", KD, 2)
        scl2 = sb("scl2", KD, 2)
        wab = sb("wab", KD, 16)
        rw = sb("rw", KD, NE)
        rbias = sb("rbias", NE)
        alog = sb("alog", 8)
        dtb = sb("dtb", 8)
        rb = sb("rb", T)
        small = sb("small", 64)
        stateB = sb("stateB", 2, 2, 2, HK)
        gw = sb("gw", 2, NT)
        slot = sb("slot", 2, NT, dt=I32)
        table = sb("table", 16, dt=I32)
        slot_tok = sb("slot_tok", NB, dt=I32)
        numi = sb("numi", 24, dt=I32)
        num = sb("num", 24)
        ARENA = 23040
        arena = sb("arena", ARENA)

        def carve(at, *shape):
            n = int(np.prod(shape))
            assert at + n <= ARENA, (at, n)
            v = arena[:, at:at + n]
            if len(shape) > 1:
                names = "abcdef"[:len(shape)]
                v = v.rearrange("p (%s) -> p %s" % (" ".join(names), " ".join(names)),
                                **dict(zip(names, shape)))
            return v

        SQ_AT, WG_AT = 11264, 20480
        sq = carve(SQ_AT, KD, T)
        xrow = carve(0, NT, D)
        modrow = carve(NT * D, 6 * D)
        c_x = carve(0, 2, PADW)
        c_u = carve(1300, 2, CONVW)
        c_yg = carve(2600, 2, T)
        c_g = carve(3900, 2, 2, 2, T)
        c_a = carve(9100, 4, T)
        c_t = carve(11700, 4, T)
        c_h = carve(14300, 4, T)
        c_wg = carve(WG_AT, 8, P)
        b_q = carve(0, 2, T)
        b_v = carve(1280, NT, 256)
        b_g = carve(2560, NT, 256)
        b_o = carve(3840, NT, 256)
        b_f = carve(5120, 4, T)
        b_k = carve(7680, 4, T)
        b_b = carve(10240, 4, T)
        b_Z = [carve(12800, 4, T), carve(15360, 4, T)]
        b_at = carve(17920, NT, 8, P)
        z_rows = carve(17408, D)
        a_qk = carve(0, 8, T)
        a_K = carve(5120, NT, 512)
        a_V = carve(7680, NT, 512)
        a_g = carve(10240, NT, 512)
        a_o = carve(12800, NT, 512)
        a_S = carve(15360, 2, 8, P)
        a_X = carve(17408, 8, P)
        a_XT = carve(18432, 8, P)
        a_AT = carve(19456, 8, P)
        a_CT = [carve(20480, 8, P), carve(21504, 8, P)]
        a_pad = carve(17408, 2, PADW)
        a_cv = carve(17408 + 2 * PADW, 2, CONVW)
        a_rn = carve(17408, 8, T)
        a_sm = carve(22530, 420)

        def smallcol(at, *shape):
            n = int(np.prod(shape))
            v = a_sm[:, at:at + n]
            if len(shape) > 1:
                v = v.rearrange("p (a b) -> p a b", a=shape[0])
            return v

        a_la = smallcol(0, NT, 8)
        a_z = smallcol(40, NT, 8)
        a_w = smallcol(80, NT, 8)
        a_beta = smallcol(120, NT, 8)
        a_gc = smallcol(160, NT, 8)
        a_beg = smallcol(200, NT, 8)
        s_beta = smallcol(240, NT, 8)
        s_gc = smallcol(280, NT, 8)
        s_beg = smallcol(320, NT, 8)
        a_nea = smallcol(360, 8)
        a_ge = smallcol(368, NT, 8)
        a_r = smallcol(40, 20)
        hTf = hT[:, :, :].rearrange("p k t -> p (k t)")

        def temp(n):
            return hTf[:, 1024 * n:1024 * (n + 1)].rearrange("p (a b) -> p a b", a=8)

        a_T1, a_dec, a_qe, a_Kd, a_U = (temp(n) for n in range(5))
        mixA = hT[:, 0:4, :]
        m_h2 = carve(0, NT, D)
        m_y = m_h2
        m_yB = carve(NT * D, NT, D)
        m_xg = carve(5120, 2, D)
        m_xgT = carve(7168, 2, KD, P)
        m_slab = carve(10752, 3, SLAB)
        m_sg, m_hid, m_hidT = (hTf[:, 1024 * n:1024 * (n + 1)].rearrange("p (a b) -> p a b", a=2) for n in range(3))
        m_dn = hTf[:, 3072:5120].rearrange("p (a b) -> p a b", a=2)
        m_out = carve(18000, 2, D)
        m_tmp = carve(10240, 8, P)
        m_p = carve(9300, NT, NE)
        m_gate = carve(9400, NT, NE)
        m_rank = carve(9500, NT, NE)
        m_gt = carve(9600, NT, NE)
        m_sel = carve(9700, NT, NE)
        m_t1 = carve(9800, NT, NE)
        m_cmp = carve(9900, MAX_OVER, NE)
        m_c4 = carve(10060, NE, 4)
        m_no = carve(10130, 4, NE)
        m_ab = carve(10200, 2, NT)
        m_idrow = carve(10220, P)
        m_col = carve(10360, 16)
        m_gs = carve(10380, NT, 4)
        m_gr = carve(10400, NT, 4)
        m_gg = carve(10420, NT, 4)
        m_of = carve(10440, 16)

        PLAN = job_plan()
        JOB = {name: (n % 4, n // 4) for n, name in enumerate(PLAN)}
        JOB.update({name: (4 + n % 4, n // 4) for n, name in enumerate(final_plan())})
        pair_full = [sem(f"pair_full{i}") for i in range(8)]
        pair_free = [sem(f"pair_free{i}") for i in range(8)]
        block_full = [sem(f"block_full{i}") for i in range(4)]
        block_free = [sem(f"block_free{i}") for i in range(4)]

        def pair(name):
            return JOB[name][0]

        def bank(name):
            return ps[:, pair(name) % 4, :]

        def full_after(name):
            return pair_full[pair(name)], JOB[name][1] + 1

        def free_before(name):
            return pair_free[pair(name)], JOB[name][1]

        def free_after(name):
            return pair_free[pair(name)], JOB[name][1] + 1

        s_a_conv = sem("a_conv")
        s_a_ct = sem("a_ct")
        s_a_d = sem("a_d")
        s_a_dec = sem("a_dec")
        s_a_eg = sem("a_eg")
        s_a_la = sem("a_la")
        s_a_ln = sem("a_ln")
        s_a_norm = sem("a_norm")
        s_a_oall = sem("a_oall")
        s_a_on = sem("a_on")
        s_a_orn = sem("a_orn")
        s_a_osq = sem("a_osq")
        s_a_oss = sem("a_oss")
        s_a_pad = sem("a_pad")
        s_a_rhs = sem("a_rhs")
        s_a_rn = sem("a_rn")
        s_a_silu = sem("a_silu")
        s_a_sq = sem("a_sq")
        s_a_state = sem("a_state")
        s_a_x0 = sem("a_x0")
        s_a_z = sem("a_z")
        s_b_d = sem("b_d")
        s_b_e = sem("b_e")
        s_b_k = sem("b_k")
        s_b_kd = sem("b_kd")
        s_b_ln = sem("b_ln")
        s_b_m = sem("b_m")
        s_b_oall = sem("b_oall")
        s_b_on = sem("b_on")
        s_b_r = sem("b_r")
        s_b_sq = sem("b_sq")
        s_b_ss = sem("b_ss")
        s_b_state = sem("b_state")
        s_b_z = sem("b_z")
        s_c_a = sem("c_a")
        s_c_done = sem("c_done")
        s_c_fin = sem("c_fin")
        s_c_lam = sem("c_lam")
        s_c_ln = sem("c_ln")
        s_c_mix = sem("c_mix")
        s_c_nc8 = sem("c_nc8")
        s_c_pad = sem("c_pad")
        s_c_sqrt = sem("c_sqrt")
        s_c_y = sem("c_y")
        s_conv_c = sem("conv_c")
        s_cs = sem("cs")
        s_eps = sem("eps")
        s_fin_h = sem("fin_h")
        s_h = sem("h")
        s_hraw = sem("hraw")
        s_ident = sem("ident")
        s_iota = sem("iota")
        s_num = sem("num")
        s_numi = sem("numi")
        s_z_rows = sem("z_rows")
        s_z_stored = sem("z_stored")
        s_sel = sem("sel")
        s_table = sem("table")
        s_h2_stored = sem("h2_stored")
        s_scattered = sem("scattered")
        s_idrow = sem("idrow")
        s_xg = [sem(f"xg{i}") for i in range(2)]
        s_m_sg = sem("m_sg")
        s_hid = sem("hid")
        s_ys_stored = [sem(f"ys_stored{i}") for i in range(2)]
        s_y_in = [sem(f"y_in{t}") for t in range(NT)]
        s_yA = sem("yA")
        s_y = sem("y")
        moe_full = [sem(f"moe_full{i}") for i in range(MSLOTS)]
        s_mod = sem("mod")
        s_r_exp = sem("r_exp")
        s_r_max = sem("r_max")
        s_rb = sem("rb")
        s_sb_in = sem("sb_in")
        s_sg_in = sem("sg_in")
        s_small_in = sem("small_in")
        s_sq = sem("sq")
        s_st_in = sem("st_in")
        s_state_stored = sem("state_stored")
        s_wg_in = sem("wg_in")
        s_wg_zero = sem("wg_zero")
        s_x2 = sem("x2")
        s_x_in = sem("x_in")
        s_y_stored = [sem(f"y_stored{i}") for i in range(2)]

        class Chain:

            def __init__(self, eng, name):
                self.eng, self.sem, self.n = eng, sem(name), 0

            def __call__(self, ins):
                ins.then_inc(self.sem, 1)
                self.n += 1

            def sync(self):
                self.eng.wait_ge(self.sem, self.n)

        SLABS = slab_plan()
        SLAB_N = {name: n for n, (name, _) in enumerate(SLABS)}
        slab_full = [sem(f"slab_full{i}") for i in range(RING)]
        LAST = {}
        for i in range(12):
            LAST[("ada", i)] = ("ada", i)
        LAST[("rg", 0)] = ("rgy", 1)
        LAST[("hq", 0)] = ("hi", 1)
        LAST[("hg", 0)] = ("hf", 1)
        LAST[("hf", 0)] = ("hf", 3)
        for i in range(3):
            LAST[("gdn", i)] = ("qkv", 4 * i + 3)
        LAST[("gdn", 3)] = ("gg", NT - 1)
        for i in range(2):
            LAST[("out", i)] = ("out", 4 * i + 3)

        def slab(name, width=512):
            n = SLAB_N[name] % RING
            return ring[:, n, 0:8 * width].rearrange("p (k n) -> p k n", k=8)

        def slab_after(name):
            n = SLAB_N[name]
            return slab_full[n % RING], 16 * (n // RING + 1)

        win = I["w_in"][0].rearrange("(k p) n -> p k n", p=P)

        def slab_source(name):
            kind, i = name
            if kind == "ada":
                return I["ada_w"][0].rearrange("(k p) n -> p k n", p=P)[:, :, 512 * i:512 * i + 512]
            if kind in ("rg", "hq", "hg", "hf", "gdn"):
                at = {"rg": O_RG, "hq": O_HQ, "hg": O_HQ + 512, "hf": O_HQ + 1024, "gdn": 512 * i}[kind]
                return win[:, :, at:at + (256 if kind == "hf" else 512)]
            if kind == "out":
                return I["w_out"][0].rearrange("(k p) n -> p k n", p=P)[:, :, 512 * i:512 * i + 512]

        def expert_slab(b, i):
            n = (3 * b + i) % MSLOTS
            v = ring[:, (len(SLABS) + n) % RING, :] if n < RING else m_slab[:, n - RING, :]
            return v.rearrange("p (k n) -> p k n", k=4 if i == 2 else 8)

        def expert_source(i, e):
            w = I[("moe_w_gate", "moe_w_up", "moe_w_down")[i]][0]
            return w[bass.DynSlice(e, 1)].rearrange("a (k p) n -> p (a k) n", p=P)

        def slab_full_of(b, i):
            m = 3 * b + i
            return moe_full[m % MSLOTS], 16 * (m // MSLOTS + 1)

        def over_blocks(eng, body):
            n = eng.value_load(table[0:1, MAX_OVER:MAX_OVER + 1], min_val=0, max_val=MAX_OVER)
            with ExitStack() as nest:
                for j in range(MAX_OVER):
                    nest.enter_context(eng.If(n > j))
                    body(NE + j)

        h2_dram = nc.dram_tensor("h2_rows", (T, D), F32, kind="Internal").ap()
        tok_dram = nc.dram_tensor("slot_tokens", (NB * P, 1), F32, kind="Internal").ap()
        ys_dram = nc.dram_tensor("slot_outputs", (NB * P, D), F32, kind="Internal").ap()

        def segs(name):
            b = bank(name)
            return ((0, CTX, b[:, 0:CTX], 0), (CTX, T, b[:, 512:1024], 1))

        def wide(v, at, n):
            v = v.unsqueeze(at)
            shape = list(v.shape)
            shape[at] = n
            return v.to_broadcast(shape)

        vb = vecB
        block = ctx.enter_context(nc.Block())

        @block.sync
        def _(sp):
            sp.dma_start(xrow[:, 0, :], I["x_prompt"][0]).then_inc(s_x_in, 16)
            sp.dma_start(xrow[:, 1:NT, :], I["x_sample"][0].rearrange("(t p) d -> p t d", p=P)).then_inc(s_x_in, 16)
            for n, (name, width) in enumerate(SLABS):
                if n >= RING:
                    sp.wait_ge(*full_after(LAST[SLABS[n - RING][0]]))
                sp.dma_start(slab(name, width), slab_source(name)).then_inc(slab_full[n % RING], 16)
            for b in range(NE):
                for i in range(3):
                    if b == 0:
                        sp.wait_ge(*full_after(LAST[SLABS[len(SLABS) - RING + i][0]]))
                    elif b == 1 and i == 0:
                        sp.wait_ge(*full_after(("rms", 1)))
                    elif b >= 2:
                        sp.wait_ge(block_full[DN if i == 2 else GU], b - 1)
                    m = (3 * b + i) % MSLOTS
                    sp.dma_start(expert_slab(b, i), expert_source(i, b)).then_inc(moe_full[m], 16)
            sp.wait_ge(s_table, 1)

            def load_over(b):
                e = sp.value_load(table[0:1, b - NE:b - NE + 1], min_val=0, max_val=NE - 1)
                for i in range(3):
                    sp.wait_ge(block_full[DN if i == 2 else GU], b - 1)
                    m = (3 * b + i) % MSLOTS
                    sp.dma_start(expert_slab(b, i), expert_source(i, e)).then_inc(moe_full[m], 16)

            over_blocks(sp, load_over)
            for t in range(NT):
                sp.wait_ge(*free_after(("fin", t)))
                dst = O["y_prompt"][0] if t == 0 else O["y_sample"][0, (t - 1) * P:t * P, :]
                sp.dma_start(dst, m_out[:, t % 2, :]).then_inc(s_y_stored[t % 2], 16)
            sp.wait_ge(s_y_stored[0], 48)
            sp.wait_ge(s_y_stored[1], 32)
            sp.wait_ge(s_state_stored, 16 * 3)

        @block.tensor
        def _(pe):
            mm = nc.tensor.matmul

            def tr(out, in_, n=P):
                return nc.tensor.transpose(out, in_, ident[0:n, 0:n])

            def project(name, w, cols, rhs=None):
                rhs = rhs or (lambda k: hT[:, k, :])
                pe.wait_ge(*free_before(name))
                for a, b, out, g in segs(name):
                    for k in range(KD):
                        last = mm(out, w[:, k, cols], rhs(k)[:, a:b], start=(k == 0), stop=(k == KD - 1))
                last.then_inc(pair_full[pair(name)], 1)

            pe.wait_ge(s_ident, 1)
            pe.wait_ge(s_st_in, 16 * 16)
            b = bank(("stage", 0))
            tr(b[:, 0:88], stA[0:88, :], 88)
            tr(b[:, 512:592], stB[0:80, :], 80).then_inc(pair_full[pair(("stage", 0))], 1)
            pe.wait_ge(s_x_in, 32)
            for t in range(NT):
                name = ("xt", t)
                pe.wait_ge(*free_before(name))
                for k in range(KD):
                    last = tr(bank(name)[:, P * k:P * k + P], xrow[:, t, P * k:P * k + P])
                last.then_inc(pair_full[pair(name)], 1)
            pe.wait_ge(s_cs, 2)
            for i in range(12):
                name = ("ada", i)
                pe.wait_ge(*slab_after(name))
                pe.wait_ge(*free_before(name))
                for k in range(KD):
                    last = mm(bank(name)[0:2, 0:512], cs[:, k, :], slab(name)[:, k, :],
                              start=(k == 0), stop=(k == KD - 1))
                last.then_inc(pair_full[pair(name)], 1)
            pe.wait_ge(*free_after(("ada", 11)))
            pe.wait_ge(*free_after(("ada", 10)))
            pe.wait_ge(*free_after(("ada", 9)))
            name = ("modT", 0)
            pe.wait_ge(*free_before(name))
            for c in range(48):
                last = tr(bank(name)[:, 2 * c:2 * c + 2], modrow[0:2, P * c:P * c + P], 2)
            last.then_inc(pair_full[pair(name)], 1)

            def rms_sums(n):
                name = ("rms", n)
                pe.wait_ge(*free_before(name))
                for k in range(KD):
                    pe.wait_ge(s_sq, KD * n + k + 1)
                    for a, b, out, g in segs(name):
                        last = mm(out, ones[:, :], sq[:, k, a:b], start=(k == 0), stop=(k == KD - 1))
                last.then_inc(pair_full[pair(name)], 1)

            rms_sums(0)
            pe.wait_ge(s_h, 16)
            w = slab(("rg", 0))
            pe.wait_ge(*slab_after(("rg", 0)))
            for b in range(2):
                project(("rgx", b), w, slice(P * b, P * b + P))
            for b in range(2):
                project(("rgy", b), w, slice(256 + P * b, 256 + P * b + P))
            pe.wait_ge(s_conv_c, 2)
            pe.wait_ge(s_wg_in, 16 * 16)
            for n in range(8):
                name = ("rgg", n)
                pe.wait_ge(*free_before(name))
                for a, b, out, g in segs(name):
                    last = mm(out, c_wg[:, n, :], c_u[:, n % 2, a + 2 * g:b + 2 * g], start=True, stop=True)
                last.then_inc(pair_full[pair(name)], 1)
            w = slab(("hq", 0))
            pe.wait_ge(*slab_after(("hq", 0)))
            for b in range(2):
                project(("hq", b), w, slice(P * b, P * b + P))

            def token_rows(kind, w, col, width, per, tiles=NT):
                for n in range((tiles + per - 1) // per):
                    name = (kind, n)
                    pe.wait_ge(*free_before(name))
                    for t in range(n * per, min(tiles, n * per + per)):
                        out = bank(name)[:, (t - n * per) * width:(t - n * per + 1) * width]
                        for k in range(KD):
                            last = mm(out, hT[:, k, P * t:P * t + P], w[:, k, col:col + width],
                                      start=(k == 0), stop=(k == KD - 1))
                    last.then_inc(pair_full[pair(name)], 1)

            token_rows("hi", w, 256, 256, 4)
            w = slab(("hg", 0))
            pe.wait_ge(*slab_after(("hg", 0)))
            token_rows("hgate", w, 0, 256, 4)
            for n in range(2):
                project(("hf", n), w, slice(256 + P * n, 256 + P * n + P))
            w = slab(("hf", 0), 256)
            pe.wait_ge(*slab_after(("hf", 0)))
            for n in range(2):
                project(("hf", 2 + n), w, slice(P * n, P * n + P))

            HALVES = [(half, dp) for half in range(2) for dp in range(4)]

            def half(v, h, dp, t):
                return v[64 * h:64 * h + 64, dp, P * t:P * t + P]

            pe.wait_ge(s_b_k, 1)
            for l in range(8):
                if l:
                    pe.wait_ge(s_b_z, l)
                for t in range(NT):
                    name = ("lev", l, t)
                    pe.wait_ge(*free_before(name))
                    for h, dp in HALVES:
                        lhs = half(b_Z[l % 2] if l else b_k, h, dp, t)
                        rhs = half(b_Z[l % 2], h, dp, t) if l else half(b_q, h, dp % 2, t)
                        last = mm(bank(name)[:, 512 * h + P * dp:512 * h + P * dp + P], lhs, rhs, start=True, stop=True)
                    last.then_inc(pair_full[pair(name)], 1)
            pe.wait_ge(s_b_kd, 1)
            for t in range(NT):
                name = ("kdt", t)
                pe.wait_ge(*free_before(name))
                for dp in range(4):
                    last = tr(bank(name)[:, P * dp:P * dp + P], b_Z[1][:, dp, P * t:P * t + P])
                last.then_inc(pair_full[pair(name)], 1)
            b_kdr = b_k.rearrange("p a t -> p (a t)").rearrange("p (t c n) -> p t c n", t=NT, c=4)
            for s in range(NT):
                seg = min(s, 1)
                name = ("ho", s)
                if s == 0:
                    pe.wait_ge(*free_after(("kdt", NT - 1)))
                    pe.wait_ge(*free_after(("lev", 7, NT - 1)))
                if s == 0:
                    pe.wait_ge(s_b_state, 1)
                else:
                    pe.wait_ge(*free_after(("hs", s - 1)))
                pe.wait_ge(*free_before(name))
                for h, dp in HALVES:
                    t = (FWD, BWD)[dp // 2][s]
                    out = bank(name)[:, 512 * h + 64 * dp:512 * h + 64 * dp + 64]
                    v = P * (dp % 2) + 64 * h
                    mm(out, half(b_Z[0], h, dp, t), stateB[64 * h:64 * h + 64, seg, dp // 2, dp % 2, :],
                       start=True, stop=False)
                    last = mm(out, b_at[:, t, 4 * h + dp, :], b_v[:, t, v:v + 64], start=False, stop=True)
                last.then_inc(pair_full[pair(name)], 1)
                name = ("hs", s)
                pe.wait_ge(*free_before(name))
                for dp in range(4):
                    t = (FWD, BWD)[dp // 2][s]
                    last = mm(bank(name)[:, P * dp:P * dp + P], b_kdr[:, t, dp, :],
                              b_v[:, t, P * (dp % 2):P * (dp % 2) + P], start=True, stop=True)
                last.then_inc(pair_full[pair(name)], 1)
            pe.wait_ge(s_b_on, 1)
            for t in range(NT):
                name = ("hmix", t)
                pe.wait_ge(*free_before(name))
                for p in range(2):
                    last = tr(bank(name)[:, P * p:P * p + P], b_o[:, t, P * p:P * p + P])
                last.then_inc(pair_full[pair(name)], 1)
            for b in range(12):
                if b % 4 == 0:
                    pe.wait_ge(*slab_after(("gdn", b // 4)))
                project(("qkv", b), slab(("gdn", b // 4)), slice(P * (b % 4), P * (b % 4) + P))
            pe.wait_ge(*slab_after(("gdn", 3)))
            token_rows("gg", slab(("gdn", 3)), 0, 512, 1)
            pe.wait_ge(s_small_in, 16 * 5)
            token_rows("ab", wab, 0, 16, NT)
            for b in range(8):
                name = ("ss", b)
                pe.wait_ge(s_a_sq, b + 1)
                pe.wait_ge(*free_before(name))
                for a, e, out, g in segs(name):
                    last = mm(out, ones[:, :], a_K.rearrange("p a b -> p (a b)")
                              .rearrange("p (n t) -> p n t", t=T)[:, b % 4, a:e], start=True, stop=True)
                last.then_inc(pair_full[pair(name)], 1)
            pe.wait_ge(s_a_norm, 1)
            for t in range(NT):
                name = ("rows", t)
                pe.wait_ge(*free_before(name))
                vT = a_o.rearrange("p a b -> p (a b)").rearrange("p (n t) -> p n t", t=T)
                for h in range(GH):
                    tr(bank(name)[:, P * h:P * h + P], a_qk[:, 4 + h, P * t:P * t + P])
                for h in range(GH):
                    last = tr(bank(name)[:, 512 + P * h:512 + P * h + P], vT[:, h, P * t:P * t + P])
                last.then_inc(pair_full[pair(name)], 1)
            name = ("gcol", 0)
            pe.wait_ge(s_a_la, 1)
            pe.wait_ge(*free_before(name))
            for t in range(NT):
                for d in range(2):
                    c = 8 * t + 4 * d
                    last = mm(bank(name)[:, c:c + 4], tri[:, d, :], a_la[:, t, 4 * d:4 * d + 4],
                              start=True, stop=True)
            last.then_inc(pair_full[pair(name)], 1)

            def eight(name, lhs, rhs):
                pe.wait_ge(*free_before(name))
                for dh in range(8):
                    last = mm(bank(name)[:, P * dh:P * dh + P], lhs(dh), rhs(dh), start=True, stop=True)
                last.then_inc(pair_full[pair(name)], 1)

            def cut(v, base):
                return lambda s: lambda dh: v[:, base + dh % 4, P * (FWD, BWD)[dh // 4][s]:P * (FWD, BWD)[dh // 4][s] + P]

            kT, qT = cut(a_qk, 4), cut(a_qk, 0)
            for s in range(NT):
                seg = min(s, 1)
                tile = lambda dh: (FWD, BWD)[dh // 4][s]
                eight(("gb", s), lambda dh: a_la[:, tile(dh), dh:dh + 1].to_broadcast([P, P]),
                      lambda dh: tri[:, dh // 4, :])
                eight(("kk", s), kT(s), kT(s))
                eight(("kq", s), kT(s), qT(s))
                for l in range(7):
                    pe.wait_ge(s_a_ct, 7 * s + l + 1)
                    if l:
                        pe.wait_ge(*free_after(("dxt", s, l - 1)))
                        if l > 1:
                            pe.wait_ge(*free_after(("dx", s, l - 1)))
                        else:
                            pe.wait_ge(s_a_x0, s + 1)
                    ct = a_CT[l % 2]
                    eight(("t1", s, l), lambda dh: ct[:, dh, :],
                          (lambda dh: a_X[:, dh, :]) if l else (lambda dh: ident[:, :]))
                    pe.wait_ge(*free_after(("t1", s, l)))
                    if 0 < l < 6:
                        eight(("dx", s, l), lambda dh: a_XT[:, dh, :], lambda dh: a_T1[:, dh, :])
                    eight(("dxt", s, l), lambda dh: a_T1[:, dh, :],
                          (lambda dh: a_XT[:, dh, :]) if l else (lambda dh: ident[:, :]))
                if s == 0:
                    pe.wait_ge(s_a_state, 1)
                else:
                    pe.wait_ge(*free_after(("ds", s - 1)))
                    pe.wait_ge(s_sg_in, 16)
                eight(("ks", s), kT(s), lambda dh: a_S[:, seg, dh, :])
                pe.wait_ge(s_a_rhs, s + 1)
                pe.wait_ge(*free_after(("dxt", s, 6)))
                eight(("u", s), lambda dh: a_XT[:, dh, :], lambda dh: a_CT[0][:, dh, :])
                pe.wait_ge(*free_after(("u", s)))
                pe.wait_ge(*free_after(("kq", s)))
                name = ("o", s)
                pe.wait_ge(*free_before(name))
                for dh in range(8):
                    out = bank(name)[:, P * dh:P * dh + P]
                    mm(out, a_qe[:, dh, :], a_S[:, seg, dh, :], start=True, stop=False)
                    last = mm(out, a_dec[:, dh, :], a_U[:, dh, :], start=False, stop=True)
                last.then_inc(pair_full[pair(name)], 1)
                eight(("ds", s), lambda dh: a_Kd[:, dh, :], lambda dh: a_U[:, dh, :])
            pe.wait_ge(s_a_on, 1)
            for t in range(NT):
                name = ("gmix", t)
                pe.wait_ge(*free_before(name))
                for h in range(GH):
                    last = tr(bank(name)[:, P * h:P * h + P], a_o[:, t, P * h:P * h + P])
                last.then_inc(pair_full[pair(name)], 1)
            for t in range(NT):
                pe.wait_ge(*free_after(("gmix", t)))
                pe.wait_ge(*free_after(("hmix", t)))
            pe.wait_ge(s_c_mix, 4)
            for n in range(KD):
                if n % 4 == 0:
                    pe.wait_ge(*slab_after(("out", n // 4)))
                project(("out", n), slab(("out", n // 4)), slice(P * (n % 4), P * (n % 4) + P),
                        rhs=lambda k: mixA[:, k, :] if k < 4 else mixBC[:, k - 4, :])
            rms_sums(1)
            pe.wait_ge(s_h, 32)
            token_rows("router", rw, 0, NE, NT)
            for t in range(NT):
                name = ("h2row", t)
                pe.wait_ge(*free_before(name))
                for k in range(KD):
                    last = tr(bank(name)[:, P * k:P * k + P], hT[:, k, P * t:P * t + P])
                last.then_inc(pair_full[pair(name)], 1)
            name = ("pos", 0)
            pe.wait_ge(s_sel, 1)
            pe.wait_ge(*free_before(name))
            for t in range(NT):
                out = bank(name)[:, NE * t:NE * t + NE]
                for u in range(t):
                    mm(out, ones[:, :], m_sel[:, u, :], start=(u == 0), stop=False)
                mm(out, tri[:, 0, :], m_sel[:, t, :], start=(t == 0), stop=True)
            for t in range(NT):
                last = mm(bank(name)[:, NE * NT:NE * NT + NE], ones[:, :], m_sel[:, t, :], start=(t == 0), stop=(t == NT - 1))
            last.then_inc(pair_full[pair(name)], 1)
            name = ("slots", 0)
            pe.wait_ge(s_idrow, 16)
            pe.wait_ge(*free_before(name))
            tr(bank(name)[:, 0:NB], m_idrow[0:NB, :], NB).then_inc(pair_full[pair(name)], 1)

            def gathered(b):
                pe.wait_ge(s_xg[b % 2], 16 * (b // 2 + 1))
                if b:
                    pe.wait_ge(block_free[XG], b)
                for k in range(KD):
                    last = tr(ps[:, XG, P * k:P * k + P], m_xg[:, b % 2, P * k:P * k + P])
                last.then_inc(block_full[XG], 1)

            def gate_up(b):
                pe.wait_ge(block_free[XG], b + 1)
                if b:
                    pe.wait_ge(block_free[GU], b)
                for i in range(2):
                    pe.wait_ge(*slab_full_of(b, i))
                    for k in range(KD):
                        last = mm(ps[:, GU, 512 * i:512 * i + 512], m_xgT[:, b % 2, k, :], expert_slab(b, i)[:, k, :],
                                  start=(k == 0), stop=(k == KD - 1))
                last.then_inc(block_full[GU], 1)

            def down(b):
                pe.wait_ge(block_free[GU], b + 1)
                if b:
                    pe.wait_ge(block_free[HD], b)
                for f in range(4):
                    last = tr(ps[:, HD, P * f:P * f + P], m_hid[:, b % 2, P * f:P * f + P])
                last.then_inc(block_full[HD], 1)
                pe.wait_ge(block_free[HD], b + 1)
                if b:
                    pe.wait_ge(block_free[DN], b)
                pe.wait_ge(*slab_full_of(b, 2))
                for n in range(2):
                    for f in range(4):
                        last = mm(ps[:, DN, 512 * n:512 * n + 512], m_hidT[:, b % 2, P * f:P * f + P],
                                  expert_slab(b, 2)[:, f, 512 * n:512 * n + 512], start=(f == 0), stop=(f == 3))
                last.then_inc(block_full[DN], 1)

            for name in PLAN[-4:]:
                pe.wait_ge(*free_after(name))
            gathered(0)
            for b in range(NE):
                gate_up(b)
                if b + 1 < NE:
                    gathered(b + 1)
                if b:
                    down(b - 1)
            down(NE - 1)

            def over(b):
                gathered(b)
                gate_up(b)
                down(b)

            pe.wait_ge(s_table, 1)
            over_blocks(pe, over)
            for t in range(NT):
                name = ("yT", t)
                pe.wait_ge(s_y, t + 1)
                pe.wait_ge(*free_before(name))
                for k in range(KD):
                    last = tr(bank(name)[:, P * k:P * k + P], m_y[:, t, P * k:P * k + P])
                last.then_inc(pair_full[pair(name)], 1)
            rms_sums(2)
            pe.wait_ge(s_fin_h, KD)
            for t in range(NT):
                name = ("fin", t)
                pe.wait_ge(*free_before(name))
                for k in range(KD):
                    last = tr(bank(name)[:, P * k:P * k + P], hT[:, k, P * t:P * t + P])
                last.then_inc(pair_full[pair(name)], 1)

        @block.scalar
        def _(act):
            A = nc.scalar.activation
            ch = Chain(act, "act_chain")
            dma = act.dma_start

            def rowsof(v, n):
                return v.rearrange("(n p) -> n p", p=P)

            st = s_st_in
            dma(stA[0:48, :], rowsof(I["ada_b"][0], 48)).then_inc(st, 16)
            dma(stA[48:56, :], rowsof(I["norm1_w"][0], 8)).then_inc(st, 16)
            dma(stA[56:64, :], rowsof(I["norm2_w"][0], 8)).then_inc(st, 16)
            dma(stA[64:72, :], rowsof(I["final_norm_w"], 8)).then_inc(st, 16)
            dma(stA[72:80, :], rowsof(I["c"][0], 8)).then_inc(st, 16)
            dma(stA[80:88, :], rowsof(I["c_ctx"], 8)).then_inc(st, 16)
            dma(stB[0:48, :], I["gdn_conv_w"][0].rearrange("j (n p) -> (j n) p", p=P)).then_inc(st, 16)
            dma(stB[48:56, :], I["rg_conv_w"][0].rearrange("j (n p) -> (j n) p", p=P)).then_inc(st, 16)
            dma(stB[56:58, :], rowsof(I["rg_conv_b"][0], 2)).then_inc(st, 16)
            dma(stB[58:66, :], I["rg_gate_b"][0].rearrange("d g (n p) -> (d g n) p", p=P)).then_inc(st, 16)
            dma(stB[66:70, :], I["rg_lambda"][0].rearrange("d (n p) -> (d n) p", p=P)).then_inc(st, 16)
            dma(stB[70:74, :], I["state_rglru"][0, 0].rearrange("d (n p) -> (d n) p", p=P)).then_inc(st, 16)
            dma(stB[74:78, :], I["hg_lb_logits"][0].rearrange("d (n p) -> (d n) p", p=P)).then_inc(st, 16)
            dma(stB[78:79, :], I["gdn_norm_w"]).then_inc(st, 16)
            for i in range(2):
                dma(stB[79:80, 64 * i:64 * i + 64], I["hg_norm_w"]).then_inc(st, 16)
            sm = s_small_in
            dma(wab[:, :, :], win[:, :, O_AB:O_AB + 16]).then_inc(sm, 16)
            dma(rw[:, :, :], I["router_w"].rearrange("(k p) e -> p k e", p=P)).then_inc(sm, 16)
            dma(rbias[:, :], I["router_b"].partition_broadcast(P)).then_inc(sm, 16)
            dma(alog[:, :], I["gdn_a_log"][0].rearrange("d h -> (d h)").partition_broadcast(P)).then_inc(sm, 16)
            dma(dtb[:, :], I["gdn_dt_bias"][0].rearrange("d h -> (d h)").partition_broadcast(P)).then_inc(sm, 16)
            dma(stateB[:, 1, :, :, :].rearrange("p d q v -> p (d q) v"),
                I["state_hgrn"][0, 0].rearrange("d (q e) k v -> (e k) (d q) v", e=2)).then_inc(s_sb_in, 16)
            act.wait_ge(s_wg_zero, 1)
            for n in range(8):
                for i in range(2):
                    dma(c_wg[64 * i:64 * i + 64, n, 64 * i:64 * i + 64],
                        I["rg_gate_w"][0, n // 4, n // 2 % 2, 2 * (n % 2) + i]).then_inc(s_wg_in, 16)

            act.wait_ge(*free_after(("stage", 0)))
            A(cs[:, :, 1], vecA[:, 72:80], ACT.Silu).then_inc(s_cs, 1)
            A(cs[:, :, 0], vecA[:, 80:88], ACT.Silu).then_inc(s_cs, 1)

            for i in range(12):
                act.wait_ge(*full_after(("ada", i)))
                A(modrow[0:2, 512 * i:512 * i + 512], bank(("ada", i))[0:2, 0:512], ACT.Copy).then_inc(pair_free[pair(("ada", i))], 1)

            def rms(n, scl, shift, sqfrom):
                sqfrom()
                for k in range(KD):
                    A(sq[:, k, :], xT[:, k, :], ACT.Square).then_inc(s_sq, 1)
                name = ("rms", n)
                act.wait_ge(*full_after(name))
                for a, b, out, g in segs(name):
                    ins = A(rb[:, a:b], out, ACT.Ln, scale=1.0 / D, bias=small[:, 0:1])
                    ch(ins) if g == 0 else ins.then_inc(pair_free[pair(name)], 1)
                act.wait_ge(*free_after(name))
                ch.sync()
                A(rb[:, :], rb[:, :], ACT.Exp, scale=-0.5).then_inc(s_rb, 1)
                if scl is not None:
                    for k in range(KD):
                        act.wait_ge(s_hraw, KD * n + k + 1)
                        for a, b, _, g in segs(name):
                            A(hT[:, k, a:b], hT[:, k, a:b], ACT.Identity, scale=scl[:, k, g:g + 1],
                                   bias=modT[:, shift + k, g:g + 1]).then_inc(s_h, 1)

            act.wait_ge(s_eps, 1)
            act.wait_ge(s_mod, 1)

            def silu_out(b):
                act.wait_ge(s_a_conv, b + 1)
                vT = a_o.rearrange("p a b -> p (a b)").rearrange("p (n t) -> p n t", t=T)
                dst = a_qk[:, b, :] if b < 8 else vT[:, b - 8, :]
                for a, e, g in SEG:
                    A(dst[:, a:e], a_cv[:, b % 2, a + 2 * g:e + 2 * g], ACT.Silu).then_inc(s_a_silu, 1)

            def l2_ln(b):
                name = ("ss", b)
                act.wait_ge(*full_after(name))
                for a, e, out, g in segs(name):
                    ins = A(a_rn[:, b, a:e], out, ACT.Ln, bias=small[:, 0:1])
                    ch(ins) if g == 0 else ins.then_inc(pair_free[pair(name)], 1)

            def x_ready():
                for t in range(NT):
                    act.wait_ge(*free_after(("xt", t)))

            rms(0, scl1, 0, x_ready)
            act.wait_ge(s_c_pad, 1)
            act.wait_ge(s_h, 16)
            for b in range(2):
                name = ("rgx", b)
                act.wait_ge(*full_after(name))
                lo, hi = bank(name)[:, 0:CTX], bank(name)[:, 512:1024]
                ch(A(c_x[:, b, 2:2 + CTX], lo, ACT.Copy))
                A(c_x[:, b, 4 + CTX:4 + T].rearrange("p (c r) -> p r c", r=ROWS),
                       hi.rearrange("p (r c) -> p r c", c=GRID_W), ACT.Copy).then_inc(pair_free[pair(name)], 1)
            for b in range(2):
                name = ("rgy", b)
                act.wait_ge(*full_after(name))
                lo, hi = bank(name)[:, 0:CTX], bank(name)[:, 512:1024]
                ch(A(c_yg[:, b, 0:CTX], lo, ACT.Gelu_apprx_tanh))
                A(c_yg[:, b, CTX:T].rearrange("p (c r) -> p r c", r=ROWS),
                       hi.rearrange("p (r c) -> p r c", c=GRID_W), ACT.Gelu_apprx_tanh).then_inc(pair_free[pair(name)], 1)
            act.wait_ge(s_c_lam, 1)
            ch(A(small[:, 8:12], small[:, 4:8], ACT.Exp))
            ch.sync()
            ch(A(small[:, 44:48], small[:, 44:48], ACT.Exp))
            A(small[:, 8:12], small[:, 8:12], ACT.Ln, bias=small[:, 1:2]).then_inc(s_c_ln, 1)
            for n in range(8):
                name = ("rgg", n)
                act.wait_ge(*full_after(name))
                for a, b, out, g in segs(name):
                    ins = A(c_g[:, n // 4, n // 2 % 2, n % 2, a:b], out, ACT.Sigmoid, bias=vb[:, 58 + n:59 + n])
                    ch(ins) if g == 0 else ins.then_inc(pair_free[pair(name)], 1)
            for n in (0, 1, 4, 5):
                act.wait_ge(*free_after(("rgg", n)))
            ch.sync()
            act.wait_ge(s_c_nc8, 1)
            for db in range(4):
                A(c_a[:, db, :], c_g[:, db // 2, 0, db % 2, :], ACT.Exp, scale=small[:, 12 + db:13 + db]).then_inc(s_c_a, 1)
            for db in range(4):
                A(c_t[:, db, :], c_g[:, db // 2, 0, db % 2, :], ACT.Tanh, scale=small[:, 12 + db:13 + db]).then_inc(s_c_a, 1)
            act.wait_ge(s_c_y, 1)
            A(c_t[:, :, :], c_h[:, :, :], ACT.Sqrt).then_inc(s_c_sqrt, 1)
            act.wait_ge(s_c_fin, 1)
            dma(O["new_rg"][0, 0].rearrange("d (n p) -> p (d n)", p=P), small[:, 20:24],
                allow_slow_non_contiguous=True).then_inc(s_state_stored, 16)
            act.wait_ge(s_c_done, 1)
            for b in range(2):
                name = ("hq", b)
                act.wait_ge(*full_after(name))
                for a, e, out, g in segs(name):
                    ins = A(b_q[:, b, a:e], out, ACT.Copy)
                    ch(ins) if g == 0 else ins.then_inc(pair_free[pair(name)], 1)
            for n in range(2):
                name = ("hi", n)
                act.wait_ge(*full_after(name))
                A(b_v[:, 4 * n:min(NT, 4 * n + 4), :], bank(name)[:, 0:256 * (4 if n == 0 else 1)]
                       .rearrange("p (t c) -> p t c", c=256), ACT.Copy).then_inc(pair_free[pair(name)], 1)
            for n in range(2):
                name = ("hgate", n)
                act.wait_ge(*full_after(name))
                A(b_g[:, 4 * n:min(NT, 4 * n + 4), :], bank(name)[:, 0:256 * (4 if n == 0 else 1)]
                       .rearrange("p (t c) -> p t c", c=256), ACT.Silu).then_inc(pair_free[pair(name)], 1)
            for n in range(4):
                name = ("hf", n)
                act.wait_ge(*full_after(name))
                for a, e, out, g in segs(name):
                    ch(A(b_f[:, n, a:e], out, ACT.Sigmoid))
                    ins = A(b_k[:, n, a:e], out, ACT.Sigmoid, scale=-1.0)
                    ch(ins) if g == 0 else ins.then_inc(pair_free[pair(name)], 1)
            act.wait_ge(s_b_m, 1)
            ch(A(b_f[:, :, :], b_f[:, :, :], ACT.Ln))
            A(b_Z[0][:, :, :], b_Z[0][:, :, :], ACT.Ln, scale=1.0 / LNSPLIT).then_inc(s_b_ln, 1)
            for l in range(7):
                act.wait_ge(s_b_d, l + 1)
                A(b_f[:, :, :], b_f[:, :, :], ACT.Exp).then_inc(s_b_e, 1)
            act.wait_ge(s_b_z, 7)
            A(b_f[:, :, :], b_b[:, :, :], ACT.Exp).then_inc(s_b_e, 1)
            act.wait_ge(s_b_d, 8)
            A(b_Z[1][:, :, :], b_Z[1][:, :, :], ACT.Exp).then_inc(s_b_e, 1)
            act.wait_ge(s_b_kd, 1)
            b_kdr = b_k.rearrange("p a t -> p (a t)").rearrange("p (t c) -> p t c", t=NT)
            for t in range(NT):
                act.wait_ge(*full_after(("kdt", t)))
                A(b_kdr[:, t, :], bank(("kdt", t))[:, 0:512], ACT.Copy).then_inc(pair_free[pair(("kdt", t))], 1)
            act.wait_ge(*free_after(("hs", 0)))
            dma(O["new_hgrn"][0, 0].rearrange("d (q e) k v -> (e k) (d q) v", e=2),
                stateB[:, 0, :, :, :].rearrange("p d q v -> p (d q) v")).then_inc(s_state_stored, 16)
            act.wait_ge(s_b_oall, 1)
            A(b_f[:, 0:2, :].rearrange("p a t -> p (a t)"), b_o[:, :, :].rearrange("p a t -> p (a t)"),
                   ACT.Square).then_inc(s_b_sq, 1)
            act.wait_ge(s_b_ss, 1)
            ch(A(small[:, 24:44], small[:, 24:44], ACT.Ln, scale=1.0 / HK, bias=small[:, 0:1]))
            ch.sync()
            A(small[:, 24:44], small[:, 24:44], ACT.Exp, scale=-0.5).then_inc(s_b_r, 1)
            for t in range(NT):
                act.wait_ge(*full_after(("hmix", t)))
                A(mixBC[:, 0:2, P * t:P * t + P], bank(("hmix", t))[:, 0:256].rearrange("p (a t) -> p a t", a=2),
                       ACT.Copy, scale=vb[:, 79:80]).then_inc(pair_free[pair(("hmix", t))], 1)
            act.wait_ge(s_a_pad, 1)
            for b in range(12):
                name = ("qkv", b)
                act.wait_ge(*full_after(name))
                if b >= 2:
                    act.wait_ge(s_a_conv, b - 1)
                for a, e, out, g in segs(name):
                    ins = A(a_pad[:, b % 2, 2 + a + 2 * g:2 + e + 2 * g], out, ACT.Copy)
                    ch(ins) if g == 0 else ins.then_inc(pair_free[pair(name)], 1)
                if b >= 1:
                    silu_out(b - 1)
            silu_out(11)
            for t in range(NT):
                act.wait_ge(*full_after(("gg", t)))
                A(a_g[:, t, :], bank(("gg", t))[:, 0:512], ACT.Silu).then_inc(pair_free[pair(("gg", t))], 1)
            sqs = a_K.rearrange("p a b -> p (a b)").rearrange("p (n t) -> p n t", t=T)
            act.wait_ge(s_a_silu, 24)
            for b in range(8):
                if b >= 4:
                    act.wait_ge(*full_after(("ss", b - 4)))
                A(sqs[:, b % 4, :], a_qk[:, b, :], ACT.Square).then_inc(s_a_sq, 1)
                if b >= 3:
                    l2_ln(b - 3)
            for b in range(5, 8):
                l2_ln(b)
            act.wait_ge(*free_after(("ss", 7)))
            act.wait_ge(*free_after(("ss", 6)))
            act.wait_ge(*free_after(("ss", 5)))
            act.wait_ge(*free_after(("ss", 4)))
            ch.sync()
            A(a_rn[:, :, :], a_rn[:, :, :], ACT.Exp, scale=-0.5).then_inc(s_a_rn, 1)
            act.wait_ge(s_a_z, 1)
            ch(A(a_w[:, :, :], a_w[:, :, :], ACT.Exp))
            ch(A(a_nea[:, :], alog[:, :], ACT.Exp))
            ch.sync()
            ch(A(a_beta[:, :, :], a_beta[:, :, :], ACT.Sigmoid))
            A(a_w[:, :, :], a_w[:, :, :], ACT.Ln, bias=small[:, 1:2]).then_inc(s_a_ln, 1)
            for t in range(NT):
                act.wait_ge(*full_after(("rows", t)))
                ch(A(a_K[:, t, :], bank(("rows", t))[:, 0:512], ACT.Copy))
                A(a_V[:, t, :], bank(("rows", t))[:, 512:1024], ACT.Copy).then_inc(pair_free[pair(("rows", t))], 1)
            act.wait_ge(*free_after(("gcol", 0)))
            A(a_beg[:, :, :], a_gc[:, :, :], ACT.Exp).then_inc(s_a_eg, 1)
            for s in range(NT):
                name = ("gb", s)
                act.wait_ge(*full_after(name))
                if s:
                    act.wait_ge(*full_after(("o", s - 1)))
                act.wait_ge(s_a_d, s + 1)
                A(a_dec[:, :, :], a_dec[:, :, :], ACT.Exp).then_inc(s_a_dec, 1)
                A(a_qe[:, :, :], bank(name).rearrange("p (a b) -> p a b", a=8), ACT.Exp).then_inc(pair_free[pair(name)], 1)
                act.wait_ge(*full_after(("u", s)))
                if s:
                    act.wait_ge(*full_after(("ds", s - 1)))
                A(a_U[:, :, :], bank(("u", s)).rearrange("p (a b) -> p a b", a=8), ACT.Copy).then_inc(pair_free[pair(("u", s))], 1)
                if s == 0:
                    act.wait_ge(*free_after(("ds", 0)))
                    dma(O["new_gdn"][0, 0].rearrange("d h k v -> k (d h) v"), a_S[:, 0, :, :]).then_inc(s_state_stored, 16)
            act.wait_ge(s_a_oall, 1)
            A(a_K[:, :, :], a_o[:, :, :], ACT.Square).then_inc(s_a_osq, 1)
            act.wait_ge(s_a_oss, 1)
            ch(A(a_r[:, :], a_r[:, :], ACT.Ln, scale=1.0 / P, bias=small[:, 0:1]))
            ch.sync()
            A(a_r[:, :], a_r[:, :], ACT.Exp, scale=-0.5).then_inc(s_a_orn, 1)
            for t in range(NT):
                act.wait_ge(*full_after(("gmix", t)))
                A(mixA[:, :, P * t:P * t + P], bank(("gmix", t))[:, 0:512].rearrange("p (a t) -> p a t", a=4),
                       ACT.Copy, scale=vb[:, 78:79]).then_inc(pair_free[pair(("gmix", t))], 1)

            def x1_ready():
                act.wait_ge(s_state_stored, 48)
                for n in range(KD):
                    act.wait_ge(*free_after(("out", n)))

            rms(1, scl2, 24, x1_ready)
            act.wait_ge(s_r_max, 1)
            A(m_p[:, :, :], m_p[:, :, :], ACT.Exp).then_inc(s_r_exp, 1)
            for t in range(NT):
                name = ("h2row", t)
                act.wait_ge(*full_after(name))
                A(m_h2[:, t, :], bank(name), ACT.Copy).then_inc(pair_free[pair(name)], 1)
                act.wait_ge(*free_after(name))
                dma(h2_dram[P * t:P * t + P, :], m_h2[:, t, :]).then_inc(s_h2_stored, 16)
            act.wait_ge(s_z_stored, 32)

            def silu_gate(b):
                act.wait_ge(block_full[GU], b + 1)
                if b >= 2:
                    act.wait_ge(s_hid, b - 1)
                A(m_sg[:, b % 2, :], ps[:, GU, 0:512], ACT.Silu).then_inc(s_m_sg, 1)

            def block_out(b):
                act.wait_ge(block_full[HD], b + 1)
                if b >= 2:
                    act.wait_ge(block_full[DN], b - 1)
                A(m_hidT[:, b % 2, :], ps[:, HD, 0:512], ACT.Copy).then_inc(block_free[HD], 1)
                act.wait_ge(block_full[DN], b + 1)
                if b >= 2:
                    act.wait_ge(s_ys_stored[b % 2], 16 * (b // 2))
                A(m_dn[:, b % 2, :], ps[:, DN, :], ACT.Copy).then_inc(block_free[DN], 1)
                act.wait_ge(block_free[DN], b + 1)
                dma(ys_dram[P * b:P * b + P, :], m_dn[:, b % 2, :]).then_inc(s_ys_stored[b % 2], 16)

            for b in range(NE):
                silu_gate(b)
                if b:
                    block_out(b - 1)
            block_out(NE - 1)

            def over(b):
                silu_gate(b)
                block_out(b)

            act.wait_ge(s_table, 1)
            over_blocks(act, over)
            act.wait_ge(s_h2_stored, 16 * NT)
            for t in range(NT):
                act.wait_ge(s_y_in[t], 32)
                A(m_y[:, t, :], m_y[:, t, :], ACT.Copy, scale=gw[:, 0, t:t + 1]).then_inc(s_yA, 1)

            def x2_ready():
                for t in range(NT):
                    act.wait_ge(s_x2, t + 1)

            rms(2, None, None, x2_ready)
            for t in range(NT):
                name = ("fin", t)
                act.wait_ge(*full_after(name))
                if t >= 2:
                    act.wait_ge(s_y_stored[t % 2], 16 * (t // 2))
                ch(A(m_out[:, t % 2, 0:512], bank(name)[:, 0:512], ACT.Copy))
                A(m_out[:, t % 2, 512:1024], bank(name)[:, 512:1024], ACT.Copy).then_inc(pair_free[pair(name)], 1)

        @block.gpsimd
        def _(pool):
            ch = Chain(pool, "pool_chain")
            ch(nc.gpsimd.memset(ident[:, :], 0.0))
            ch.sync()
            nc.gpsimd.affine_select(out=ident[:, :], in_=ident[:, :], compare_op=ALU.not_equal, fill=1.0,
                                         base=0, pattern=[[-1, P]], channel_multiplier=1).then_inc(s_ident, 1)
            ch(nc.gpsimd.memset(ones[:, :], 1.0))
            ch.sync()
            for d, sign in ((0, 1), (1, -1)):
                ch(nc.gpsimd.affine_select(out=tri[:, d, :], in_=ones[:, :], compare_op=ALU.is_ge, fill=0.0,
                                           base=0, pattern=[[sign, P]], channel_multiplier=-sign))
            ch(nc.gpsimd.iota(vi[:, 0, :], pattern=[[1, P]], base=0, channel_multiplier=0))
            nc.gpsimd.iota(vi[:, 1, :], pattern=[[0, P]], base=0, channel_multiplier=1).then_inc(s_iota, 1)
            nc.gpsimd.memset(c_wg[:, :, :], 0.0).then_inc(s_wg_zero, 1)
            ch(nc.gpsimd.iota(numi[:, 0:16], pattern=[[1, 16]], base=0, channel_multiplier=0))
            ch.sync()
            nc.gpsimd.iota(numi[:, 16:16 + NT], pattern=[[P, NT]], base=0, channel_multiplier=1).then_inc(s_numi, 1)
            nc.gpsimd.memset(z_rows[:, :], 0.0).then_inc(s_z_rows, 1)
            pool.wait_ge(s_z_rows, 1)
            pool.dma_start(tok_dram.rearrange("(b p) o -> b (p o)", p=P), z_rows[0:NB, 0:P]).then_inc(s_z_stored, 16)
            pool.dma_start(ys_dram[NE * P:NB * P, :].rearrange("(b p) d -> p b d", p=P),
                           wide(z_rows[:, :], 1, MAX_OVER)).then_inc(s_z_stored, 16)
            pool.wait_ge(*full_after(("modT", 0)))
            nc.gpsimd.memset(c_x[:, :, :], 0.0).then_inc(s_c_pad, 1)
            pool.wait_ge(*full_after(("hmix", NT - 1)))
            nc.gpsimd.memset(a_pad[:, :, :], 0.0).then_inc(s_a_pad, 1)
            nc.gpsimd.memset(a_S[:, 0, :, :], 0.0).then_inc(s_a_state, 1)
            pool.dma_start(a_S[:, 1, :, :], I["state_gdn"][0, 0].rearrange("d h k v -> k (d h) v")).then_inc(s_sg_in, 16)
            for s in range(NT):
                pool.wait_ge(*free_after(("kk", s)))
                for l in range(7):
                    if l >= 2:
                        pool.wait_ge(*full_after(("t1", s, l - 2)))
                    elif s and l == 0:
                        pool.wait_ge(*full_after(("u", s - 1)))
                    for d in range(2):
                        ins = nc.gpsimd.tensor_tensor(out=a_CT[l % 2][:, 4 * d:4 * d + 4, :], in0=a_AT[:, 4 * d:4 * d + 4, :],
                                                      in1=wide(lmask[:, d, l, :], 1, 4), op=MULT)
                        ch(ins) if d == 0 else ins.then_inc(s_a_ct, 1)
            scatter = bass.IndirectOffsetOnAxis
            pool.wait_ge(s_z_stored, 32)
            pool.wait_ge(s_table, 1)
            for t in range(NT):
                for c in range(2):
                    pool.indirect_dma_start(out=tok_dram, out_offset=scatter(ap=slot[:, c, t:t + 1], axis=0),
                                            in_=num[:, 16 + t:17 + t], in_offset=None).then_inc(s_scattered, 16)
            pool.wait_ge(s_scattered, 16 * 2 * NT)
            pool.dma_start(m_idrow[0:NB, :], tok_dram.rearrange("(b p) o -> b (p o)", p=P)).then_inc(s_idrow, 16)
            pool.wait_ge(s_h2_stored, 16 * NT)
            pool.wait_ge(*free_after(("slots", 0)))

            def gather(b):
                if b >= 2:
                    pool.wait_ge(block_full[XG], b - 1)
                pool.indirect_dma_start(out=m_xg[:, b % 2, :], out_offset=None, in_=h2_dram,
                                        in_offset=scatter(ap=slot_tok[:, b:b + 1], axis=0)).then_inc(s_xg[b % 2], 16)

            def stored(b):
                pool.wait_ge(s_ys_stored[b % 2], 16 * (b // 2 + 1))

            for b in range(NE):
                gather(b)
            over_blocks(pool, gather)
            stored(NE - 2)
            stored(NE - 1)
            over_blocks(pool, stored)
            for t in range(NT):
                for c, dst in ((0, m_y), (1, m_yB)):
                    pool.indirect_dma_start(out=dst[:, t, :], out_offset=None, in_=ys_dram,
                                            in_offset=scatter(ap=slot[:, c, t:t + 1], axis=0)).then_inc(s_y_in[t], 16)

        @block.vector
        def _(dve):
            ch = Chain(dve, "dve_chain")
            V = nc.vector
            TT, TS, STT = V.tensor_tensor, V.tensor_scalar, V.scalar_tensor_tensor

            def link(ins):
                ch(ins)
                ch.sync()

            ch(V.memset(small[:, 0:1], EPS))
            V.memset(small[:, 1:2], 1.0).then_inc(s_eps, 1)
            ch(V.memset(stateB[:, 0, :, :, :], 0.0))
            dve.wait_ge(s_numi, 1)
            V.tensor_copy(num[:, 0:16 + NT], numi[:, 0:16 + NT]).then_inc(s_num, 1)
            dve.wait_ge(s_iota, 1)
            link(TT(out=vi[:, 0, :], in0=vi[:, 0, :], in1=vi[:, 1, :], op=ALU.bitwise_xor))
            link(V.tensor_copy(vf[:, 0, :], vi[:, 0, :]))
            for l, w in enumerate(LEVELS):
                link(TS(vf[:, 1, :], vf[:, 0, :], float(w), None, ALU.is_ge))
                link(STT(out=vf[:, 1, :], in0=vf[:, 0, :], scalar=float(2 * w), in1=vf[:, 1, :], op0=ALU.is_lt, op1=MULT))
                for d in range(2):
                    link(TT(out=lmask[:, d, l, :], in0=vf[:, 1, :], in1=tri[:, d, :], op=MULT))
            dve.wait_ge(*full_after(("stage", 0)))
            ch(V.tensor_copy(vecA[:, :], bank(("stage", 0))[:, 0:88]))
            V.tensor_copy(vecB[:, :], bank(("stage", 0))[:, 512:592]).then_inc(pair_free[pair(("stage", 0))], 1)
            for t in range(NT):
                name = ("xt", t)
                dve.wait_ge(*full_after(name))
                V.tensor_copy(xT[:, :, P * t:P * t + P], bank(name).rearrange("p (a b) -> p a b", a=KD)).then_inc(pair_free[pair(name)], 1)
            name = ("modT", 0)
            dve.wait_ge(*full_after(name))
            dve.wait_ge(*free_after(("stage", 0)))
            TT(out=modT[:, :, :], in0=bank(name)[:, 0:96].rearrange("p (a b) -> p a b", b=2),
                    in1=wide(vecA[:, 0:48], 2, 2), op=ADD).then_inc(pair_free[pair(name)], 1)
            dve.wait_ge(*free_after(name))
            ch(STT(out=scl1[:, :, :], in0=modT[:, 8:16, :], scalar=1.0, in1=wide(vecA[:, 48:56], 2, 2), op0=ADD, op1=MULT))
            STT(out=scl2[:, :, :], in0=modT[:, 32:40, :], scalar=1.0, in1=wide(vecA[:, 56:64], 2, 2), op0=ADD, op1=MULT).then_inc(s_mod, 1)

            def scale_x(n):
                dve.wait_ge(s_rb, n + 1)
                for k in range(KD):
                    TT(out=hT[:, k, :], in0=xT[:, k, :], in1=rb[:, :], op=MULT).then_inc(s_hraw, 1)

            for t in range(NT):
                dve.wait_ge(*free_after(("xt", t)))
            ch(STT(out=small[:, 4:8], in0=vb[:, 66:70], scalar=-1.0, in1=vb[:, 66:70], op0=MULT, op1=MIN))
            ch(TT(out=small[:, 44:48], in0=vb[:, 74:78], in1=vb[:, 74:78], op=SUB))
            TS(small[:, 16:20], vb[:, 66:70], -1.0, 0.0, MULT, MAX).then_inc(s_c_lam, 1)
            scale_x(0)
            for b in range(2):
                dve.wait_ge(*free_after(("rgx", b)))
                link(TS(c_u[:, b, :], c_x[:, b, 0:CONVW], vb[:, 48 + b:49 + b], vb[:, 56 + b:57 + b], MULT, ADD))
                for j in range(1, 4):
                    ins = STT(out=c_u[:, b, :], in0=c_x[:, b, j:j + CONVW], scalar=vb[:, 48 + 2 * j + b:49 + 2 * j + b],
                              in1=c_u[:, b, :], op0=MULT, op1=ADD)
                    link(ins) if j < 3 else ins.then_inc(s_conv_c, 1)
            dve.wait_ge(s_conv_c, 2)
            dve.wait_ge(s_c_ln, 1)
            link(TT(out=small[:, 8:12], in0=small[:, 8:12], in1=small[:, 16:20], op=ADD))
            TS(small[:, 12:16], small[:, 8:12], -RG_C, None, MULT).then_inc(s_c_nc8, 1)
            link(V.reciprocal(small[:, 48:52], small[:, 44:48]))
            link(TT(out=small[:, 48:52], in0=small[:, 48:52], in1=small[:, 44:48], op=MULT))
            link(TT(out=small[:, 48:52], in0=small[:, 48:52], in1=small[:, 48:52], op=SUB))
            link(TS(small[:, 52:56], small[:, 48:52], -1.0, 1.0, MULT, ADD))
            dve.wait_ge(s_c_a, 8)
            link(TT(out=c_h[:, :, :], in0=c_a[:, :, :], in1=c_a[:, :, :], op=MULT))
            link(STT(out=c_h[:, :, :], in0=c_h[:, :, :], scalar=1.0, in1=c_t[:, :, :], op0=ADD, op1=MULT))
            TS(c_h[:, :, :], c_h[:, :, :], -1.0, 0.0, MULT, MAX).then_inc(s_c_y, 1)
            for d in range(2):
                for a, e, g in SEG:
                    ch(TT(out=c_g[:, d, 1, :, a:e], in0=c_g[:, d, 1, :, a:e], in1=c_u[:, :, a + 2 * g:e + 2 * g], op=MULT))
            ch.sync()
            dve.wait_ge(s_c_sqrt, 1)
            for d in range(2):
                ch(TT(out=c_t[:, 2 * d:2 * d + 2, :], in0=c_t[:, 2 * d:2 * d + 2, :], in1=c_g[:, d, 1, :, :], op=MULT))
            ch.sync()
            for db in range(4):
                for a, e, g in SEG:
                    way = slice(None, None, -1) if db // 2 else slice(None)
                    ch(V.tensor_tensor_scan(c_h[:, db, a:e][:, way], c_a[:, db, a:e][:, way], c_t[:, db, a:e][:, way],
                                            vb[:, 70 + db:71 + db] if g else 0.0, MULT, ADD))
            ch.sync()
            ch(V.tensor_copy(small[:, 20:22], c_h[:, 0:2, CTX - 1]))
            V.tensor_copy(small[:, 22:24], c_h[:, 2:4, 0]).then_inc(s_c_fin, 1)
            ch.sync()
            dve.wait_ge(s_c_fin, 1)
            link(TT(out=c_h[:, 0:2, :], in0=c_h[:, 0:2, :], in1=c_h[:, 2:4, :], op=ADD))
            for b in range(2):
                TT(out=mixBC[:, 2 + b, 0:CTX], in0=c_h[:, b, 0:CTX], in1=c_yg[:, b, 0:CTX], op=MULT).then_inc(s_c_mix, 1)
                ins = TT(out=mixBC[:, 2 + b, CTX:T].rearrange("p (r c) -> p c r", c=GRID_W),
                         in0=c_h[:, b, CTX:T].rearrange("p (c r) -> p c r", r=ROWS),
                         in1=c_yg[:, b, CTX:T].rearrange("p (c r) -> p c r", r=ROWS), op=MULT)
                ins.then_inc(s_c_mix, 1)
            dve.wait_ge(s_c_mix, 4)
            V.memset(b_o[:, :, :], 0.0).then_inc(s_c_done, 1)
            dve.wait_ge(*free_after(("hf", 3)))
            for dp in range(4):
                ch(TS(b_f[:, dp, :], b_f[:, dp, :], small[:, 52 + dp:53 + dp], small[:, 48 + dp:49 + dp], MULT, ADD))
                ins = TS(b_k[:, dp, :], b_k[:, dp, :], small[:, 52 + dp:53 + dp], None, MULT)
                ch(ins) if dp < 3 else ins.then_inc(s_b_k, 1)
            dve.wait_ge(s_b_k, 1)
            ch.sync()
            link(TS(b_Z[0][:, :, :], b_f[:, :, :], F_MIN, LNSPLIT, MAX, MIN))
            TS(b_f[:, :, :], b_f[:, :, :], LNSPLIT, None, MAX).then_inc(s_b_m, 1)
            dve.wait_ge(s_b_ln, 1)
            link(TT(out=b_f[:, :, :], in0=b_f[:, :, :], in1=b_Z[0][:, :, :], op=ADD))
            for dp in range(4):
                way = slice(None, None, -1) if dp // 2 else slice(None)
                for t in range(NT):
                    ch(V.tensor_tensor_scan(b_b[:, dp, P * t:P * t + P][:, way], ones[:, :],
                                            b_f[:, dp, P * t:P * t + P][:, way], 0.0, MULT, ADD))
            ch.sync()

            def blocks(v, d, w):
                v = v[:, 2 * d:2 * d + 2, :] if v.shape[1] == 4 else v
                return v.rearrange("p a t -> p (a t)").rearrange("p (n w) -> p n w", w=w)

            def level_out(L):
                if L == 0:
                    dve.wait_ge(s_z_stored, 32)
                for t in range(NT):
                    name = ("lev", L, t)
                    dve.wait_ge(*full_after(name))
                    src = bank(name).rearrange("p (e d q i) -> p e d q i", e=2, d=2, q=2)
                    dst = b_at[:, t, :, :].rearrange("p (e d q) i -> p e d q i", e=2, d=2)
                    if L == 0:
                        TT(out=b_at[:, t, :, :], in0=bank(name).rearrange("p (a i) -> p a i", a=8),
                                in1=wide(ident[:, :], 1, 8), op=MULT).then_inc(pair_free[pair(name)], 1)
                    else:
                        dve.wait_ge(*free_after(("lev", L - 1, t)))
                        msk = wide(lmask[:, :, L - 1, :].bitcast(I32), 2, 2)
                        ch(V.copy_predicated(dst[:, 0], msk, src[:, 0]))
                        V.copy_predicated(dst[:, 1], msk, src[:, 1]).then_inc(pair_free[pair(name)], 1)

            for l, s in enumerate(LEVELS):
                w, n = 2 * s, 2 * T // (2 * s)
                L = l + 1
                for d in range(2):
                    b, E = blocks(b_b, d, w), blocks(b_f, d, w)
                    mid = b[:, :, s - 1:s] if d == 0 else b[:, :, s:s + 1]
                    mid = mid.to_broadcast([P, n, s])
                    lo, hi = b[:, :, 0:s], b[:, :, s:w]
                    ch(TT(out=E[:, :, 0:s], in0=mid if d == 0 else lo, in1=lo if d == 0 else mid, op=SUB))
                    ins = TT(out=E[:, :, s:w], in0=hi if d == 0 else mid, in1=mid if d == 0 else hi, op=SUB)
                    ch(ins) if d == 0 else ins.then_inc(s_b_d, 1)
                level_out(l)
                dve.wait_ge(s_b_e, L)
                if L >= 3:
                    dve.wait_ge(*full_after(("lev", L - 2, NT - 1)))
                for d in range(2):
                    E, Z, q, k = (blocks(v, d, w) for v in (b_f, b_Z[L % 2], b_q, b_k))
                    left, right = (k, q) if d == 0 else (q, k)
                    ch(TT(out=Z[:, :, 0:s], in0=left[:, :, 0:s], in1=E[:, :, 0:s], op=MULT))
                    ins = TT(out=Z[:, :, s:w], in0=right[:, :, s:w], in1=E[:, :, s:w], op=MULT)
                    ch(ins) if d == 0 else ins.then_inc(s_b_z, 1)
                ch.sync()
                dve.wait_ge(s_b_z, L)
            level_out(7)
            dve.wait_ge(s_b_e, 8)
            for d in range(2):
                ch(TT(out=b_Z[0][:, 2 * d:2 * d + 2, :], in0=b_q[:, :, :], in1=b_f[:, 2 * d:2 * d + 2, :], op=MULT))
            ends = b_f.rearrange("p q (t c) -> p t q c", c=P)
            ch(V.tensor_copy(b_end[:, :, 0:2], ends[:, :, 0:2, P - 1]))
            ch(V.tensor_copy(b_end[:, 0:1, 2:4], ends[:, 0:1, 2:4, 0]))
            ch(V.tensor_copy(b_end[:, 1:NT, 2:4], ends[:, 1:NT, 2:4, 0][:, ::-1]))
            for d in range(2):
                b, Z = blocks(b_b, d, P), blocks(b_Z[1], d, P)
                end = (b[:, :, P - 1:P] if d == 0 else b[:, :, 0:1]).to_broadcast([P, 2 * NT, P])
                ins = TT(out=Z, in0=end, in1=b, op=SUB)
                ch(ins) if d == 0 else ins.then_inc(s_b_d, 1)
            ch.sync()
            dve.wait_ge(s_b_e, 9)
            TT(out=b_Z[1][:, :, :], in0=b_Z[1][:, :, :], in1=b_k[:, :, :], op=MULT).then_inc(s_b_kd, 1)
            dve.wait_ge(s_sb_in, 16)
            V.memset(small[:, 57:58], 0.0).then_inc(s_b_state, 1)
            ch.sync()
            for s in range(NT):
                name = ("ho", s)
                dve.wait_ge(*full_after(name))
                for d in range(2):
                    o = b_o[:, (FWD, BWD)[d][s], :].rearrange("p (q e v) -> p e q v", q=2, e=2)
                    src = bank(name).rearrange("p (e x) -> p e x", e=2)[:, :, P * d:P * d + P]
                    ins = TT(out=o, in0=src.rearrange("p e (q v) -> p e q v", q=2), in1=o, op=ADD)
                    if d == 0:
                        link(ins)
                    else:
                        ins.then_inc(pair_free[pair(name)], 1)
                name = ("hs", s)
                dve.wait_ge(*full_after(name))
                S = stateB[:, min(s, 1), :, :, :].rearrange("p d q v -> p (d q) v")
                link(TT(out=S, in0=S, in1=wide(b_end[:, s, :], 2, HK), op=MULT))
                src = bank(name)[:, 0:512].rearrange("p (c v) -> p c v", c=4)
                ch(TT(out=S[0:64], in0=src[0:64, :, 0:64], in1=S[0:64], op=ADD))
                TT(out=S[64:128], in0=src[64:128, :, 64:128], in1=S[64:128], op=ADD).then_inc(pair_free[pair(name)], 1)
                dve.wait_ge(*free_after(name))
                dve.wait_ge(*free_after(("ho", s)))
                ch.sync()
            V.memset(small[:, 58:59], 0.0).then_inc(s_b_oall, 1)
            dve.wait_ge(s_b_sq, 1)
            V.tensor_reduce(small[:, 24:44], b_f[:, 0:2, :].rearrange("p a t -> p (a t)")
                                 .rearrange("p (n v) -> p n v", v=HK), AX.X, ADD).then_inc(s_b_ss, 1)
            dve.wait_ge(s_b_r, 1)
            o = b_o.rearrange("p t c -> p (t c)").rearrange("p (n v) -> p n v", v=HK)
            link(TT(out=o, in0=o, in1=wide(small[:, 24:44], 2, HK), op=MULT))
            TT(out=b_o[:, :, :], in0=b_o[:, :, :], in1=b_g[:, :, :], op=MULT).then_inc(s_b_on, 1)
            for b in range(12):
                dve.wait_ge(*free_after(("qkv", b)))
                if b >= 2:
                    dve.wait_ge(s_a_silu, 2 * (b - 1))
                link(TS(a_cv[:, b % 2, :], a_pad[:, b % 2, 0:CONVW], vb[:, b:b + 1], None, MULT))
                for j in range(1, 4):
                    ins = STT(out=a_cv[:, b % 2, :], in0=a_pad[:, b % 2, j:j + CONVW], scalar=vb[:, 12 * j + b:12 * j + b + 1],
                              in1=a_cv[:, b % 2, :], op0=MULT, op1=ADD)
                    link(ins) if j < 3 else ins.then_inc(s_a_conv, 1)
            name = ("ab", 0)
            dve.wait_ge(*full_after(name))
            dve.wait_ge(s_small_in, 16 * 5)
            ab = bank(name)[:, 0:16 * NT].rearrange("p (t c) -> p t c", c=16)
            ch(TT(out=a_z[:, :, :], in0=ab[:, :, 0:8], in1=wide(dtb[:, :], 1, NT), op=ADD))
            V.tensor_copy(a_beta[:, :, :], ab[:, :, 8:16]).then_inc(pair_free[pair(name)], 1)
            dve.wait_ge(*free_after(name))
            ch.sync()
            link(STT(out=a_w[:, :, :], in0=a_z[:, :, :], scalar=-1.0, in1=a_z[:, :, :], op0=MULT, op1=MIN))
            TS(a_z[:, :, :], a_z[:, :, :], 0.0, None, MAX).then_inc(s_a_z, 1)
            dve.wait_ge(s_a_rn, 1)
            ch(STT(out=a_qk[:, 0:4, :], in0=a_qk[:, 0:4, :], scalar=float(P) ** -0.5, in1=a_rn[:, 0:4, :], op0=MULT, op1=MULT))
            TT(out=a_qk[:, 4:8, :], in0=a_qk[:, 4:8, :], in1=a_rn[:, 4:8, :], op=MULT).then_inc(s_a_norm, 1)
            dve.wait_ge(s_a_ln, 1)
            dve.wait_ge(s_a_z, 1)
            link(TT(out=a_w[:, :, :], in0=a_w[:, :, :], in1=a_z[:, :, :], op=ADD))
            STT(out=a_la[:, :, :], in0=a_w[:, :, :], scalar=-1.0, in1=wide(a_nea[:, :], 1, NT), op0=MULT, op1=MULT).then_inc(s_a_la, 1)
            name = ("gcol", 0)
            dve.wait_ge(*full_after(name))
            V.tensor_copy(a_gc[:, :, :], bank(name)[:, 0:8 * NT].rearrange("p (t c) -> p t c", c=8)).then_inc(pair_free[pair(name)], 1)
            dve.wait_ge(s_a_eg, 1)
            link(TT(out=a_beg[:, :, :], in0=a_beg[:, :, :], in1=a_beta[:, :, :], op=MULT))
            for dst, src in ((s_beta, a_beta), (s_gc, a_gc), (s_beg, a_beg)):
                ch(V.tensor_copy(dst[:, :, 0:4], src[:, :, 0:4]))
                ch(V.tensor_copy(dst[:, 0:1, 4:8], src[:, 0:1, 4:8]))
                ch(V.tensor_copy(dst[:, 1:NT, 4:8], src[:, 1:NT, 4:8][:, ::-1]))
            ch.sync()
            dve.wait_ge(*free_after(("rows", NT - 1)))
            ch(V.memset(a_o[:, :, :], 0.0))
            eight = lambda v: v.rearrange("p (a b) -> p a b", a=8)
            for s in range(NT):
                tile = lambda d: (FWD, BWD)[d][s]
                name = ("gb", s)
                dve.wait_ge(*full_after(name))
                if s:
                    dve.wait_ge(*full_after(("ds", s - 1)))
                link(TT(out=a_dec[:, :, :], in0=eight(bank(name)), in1=wide(s_gc[:, s, :], 2, P), op=SUB))
                TS(a_dec[:, :, :], a_dec[:, :, :], 0.0, None, MIN).then_inc(s_a_d, 1)
                dve.wait_ge(s_a_dec, s + 1)
                dve.wait_ge(*free_after(name))
                for d in range(2):
                    last = P - 1 if d == 0 else 0
                    h = slice(4 * d, 4 * d + 4)
                    ch(TT(out=a_Kd[:, h, :], in0=a_K[:, tile(d), :].rearrange("p (h c) -> p h c", h=4),
                          in1=a_dec[:, h, last:last + 1].to_broadcast([P, 4, P]), op=MULT))
                    ch(V.tensor_copy(a_ge[:, s, h], a_qe[:, h, last]))
                ch.sync()
                for d in range(2):
                    h = slice(4 * d, 4 * d + 4)
                    ch(TT(out=a_qe[:, h, :], in0=a_qe[:, h, :], in1=a_qk[:, 0:4, P * tile(d):P * tile(d) + P], op=MULT))
                    ch(TT(out=a_dec[:, h, :], in0=a_dec[:, h, :], in1=wide(tri[:, d, :], 1, 4), op=MULT))
                ch.sync()
                if s:
                    dve.wait_ge(s_a_ct, 7 * s)
                name = ("kk", s)
                dve.wait_ge(*full_after(name))
                TT(out=a_AT[:, :, :], in0=eight(bank(name)), in1=a_dec[:, :, :], op=MULT).then_inc(pair_free[pair(name)], 1)
                name = ("kq", s)
                dve.wait_ge(*full_after(name))
                TT(out=a_dec[:, :, :], in0=eight(bank(name)), in1=a_dec[:, :, :], op=MULT).then_inc(pair_free[pair(name)], 1)
                for l in range(7):
                    name = ("t1", s, l)
                    dve.wait_ge(*full_after(name))
                    TT(out=a_T1[:, :, :], in0=eight(bank(name)), in1=wide(s_beta[:, s, :], 2, P), op=MULT).then_inc(pair_free[pair(name)], 1)
                    if l == 0:
                        dve.wait_ge(*free_after(name))
                        TT(out=a_X[:, :, :], in0=wide(ident[:, :], 1, 8), in1=a_T1[:, :, :], op=SUB).then_inc(s_a_x0, 1)
                        dve.wait_ge(s_a_x0, s + 1)
                    elif l < 6:
                        name = ("dx", s, l)
                        dve.wait_ge(*full_after(name))
                        if l > 1:
                            dve.wait_ge(*free_after(("dx", s, l - 1)))
                        TT(out=a_X[:, :, :], in0=a_X[:, :, :], in1=eight(bank(name)), op=SUB).then_inc(pair_free[pair(name)], 1)
                    name = ("dxt", s, l)
                    dve.wait_ge(*full_after(name))
                    if l:
                        dve.wait_ge(*free_after(("dxt", s, l - 1)))
                    xt0 = a_XT[:, :, :] if l else wide(ident[:, :], 1, 8)
                    TT(out=a_XT[:, :, :], in0=xt0, in1=eight(bank(name)), op=SUB).then_inc(pair_free[pair(name)], 1)
                name = ("ks", s)
                dve.wait_ge(*full_after(name))
                TT(out=a_CT[1][:, :, :], in0=eight(bank(name)), in1=wide(s_beg[:, s, :], 2, P), op=MULT).then_inc(pair_free[pair(name)], 1)
                for d in range(2):
                    h = slice(4 * d, 4 * d + 4)
                    ch(TT(out=a_CT[0][:, h, :], in0=a_V[:, tile(d), :].rearrange("p (h c) -> p h c", h=4),
                          in1=wide(s_beta[:, s, h], 2, P), op=MULT))
                ch.sync()
                dve.wait_ge(*free_after(name))
                TT(out=a_CT[0][:, :, :], in0=a_CT[0][:, :, :], in1=a_CT[1][:, :, :], op=SUB).then_inc(s_a_rhs, 1)
                dve.wait_ge(s_a_rhs, s + 1)
                name = ("o", s)
                dve.wait_ge(*full_after(name))
                for d in range(2):
                    o = a_o[:, tile(d), :]
                    ins = TT(out=o, in0=bank(name)[:, 512 * d:512 * d + 512], in1=o, op=ADD)
                    if d == 0:
                        link(ins)
                    else:
                        ins.then_inc(pair_free[pair(name)], 1)
                name = ("ds", s)
                dve.wait_ge(*full_after(name))
                S = a_S[:, min(s, 1), :, :]
                if s == 1:
                    dve.wait_ge(s_sg_in, 16)
                if s == 0:
                    dve.wait_ge(s_a_state, 1)
                link(TT(out=S, in0=S, in1=wide(a_ge[:, s, :], 2, P), op=MULT))
                TT(out=S, in0=S, in1=eight(bank(name)), op=ADD).then_inc(pair_free[pair(name)], 1)
                dve.wait_ge(*free_after(name))
                dve.wait_ge(*free_after(("o", s)))
            V.memset(small[:, 59:60], 0.0).then_inc(s_a_oall, 1)
            dve.wait_ge(s_a_osq, 1)
            V.tensor_reduce(a_r[:, :], a_K.rearrange("p t (h v) -> p (t h) v", h=4), AX.X, ADD).then_inc(s_a_oss, 1)
            dve.wait_ge(s_a_orn, 1)
            o = a_o.rearrange("p t (h v) -> p (t h) v", h=4)
            link(TT(out=o, in0=o, in1=wide(a_r[:, :], 2, P), op=MULT))
            TT(out=a_o[:, :, :], in0=a_o[:, :, :], in1=a_g[:, :, :], op=MULT).then_inc(s_a_on, 1)
            for n in range(KD):
                name = ("out", n)
                dve.wait_ge(*full_after(name))
                for a, e, out, g in segs(name):
                    ins = STT(out=xT[:, n, a:e], in0=out, scalar=modT[:, 16 + n, g:g + 1], in1=xT[:, n, a:e],
                              op0=MULT, op1=ADD)
                    ch(ins) if g == 0 else ins.then_inc(pair_free[pair(name)], 1)
            for n in range(KD):
                dve.wait_ge(*free_after(("out", n)))
            scale_x(1)
            name = ("router", 0)
            dve.wait_ge(*full_after(name))
            link(TT(out=m_p[:, :, :], in0=bank(name)[:, 0:NT * NE].rearrange("p (t e) -> p t e", e=NE),
                    in1=wide(rbias[:, :], 1, NT), op=ADD))
            link(V.tensor_reduce(m_col[:, 0:NT], m_p[:, :, :], AX.X, MAX))
            V.memset(m_gg[:, :, :], 0.0).then_inc(pair_free[pair(name)], 1)
            TT(out=m_p[:, :, :], in0=m_p[:, :, :], in1=wide(m_col[:, 0:NT], 2, NE), op=SUB).then_inc(s_r_max, 1)
            dve.wait_ge(s_r_exp, 1)
            link(V.tensor_reduce(m_col[:, 0:NT], m_p[:, :, :], AX.X, ADD))
            link(V.reciprocal(m_col[:, 8:8 + NT], m_col[:, 0:NT]))
            link(TT(out=m_p[:, :, :], in0=m_p[:, :, :], in1=wide(m_col[:, 8:8 + NT], 2, NE), op=MULT))

            def rank4(values, rank, tmp):
                for i in range(4):
                    ch(V.memset(rank[:, :, i:i + 1], float(i)))
                ch.sync()
                for off in range(1, 4):
                    n = 4 - off
                    link(TT(out=tmp[:, :, 0:n], in0=values[:, :, off:4], in1=values[:, :, 0:n], op=ALU.is_gt))
                    link(TT(out=rank[:, :, 0:n], in0=rank[:, :, 0:n], in1=tmp[:, :, 0:n], op=ADD))
                    link(TT(out=rank[:, :, off:4], in0=rank[:, :, off:4], in1=tmp[:, :, 0:n], op=SUB))

            fours = lambda v: v.rearrange("p t e -> p (t e)").rearrange("p (n e) -> p n e", e=4)
            rank4(fours(m_p), fours(m_rank), fours(m_gt))
            link(STT(out=m_gate[:, :, :], in0=m_rank[:, :, :], scalar=2.0, in1=m_p[:, :, :], op0=ALU.is_lt, op1=MULT))
            link(V.tensor_reduce(m_gs.rearrange("p t g -> p (t g)"), fours(m_gate), AX.X, ADD))
            dve.wait_ge(*free_after(("router", 0)))
            rank4(m_gs, m_gr, m_gg)
            link(TS(m_gr[:, :, :], m_gr[:, :, :], 1.0, None, ALU.is_lt))
            link(TT(out=fours(m_gate), in0=fours(m_gate), in1=wide(m_gr.rearrange("p t g -> p (t g)"), 2, 4), op=MULT))
            STT(out=fours(m_sel), in0=fours(m_rank), scalar=2.0, in1=wide(m_gr.rearrange("p t g -> p (t g)"), 2, 4),
                op0=ALU.is_lt, op1=MULT).then_inc(s_sel, 1)
            dve.wait_ge(s_sel, 1)
            link(V.tensor_reduce(m_col[:, 0:NT], m_gate[:, :, :], AX.X, ADD))
            link(V.reciprocal(m_col[:, 8:8 + NT], m_col[:, 0:NT]))
            link(TT(out=m_gate[:, :, :], in0=m_gate[:, :, :], in1=wide(m_col[:, 8:8 + NT], 2, NE), op=MULT))
            name = ("pos", 0)
            dve.wait_ge(*full_after(name))
            place = bank(name)[:, 0:NT * NE].rearrange("p (t e) -> p t e", e=NE)
            ch(V.tensor_copy(m_t1[:, :, :], place))
            V.tensor_copy(m_no[:, 0, :], bank(name)[:, NT * NE:NT * NE + NE]).then_inc(pair_free[pair(name)], 1)
            ch.sync()
            dve.wait_ge(s_num, 1)
            dve.wait_ge(*free_after(name))
            link(STT(out=m_c4[:, :, :], in0=wide(m_no[:, 0, :], 2, 4), scalar=1.0 / P,
                     in1=wide(num[:, 1:5], 1, NE), op0=MULT, op1=ALU.is_gt))
            link(V.tensor_reduce(m_no[:, 1, :], m_c4[:, :, :], AX.X, ADD))
            link(V.tensor_tensor_scan(m_no[:, 2, :], ones[:, 0:NE], m_no[:, 1, :], 0.0, MULT, ADD))
            link(TT(out=m_no[:, 3, :], in0=m_no[:, 2, :], in1=m_no[:, 1, :], op=SUB))
            link(TT(out=m_no[:, 3, :], in0=m_no[:, 3, :], in1=num[:, 0:NE], op=SUB))
            link(TS(m_no[:, 3, :], m_no[:, 3, :], float(NE - 1), float(P), ADD, MULT))
            link(STT(out=m_gt[:, :, :], in0=m_t1[:, :, :], scalar=float(P), in1=wide(m_no[:, 3, :], 1, NT),
                     op0=ALU.is_gt, op1=MULT))
            link(TT(out=m_t1[:, :, :], in0=m_t1[:, :, :], in1=m_gt[:, :, :], op=ADD))
            link(STT(out=m_t1[:, :, :], in0=wide(num[:, 0:NE], 1, NT), scalar=float(P), in1=m_t1[:, :, :], op0=MULT, op1=ADD))
            link(TT(out=m_t1[:, :, :], in0=m_t1[:, :, :], in1=m_sel[:, :, :], op=MULT))
            link(V.tensor_reduce(m_ab[:, 1, :], m_t1[:, :, :], AX.X, MAX))
            link(V.tensor_reduce(m_ab[:, 0, :], m_t1[:, :, :], AX.X, ADD))
            link(TT(out=m_ab[:, 0, :], in0=m_ab[:, 0, :], in1=m_ab[:, 1, :], op=SUB))
            ch(TS(slot[:, :, :], m_ab[:, :, :], -1.0, None, ADD))
            link(TT(out=m_cmp[:, :, :], in0=wide(m_no[:, 2, :], 1, MAX_OVER), in1=wide(num[:, 0:MAX_OVER], 2, NE), op=ALU.is_le))
            link(V.tensor_reduce(m_of[:, 0:MAX_OVER], m_cmp[:, :, :], AX.X, ADD))
            ch(V.tensor_copy(m_of[:, MAX_OVER:MAX_OVER + 1], m_no[:, 2, NE - 1:NE]))
            ch.sync()
            TS(table[:, 0:MAX_OVER + 1], m_of[:, 0:MAX_OVER + 1], float(NE - 1), None, MIN).then_inc(s_table, 1)
            for c in range(2):
                link(TT(out=m_gt[:, :, :], in0=m_t1[:, :, :], in1=wide(m_ab[:, c, :], 2, NE), op=ALU.is_equal))
                link(TT(out=m_gt[:, :, :], in0=m_gt[:, :, :], in1=m_gate[:, :, :], op=MULT))
                link(V.tensor_reduce(gw[:, c, :], m_gt[:, :, :], AX.X, ADD))
            name = ("slots", 0)
            dve.wait_ge(*full_after(name))
            V.tensor_copy(slot_tok[:, :], bank(name)[:, 0:NB]).then_inc(pair_free[pair(name)], 1)

            def transposed(b):
                dve.wait_ge(block_full[XG], b + 1)
                if b >= 2:
                    dve.wait_ge(block_full[GU], b - 1)
                V.tensor_copy(m_xgT[:, b % 2, :, :], ps[:, XG, :].rearrange("p (a b) -> p a b", a=KD)).then_inc(block_free[XG], 1)

            def hidden(b):
                dve.wait_ge(s_m_sg, b + 1)
                if b >= 2:
                    dve.wait_ge(block_full[HD], b - 1)
                TT(out=m_hid[:, b % 2, :], in0=ps[:, GU, 512:1024], in1=m_sg[:, b % 2, :], op=MULT).then_inc(s_hid, 1)
                dve.wait_ge(s_hid, b + 1)
                V.memset(small[:, 60:61], 0.0).then_inc(block_free[GU], 1)

            transposed(0)
            for b in range(NE):
                hidden(b)
                if b + 1 < NE:
                    transposed(b + 1)

            def over(b):
                transposed(b)
                hidden(b)

            dve.wait_ge(s_table, 1)
            over_blocks(dve, over)
            for t in range(NT):
                dve.wait_ge(s_yA, t + 1)
                dve.wait_ge(s_y_in[t], 32)
                STT(out=m_y[:, t, :], in0=m_yB[:, t, :], scalar=gw[:, 1, t:t + 1], in1=m_y[:, t, :],
                    op0=MULT, op1=ADD).then_inc(s_y, 1)
            for t in range(NT):
                name = ("yT", t)
                dve.wait_ge(*full_after(name))
                g = min(t, 1)
                TT(out=m_tmp[:, :, :], in0=eight(bank(name)), in1=wide(modT[:, 40:48, g], 2, P), op=MULT).then_inc(pair_free[pair(name)], 1)
                dve.wait_ge(*free_after(name))
                TT(out=xT[:, :, P * t:P * t + P], in0=xT[:, :, P * t:P * t + P], in1=m_tmp[:, :, :], op=ADD).then_inc(s_x2, 1)
                dve.wait_ge(s_x2, t + 1)
            dve.wait_ge(s_rb, 3)
            for k in range(KD):
                STT(out=hT[:, k, :], in0=xT[:, k, :], scalar=vecA[:, 64 + k:65 + k], in1=rb[:, :],
                         op0=MULT, op1=MULT).then_inc(s_fin_h, 1)


def build(nc, inputs):
    arrays, I = {}, {}
    for name, a in inputs.items():
        a = np.ascontiguousarray(a)
        arrays[f"in_{name}"] = a
        I[name] = nc.dram_tensor(f"in_{name}", a.shape, mybir.dt.from_np(a.dtype), kind="ExternalInput").ap()
    O = {}
    for name, shape in OUTS.items():
        O[name] = nc.dram_tensor(f"out_{name}", shape, F32, kind="ExternalOutput").ap()
    layer_program(nc, I, O)
    return arrays


OUTS = {"y_prompt": (1, CTX, D), "y_sample": (1, LAT, D), "new_gdn": (1, 1, 2, GH, P, P),
        "new_hgrn": (1, 1, 2, HH, HK, HK), "new_rg": (1, 1, 2, 256)}


def kernel(**inputs):
    import concourse.bacc as _bacc
    from concourse.bass_utils import run_bass_kernel_spmd as _run

    nc = _bacc.Bacc("TRN2", target_bir_lowering=False, num_devices=1)
    arrays = build(nc, inputs)
    r = _run(nc, [arrays], core_ids=[0])
    return tuple(r.results[0][f"out_{name}"] for name in OUTS)
```

```python
from contextlib import ExitStack

import numpy as np
import concourse.bass as bass
from concourse import mybir

F32 = mybir.dt.float32
I32 = mybir.dt.int32
U32 = mybir.dt.uint32
ACT = mybir.ActivationFunctionType
ALU = mybir.AluOpType
AX = mybir.AxisListType

P = 128
D = 1024
KD = D // P
CTX, LAT = 128, 512
T = CTX + LAT
NT = T // P
GH = 4
HH, HK = 4, 64
NE = 16
FF = 512
EPS = 1e-6
RG_C = 8.0
F_MIN = 1e-30
LNSPLIT = 2.0 ** -60
GRID_W, ROWS = 64, LAT // 64
PADW = 2 + CTX + 2 + LAT + 1
CONVW = PADW - 3
SEG = ((0, CTX, 0), (CTX, T, 1))
FWD = (0, 1, 2, 3, 4)
BWD = (0, 4, 3, 2, 1)
LEVELS = (1, 2, 4, 8, 16, 32, 64)
O_QKV, O_G, O_AB, O_HQ, O_HF1, O_RG = 0, 1536, 2048, 2064, 3088, 3344
O_PARTS = ((slice(0, 1), slice(2, 4)), (slice(1, 5, 3),))
OUT_ORDER = (4, 5, 6, 7, 0, 1, 2, 3)
RING = 3
MAX_OVER = (2 * T - 1) // P
NB = NE + MAX_OVER
XG, GU, HD, DN = range(4)
MSLOTS = 6
SLAB = 8 * 512
MULT, ADD, SUB, MAX, MIN = ALU.mult, ALU.add, ALU.subtract, ALU.max, ALU.min


def slab_plan():
    s = [(("ada", i), 512) for i in range(4)]
    s += [(("rg", 0), 512), (("hq", 0), 512), (("hg", 0), 512), (("hf", 0), 256)]
    s += [(("ada", i), 512) for i in range(4, 12)]
    s += [(("gdn", i), 512) for i in range(4)]
    s += [(("out", i), 512) for i in (1, 0)]
    return s


def gdn_order():
    order = [("gb", 0), ("exp", 0), ("bb", 0), ("kk", 0), ("kq", 0)]
    for s in range(NT):
        for l in range(7):
            order.append(("level", s, l))
            if s:
                order += {1: [("ks", s - 1)], 2: [("u", s - 1)], 3: [("o", s - 1), ("ds", s - 1)]}.get(l, [])
            if s + 1 < NT:
                order += {4: [("gb", s + 1)], 5: [("exp", s + 1), ("bb", s + 1), ("kk", s + 1), ("kq", s + 1)]}.get(l, [])
    return order + [(kind, NT - 1) for kind in ("ks", "u", "o")]


START = (("ada", 0), ("xt", 0), ("xt", 1), ("adaT", 0), ("ada", 1), ("xt", 2), ("xt", 3), ("xt", 4), ("adaT", 1),
         ("rms", 0), ("ada", 2), ("adaT", 2), ("ada", 3), ("adaT", 3))


def job_plan():
    j = [("stage", 0)] + list(START)
    j += [("rgx", b) for b in range(2)] + [("rgy", b) for b in range(2)]
    j += [("hq", b) for b in range(2)] + [("hi", n) for n in range(2)] + [("hgate", n) for n in range(2)]
    j += [("rgg", n) for n in range(8)]
    j += [("hf", n) for n in range(4)]
    j += [("ada", 4), ("ada", 5), ("adaT", 4)]
    for l in range(8):
        j += [("lev", l, t) for t in range(NT)] + [("adaT", 4 + l)] * (l > 0) + [("ada", 6 + l)] * (l < 6)
    j += [("qkv", 0)] + [("kdt", t) for t in range(NT)]
    for s in range(NT):
        j += [("ho", s), ("hs", s), ("qkv", s + 1)]
    j += [("qkv", 6), ("qkv", 7)]
    j += [("hmix", t) for t in range(NT)] + [("ab", 0)]
    for b in range(8, 12):
        j += [("qkv", b)] + [("abT", 0)] * (b == 8) + [("ss", 2 * b - 16), ("ss", 2 * b - 15)]
    j += [("gg", t) for t in range(NT)] + [("gcol", 0)] + [("rows", t) for t in range(NT)]
    for stage in gdn_order():
        kind, s = stage[:2]
        if kind == "level":
            l = stage[2]
            halves = [[("t1", s, l, g)] for g in range(2)] if l else []
            for g in range(2):
                halves += [[("x0", s, g)]] if l == 0 else [[("dx", s, l, g)] * (l < 6) + [("dxt", s, l, g)]]
            j += sum(halves, [])
        elif kind != "exp":
            j.append(stage)
    j += [("gmix", t) for t in range(NT)]
    j += [("out", n) for n in OUT_ORDER]
    j += [("rms", 1), ("router", 0), ("routerT", 0)]
    j += [("h2row", t) for t in range(3)] + [("pos", 0)] + [("h2row", t) for t in range(3, NT)]
    j += [("rowvec", i) for i in range(3)] + [("xrow", t) for t in range(NT)] + [("slots", 0)]
    return j


def layer_program(nc, I, O, stop=None):
    ctx = ExitStack()
    with ctx:
        def sb(name, *shape, dt=F32):
            return ctx.enter_context(nc.sbuf_tensor(name, [P, *shape], dt))

        def sem(name):
            return ctx.enter_context(nc.semaphore(name))

        SLABS = slab_plan()
        SLAB_N = {name: n for n, (name, _) in enumerate(SLABS)}

        ps = ctx.enter_context(nc.psum_tensor("ps", [P, 4, 1024], F32))
        ring = sb("ring", RING, SLAB)
        xT = sb("xT", KD, T)
        hT = sb("hT", KD, T)
        mixBC = sb("mixBC", 4, T)
        ident = sb("ident", P)
        ones = sb("ones", P)
        tri = sb("tri", 2, P)
        lmask = sb("lmask", 2, 7, P)
        vi = sb("vi", 2, P, dt=I32)
        vf = sb("vf", 2, P)
        b_end = sb("b_end", NT, 4)
        stA = sb("stA", P)
        stB = sb("stB", P)
        vecA = sb("vecA", 88)
        vecB = sb("vecB", 80)
        cs = sb("cs", KD, 2)
        modT = sb("modT", 48, 2)
        scl1 = sb("scl1", KD, 2)
        scl2 = sb("scl2", KD, 2)
        wab = sb("wab", KD, 16)
        rw = sb("rw", KD, NE)
        rbias = sb("rbias", NE)
        alog = sb("alog", 8)
        dtb = sb("dtb", 8)
        rb = sb("rb", T)
        small = sb("small", 64)
        stateB = sb("stateB", 2, 2, 2, HK)
        gw = sb("gw", 2, NT)
        slot = sb("slot", 2, NT, dt=I32)
        table = sb("table", 16, dt=I32)
        slot_tok = sb("slot_tok", NB, dt=I32)
        numi = sb("numi", 24, dt=I32)
        num = sb("num", 24)
        ARENA = 23040
        arena = sb("arena", ARENA)

        def carve(at, *shape):
            n = int(np.prod(shape))
            assert at + n <= ARENA, (at, n)
            v = arena[:, at:at + n]
            if len(shape) > 1:
                names = "abcdef"[:len(shape)]
                v = v.rearrange("p (%s) -> p %s" % (" ".join(names), " ".join(names)),
                                **dict(zip(names, shape)))
            return v

        SQ_AT, WG_AT = 11264, 16820
        sq = carve(SQ_AT, KD, T)
        xrow = carve(0, NT, D)
        xsq = carve(SQ_AT, D)
        c_x = carve(0, 2, PADW)
        c_u = carve(1300, 2, CONVW)
        c_yg = carve(2600, 2, T)
        c_g = carve(3900, 2, 2, 2, T)
        c_a = carve(9100, 4, T)
        c_t = carve(11700, 4, T)
        c_h = carve(14260, 4, T)
        c_wg = carve(WG_AT, 8, P)
        b_f = carve(0, 4, T)
        b_b = carve(2560, 4, T)
        b_k = carve(5120, 4, T)
        b_Z = [carve(7680, 4, T), carve(10240, 4, T)]
        b_at = carve(12800, NT, 8, P)
        b_q = carve(17920, 2, T)
        b_v = carve(19200, NT, 256)
        b_g = carve(20480, NT, 256)
        b_o = carve(21760, NT, 256)
        b_osq = carve(7680, 2 * T)
        z_rows = carve(21760, D)
        a_qk = carve(0, 8, T)
        a_K = carve(5120, NT, 512)
        a_V = carve(7680, NT, 512)
        a_g = carve(10240, NT, 512)
        a_o = carve(12800, NT, 512)
        a_S = carve(15360, 2, 8, P)
        a_X = carve(17408, 8, P)
        a_XT0 = carve(18432, 8, P)
        a_AT = carve(19456, 8, P)
        a_pad = lambda b: carve((17920 if b < 8 else 7680, 10240)[b % 2], PADW)
        a_cv = lambda b: carve((11530, 10886 if b < 8 else 8980)[b % 2], CONVW)
        a_rn = carve(17408, 8, T)
        a_sm = carve(22530, 420)

        def smallcol(at, *shape):
            n = int(np.prod(shape))
            v = a_sm[:, at:at + n]
            if len(shape) > 1:
                v = v.rearrange("p (a b) -> p a b", a=shape[0])
            return v

        a_la = smallcol(0, NT, 8)
        a_z = smallcol(40, NT, 8)
        a_w = smallcol(80, NT, 8)
        a_beta = smallcol(120, NT, 8)
        a_gc = smallcol(160, NT, 8)
        a_beg = smallcol(200, NT, 8)
        s_beta = smallcol(240, NT, 8)
        s_gc = smallcol(280, NT, 8)
        s_beg = smallcol(320, NT, 8)
        a_nea = smallcol(360, 8)
        a_ge = smallcol(368, NT, 8)
        a_rt = smallcol(40, NT, GH)
        hTf = hT[:, :, :].rearrange("p k t -> p (k t)")

        def temp(n):
            return hTf[:, 1024 * n:1024 * (n + 1)].rearrange("p (a b) -> p a b", a=8)

        def spare(n):
            at = (SLAB_N[("gdn", 3)] + (0, 2)[n // 4]) % RING
            return ring[:, at, 1024 * (n % 4):1024 * (n % 4 + 1)].rearrange("p (a b) -> p a b", a=8)

        a_abT = carve(5120, T)
        a_T1, a_U, a_R = temp(0), temp(4), spare(4)
        a_CT = [carve(20480, 8, P), carve(21504, 8, P), spare(5)]
        a_dec, a_qe, a_Kd, a_XT = ([a, b] for a, b in zip([temp(1), temp(2), temp(3), a_XT0],
                                                          [spare(n) for n in range(4)]))
        mixA = hT[:, 0:4, :]
        m_h2 = carve(0, NT, D)
        m_y = m_h2
        m_yB = carve(NT * D, NT, D)
        m_xg = carve(5120, 2, D)
        m_xgT = carve(7168, 2, KD, P)
        m_slab = carve(10752, 3, SLAB)
        m_sg, m_hid, m_hidT = (hTf[:, 1024 * n:1024 * (n + 1)].rearrange("p (a b) -> p a b", a=2) for n in range(3))
        m_dn = hTf[:, 3072:5120].rearrange("p (a b) -> p a b", a=2)
        m_xr = lambda t: xT[:, :, P * t:P * t + P]
        m_gt = [mixBC[:, 0:4, :].rearrange("p a t -> p (a t)")[:, D * g:D * g + D] for g in range(2)]
        m_fw = lmask[:, 0:2, :, :].rearrange("p d l t -> p (d l t)")[:, 0:D]
        m_x2 = carve(10752, NT, D)
        m_sq = carve(15872, D)
        m_out = carve(16896, NT, D)
        m_p = carve(9300, NT, NE)
        m_gate = carve(9400, NT, NE)
        m_rank = carve(9500, NT, NE)
        m_cg = carve(9600, NT, NE)
        m_sel = carve(9700, NT, NE)
        m_t1 = carve(9800, NT, NE)
        m_cmp = carve(9900, MAX_OVER, NE)
        m_c4 = carve(10060, NE, 4)
        m_no = carve(10130, 4, NE)
        m_ab = carve(10200, 2, NT)
        m_idrow = carve(10220, P)
        m_col = carve(10360, 16)
        m_gs = carve(10380, NT, 4)
        m_gr = carve(10400, NT, 4)
        m_lgT = carve(7168, T)
        m_tot, m_run, m_more = (carve(7808 + 80 * n, NE, NT) for n in range(3))
        m_left = carve(10420, 4, 4)
        m_r4 = [carve(8600, 4 * NT, 4, 4), carve(8920, 4 * NT, 4, 4)]
        m_of = carve(10440, 16)

        PLAN = job_plan()
        JOB = {name: (n % 4, n // 4) for n, name in enumerate(PLAN)}
        pair_full = [sem(f"pair_full{i}") for i in range(4)]
        pair_free = [sem(f"pair_free{i}") for i in range(4)]
        block_full = [sem(f"block_full{i}") for i in range(4)]
        block_free = [sem(f"block_free{i}") for i in range(4)]

        def pair(name):
            return JOB[name][0]

        def bank(name):
            return ps[:, pair(name), :]

        def full_after(name):
            return pair_full[pair(name)], JOB[name][1] + 1

        def free_before(name):
            return pair_free[pair(name)], JOB[name][1]

        def free_after(name):
            return pair_free[pair(name)], JOB[name][1] + 1

        s_a_conv = sem("a_conv")
        s_a_ct = sem("a_ct")
        s_a_ct0 = sem("a_ct0")
        s_a_d = sem("a_d")
        s_a_dec = sem("a_dec")
        s_a_eg = sem("a_eg")
        s_a_la = sem("a_la")
        s_a_ln = sem("a_ln")
        s_a_norm = sem("a_norm")
        s_a_oall = sem("a_oall")
        s_a_on = sem("a_on")
        s_a_orn = sem("a_orn")
        s_a_osq = sem("a_osq")
        s_a_oss = sem("a_oss")
        s_a_pad = sem("a_pad")
        s_a_rhs = sem("a_rhs")
        s_a_rn = sem("a_rn")
        s_a_silu = sem("a_silu")
        s_a_sq = sem("a_sq")
        s_a_state = sem("a_state")
        s_a_x0 = sem("a_x0")
        s_a_z = sem("a_z")
        s_b_d = sem("b_d")
        s_b_e = sem("b_e")
        s_b_k = sem("b_k")
        s_b_kd = sem("b_kd")
        s_b_ln = sem("b_ln")
        s_b_m = sem("b_m")
        s_b_oall = sem("b_oall")
        s_b_on = sem("b_on")
        s_b_r = sem("b_r")
        s_b_sq = sem("b_sq")
        s_b_ss = sem("b_ss")
        s_b_state = sem("b_state")
        s_b_z = sem("b_z")
        s_c_a = sem("c_a")
        s_c_done = sem("c_done")
        s_c_fin = sem("c_fin")
        s_c_lam = sem("c_lam")
        s_c_ln = sem("c_ln")
        s_c_mix = sem("c_mix")
        s_c_nc8 = sem("c_nc8")
        s_c_pad = sem("c_pad")
        s_c_sqrt = sem("c_sqrt")
        s_c_y = sem("c_y")
        s_conv_c = sem("conv_c")
        s_cs = sem("cs")
        s_eps = sem("eps")
        s_h = sem("h")
        s_hraw = sem("hraw")
        s_ident = sem("ident")
        s_iota = sem("iota")
        s_num = sem("num")
        s_numi = sem("numi")
        s_z_rows = sem("z_rows")
        s_z_stored = sem("z_stored")
        s_sel = sem("sel")
        s_slot = sem("slot")
        s_table = sem("table")
        s_h2_stored = sem("h2_stored")
        s_scattered = sem("scattered")
        s_idrow = sem("idrow")
        s_xg = [sem(f"xg{i}") for i in range(2)]
        s_m_sg = sem("m_sg")
        s_hid = sem("hid")
        s_ys_stored = [sem(f"ys_stored{i}") for i in range(2)]
        s_y_in = [sem(f"y_in{t}") for t in range(NT)]
        s_yA = sem("yA")
        moe_full = [sem(f"moe_full{i}") for i in range(MSLOTS)]
        s_mod = sem("mod")
        s_r_exp = sem("r_exp")
        s_r_max = sem("r_max")
        s_rb = sem("rb")
        s_r0 = sem("r0")
        s_sb_in = sem("sb_in")
        s_sg_in = sem("sg_in")
        s_small_in = sem("small_in")
        s_sq = sem("sq")
        s_sq_sum = sem("sq_sum")
        s_st_in = sem("st_in")
        s_state_stored = sem("state_stored")
        s_wg_in = sem("wg_in")
        s_wg_zero = sem("wg_zero")
        s_x2 = sem("x2")
        s_x_in = sem("x_in")
        s_y_stored = sem("y_stored")
        s_out = sem("out")
        s_x2rs = sem("x2rs")

        class Chain:

            def __init__(self, eng, name):
                self.eng, self.sem, self.n = eng, sem(name), 0

            def __call__(self, ins):
                ins.then_inc(self.sem, 1)
                self.n += 1

            def sync(self):
                self.eng.wait_ge(self.sem, self.n)

        slab_full = [sem(f"slab_full{i}") for i in range(RING)]
        LAST = {}
        for i in range(12):
            LAST[("ada", i)] = ("adaT", i)
        LAST[("rg", 0)] = ("rgy", 1)
        LAST[("hq", 0)] = ("hi", 1)
        LAST[("hg", 0)] = ("hf", 1)
        LAST[("hf", 0)] = ("hf", 3)
        for i in range(3):
            LAST[("gdn", i)] = ("qkv", 4 * i + 3)
        LAST[("gdn", 3)] = ("gg", NT - 1)
        for i in range(2):
            LAST[("out", i)] = ("out", 4 * i + 3)

        def slab(name, width=512):
            n = SLAB_N[name] % RING
            return ring[:, n, 0:8 * width].rearrange("p (k n) -> p k n", k=8)

        def slab_after(name):
            n = SLAB_N[name]
            return slab_full[n % RING], 16 * (n // RING + 1)

        win = I["w_in"][0].rearrange("(k p) n -> p k n", p=P)

        def slab_source(name):
            kind, i = name
            if kind == "ada":
                return I["ada_w"][0].rearrange("(k p) n -> p k n", p=P)[:, :, 512 * i:512 * i + 512]
            if kind in ("rg", "hq", "hg", "hf", "gdn"):
                at = {"rg": O_RG, "hq": O_HQ, "hg": O_HQ + 512, "hf": O_HQ + 1024, "gdn": 512 * i}[kind]
                return win[:, :, at:at + (256 if kind == "hf" else 512)]
            if kind == "out":
                return I["w_out"][0].rearrange("(k p) n -> p k n", p=P)[:, :, 512 * i:512 * i + 512]

        def expert_slab(b, i):
            n = (3 * b + i) % MSLOTS
            v = ring[:, (len(SLABS) + n) % RING, :] if n < RING else m_slab[:, n - RING, :]
            return v.rearrange("p (k n) -> p k n", k=4 if i == 2 else 8)

        def expert_source(i, e):
            w = I[("moe_w_gate", "moe_w_up", "moe_w_down")[i]][0]
            return w[bass.DynSlice(e, 1)].rearrange("a (k p) n -> p (a k) n", p=P)

        def slab_full_of(b, i):
            m = 3 * b + i
            return moe_full[m % MSLOTS], 16 * (m // MSLOTS + 1)

        def over_blocks(eng, body):
            n = eng.value_load(table[0:1, MAX_OVER:MAX_OVER + 1], min_val=0, max_val=MAX_OVER)
            with ExitStack() as nest:
                for j in range(MAX_OVER):
                    nest.enter_context(eng.If(n > j))
                    body(NE + j)

        h2_dram = nc.dram_tensor("h2_rows", (T, D), F32, kind="Internal").ap()
        tok_dram = nc.dram_tensor("slot_tokens", (NB * P, 1), F32, kind="Internal").ap()
        ys_dram = nc.dram_tensor("slot_outputs", (NB * P, D), F32, kind="Internal").ap()

        def segs(name):
            b = bank(name)
            return ((0, CTX, b[:, 0:CTX], 0), (CTX, T, b[:, 512:1024], 1))

        def wide(v, at, n):
            v = v.unsqueeze(at)
            shape = list(v.shape)
            shape[at] = n
            return v.to_broadcast(shape)

        vb = vecB
        block = ctx.enter_context(nc.Block())

        @block.sync
        def _(sp):
            for n, (name, width) in enumerate(SLABS):
                if n == 1:
                    sp.wait_ge(s_st_in, 16 * 16)
                    sp.dma_start(xrow[:, 0, :], I["x_prompt"][0]).then_inc(s_x_in, 16)
                    sp.dma_start(xrow[:, 1:NT, :], I["x_sample"][0].rearrange("(t p) d -> p t d", p=P)).then_inc(s_x_in, 16)
                if n >= RING:
                    sp.wait_ge(*full_after(LAST[SLABS[n - RING][0]]))
                if n == len(SLABS) - 1:
                    sp.wait_ge(*full_after(("gmix", 0)))
                sp.dma_start(slab(name, width), slab_source(name)).then_inc(slab_full[n % RING], 16)
            for b in range(NE):
                for i in range(3):
                    if b == 0:
                        sp.wait_ge(*full_after(LAST[SLABS[len(SLABS) - RING + i][0]]))
                    elif b == 1 and i == 0:
                        sp.wait_ge(*full_after(("rms", 1)))
                    elif b >= 2:
                        sp.wait_ge(block_full[DN if i == 2 else GU], b - 1)
                    m = (3 * b + i) % MSLOTS
                    sp.dma_start(expert_slab(b, i), expert_source(i, b)).then_inc(moe_full[m], 16)
            sp.wait_ge(s_table, 1)

            def load_over(b):
                e = sp.value_load(table[0:1, b - NE:b - NE + 1], min_val=0, max_val=NE - 1)
                for i in range(3):
                    sp.wait_ge(block_full[DN if i == 2 else GU], b - 1)
                    m = (3 * b + i) % MSLOTS
                    sp.dma_start(expert_slab(b, i), expert_source(i, e)).then_inc(moe_full[m], 16)

            over_blocks(sp, load_over)
            for t in range(NT):
                sp.wait_ge(s_out, t + 1)
                dst = O["y_prompt"][0] if t == 0 else O["y_sample"][0, (t - 1) * P:t * P, :]
                sp.dma_start(dst, m_out[:, t, :]).then_inc(s_y_stored, 16)
            sp.wait_ge(s_y_stored, 16 * NT)
            sp.wait_ge(s_state_stored, 16 * 3)

        @block.tensor
        def _(pe):
            mm = nc.tensor.matmul

            def tr(out, in_, n=P):
                return nc.tensor.transpose(out, in_, ident[0:n, 0:n])

            def project(name, w, cols, rhs=None, h_comes=False):
                rhs = rhs or (lambda k: hT[:, k, :])
                pe.wait_ge(*free_before(name))
                for k in range(KD):
                    if h_comes:
                        pe.wait_ge(s_h, 2 * (k + 1))
                    for a, b, out, g in segs(name):
                        last = mm(out, w[:, k, cols], rhs(k)[:, a:b], start=(k == 0), stop=(k == KD - 1))
                last.then_inc(pair_full[pair(name)], 1)

            pe.wait_ge(s_ident, 1)
            pe.wait_ge(s_st_in, 16 * 16)
            b = bank(("stage", 0))
            tr(b[:, 0:88], stA[0:88, :], 88)
            tr(b[:, 512:592], stB[0:80, :], 80).then_inc(pair_full[pair(("stage", 0))], 1)
            pe.wait_ge(s_cs, 2)

            def modulation(i):
                name = ("ada", i)
                pe.wait_ge(*slab_after(name))
                pe.wait_ge(*free_before(name))
                for k in range(KD):
                    last = mm(bank(name)[0:2, 0:512], cs[:, k, :], slab(name)[:, k, :],
                              start=(k == 0), stop=(k == KD - 1))
                last.then_inc(pair_full[pair(name)], 1)

            def modulation_columns(i):
                name = ("adaT", i)
                pe.wait_ge(*free_after(("ada", i)))
                pe.wait_ge(*free_before(name))
                for c in range(4):
                    last = tr(bank(name)[:, 2 * c:2 * c + 2], slab(("ada", i))[0:2, 0, P * c:P * c + P], 2)
                last.then_inc(pair_full[pair(name)], 1)

            for name in START:
                if name[0] == "rms":
                    pe.wait_ge(s_r0, 1)
                    pe.wait_ge(*free_before(name))
                    for t in range(NT):
                        last = mm(bank(name)[:, P * t:P * t + P], small[:, 24 + t:25 + t].to_broadcast([P, P]), ident[:, :],
                                  start=True, stop=True)
                    last.then_inc(pair_full[pair(name)], 1)
                elif name[0] == "xt":
                    pe.wait_ge(s_x_in, 32)
                    pe.wait_ge(*free_before(name))
                    for k in range(KD):
                        last = tr(bank(name)[:, P * k:P * k + P], xrow[:, name[1], P * k:P * k + P])
                    last.then_inc(pair_full[pair(name)], 1)
                else:
                    (modulation if name[0] == "ada" else modulation_columns)(name[1])

            w = slab(("rg", 0))
            pe.wait_ge(*slab_after(("rg", 0)))
            for b in range(2):
                project(("rgx", b), w, slice(P * b, P * b + P), h_comes=(b == 0))
            for b in range(2):
                project(("rgy", b), w, slice(256 + P * b, 256 + P * b + P))
            w = slab(("hq", 0))
            pe.wait_ge(*slab_after(("hq", 0)))
            for b in range(2):
                project(("hq", b), w, slice(P * b, P * b + P))

            def token_rows(kind, w, col, width, per, tiles=NT):
                for n in range((tiles + per - 1) // per):
                    name = (kind, n)
                    pe.wait_ge(*free_before(name))
                    for t in range(n * per, min(tiles, n * per + per)):
                        out = bank(name)[:, (t - n * per) * width:(t - n * per + 1) * width]
                        for k in range(KD):
                            last = mm(out, hT[:, k, P * t:P * t + P], w[:, k, col:col + width],
                                      start=(k == 0), stop=(k == KD - 1))
                    last.then_inc(pair_full[pair(name)], 1)

            token_rows("hi", w, 256, 256, 4)
            w = slab(("hg", 0))
            pe.wait_ge(*slab_after(("hg", 0)))
            token_rows("hgate", w, 0, 256, 4)
            pe.wait_ge(s_conv_c, 2)
            pe.wait_ge(s_wg_in, 16 * 16)
            for n in range(8):
                name = ("rgg", n)
                pe.wait_ge(*free_before(name))
                for a, b, out, g in segs(name):
                    last = mm(out, c_wg[:, n, :], c_u[:, n % 2, a + 2 * g:b + 2 * g], start=True, stop=True)
                last.then_inc(pair_full[pair(name)], 1)
            for n in range(2):
                project(("hf", n), w, slice(256 + P * n, 256 + P * n + P))
            w = slab(("hf", 0), 256)
            pe.wait_ge(*slab_after(("hf", 0)))
            for n in range(2):
                project(("hf", 2 + n), w, slice(P * n, P * n + P))

            def narrow(kind, w, ready):
                name = (kind, 0)
                pe.wait_ge(*free_before(name))
                for k in range(KD):
                    pe.wait_ge(s_h, ready + 2 * (k + 1))
                    for a, b, out, g in segs(name):
                        last = mm(out[0:16, :], w[:, k, :], hT[:, k, a:b], start=(k == 0), stop=(k == KD - 1))
                last.then_inc(pair_full[pair(name)], 1)

            def narrow_rows(kind, v):
                name = (kind + "T", 0)
                pe.wait_ge(*free_after((kind, 0)))
                pe.wait_ge(*free_before(name))
                for t in range(NT):
                    last = tr(bank(name)[:, 16 * t:16 * t + 16], v[0:16, P * t:P * t + P], 16)
                last.then_inc(pair_full[pair(name)], 1)

            HALVES = [(half, dp) for dp in range(4) for half in range(2)]

            def half(v, h, dp, t):
                return v[64 * h:64 * h + 64, dp, P * t:P * t + P]

            modulation(4)
            modulation(5)
            modulation_columns(4)
            pe.wait_ge(s_b_k, 1)
            for l in range(8):
                if l:
                    pe.wait_ge(s_b_z, l)
                for t in range(NT):
                    name = ("lev", l, t)
                    pe.wait_ge(*free_before(name))
                    for h, dp in HALVES:
                        lhs = half(b_Z[l % 2] if l else b_k, h, dp, t)
                        rhs = half(b_Z[l % 2], h, dp, t) if l else half(b_q, h, dp % 2, t)
                        last = mm(bank(name)[:, 512 * h + P * dp:512 * h + P * dp + P], lhs, rhs, start=True, stop=True)
                    last.then_inc(pair_full[pair(name)], 1)
                if l:
                    modulation_columns(4 + l)
                if l < 6:
                    modulation(6 + l)
            def qkv(b):
                if b % 4 == 0:
                    pe.wait_ge(*slab_after(("gdn", b // 4)))
                project(("qkv", b), slab(("gdn", b // 4)), slice(P * (b % 4), P * (b % 4) + P))

            qkv(0)
            pe.wait_ge(s_b_kd, 1)
            for t in range(NT):
                name = ("kdt", t)
                pe.wait_ge(*free_before(name))
                for dp in range(4):
                    last = tr(bank(name)[:, P * dp:P * dp + P], b_Z[1][:, dp, P * t:P * t + P])
                last.then_inc(pair_full[pair(name)], 1)
            b_kdr = b_k.rearrange("p a t -> p (a t)").rearrange("p (t c n) -> p t c n", t=NT, c=4)

            for s in range(NT):
                seg = min(s, 1)
                name = ("ho", s)
                if s == 0:
                    pe.wait_ge(*free_after(("kdt", NT - 1)))
                    pe.wait_ge(*free_after(("lev", 7, NT - 1)))
                if s == 0:
                    pe.wait_ge(s_b_state, 1)
                else:
                    pe.wait_ge(*free_after(("hs", s - 1)))
                pe.wait_ge(*free_before(name))
                for h, dp in HALVES:
                    t = (FWD, BWD)[dp // 2][s]
                    out = bank(name)[:, 512 * h + 64 * dp:512 * h + 64 * dp + 64]
                    v = P * (dp % 2) + 64 * h
                    mm(out, half(b_Z[0], h, dp, t), stateB[64 * h:64 * h + 64, seg, dp // 2, dp % 2, :],
                       start=True, stop=False)
                    last = mm(out, b_at[:, t, 4 * h + dp, :], b_v[:, t, v:v + 64], start=False, stop=True)
                last.then_inc(pair_full[pair(name)], 1)
                name = ("hs", s)
                pe.wait_ge(*free_before(name))
                for dp in range(4):
                    t = (FWD, BWD)[dp // 2][s]
                    last = mm(bank(name)[:, P * dp:P * dp + P], b_kdr[:, t, dp, :],
                              b_v[:, t, P * (dp % 2):P * (dp % 2) + P], start=True, stop=True)
                last.then_inc(pair_full[pair(name)], 1)
                qkv(s + 1)
            qkv(6)
            qkv(7)
            pe.wait_ge(s_b_on, 1)
            for t in range(NT):
                name = ("hmix", t)
                pe.wait_ge(*free_before(name))
                for p in range(2):
                    last = tr(bank(name)[:, P * p:P * p + P], b_o[:, t, P * p:P * p + P])
                last.then_inc(pair_full[pair(name)], 1)
            pe.wait_ge(s_small_in, 16 * 5)
            narrow("ab", wab, 0)
            for b in range(8, 12):
                qkv(b)
                if b == 8:
                    narrow_rows("ab", a_abT)
                for n in (2 * b - 16, 2 * b - 15):
                    name = ("ss", n)
                    pe.wait_ge(s_a_sq, n + 1)
                    pe.wait_ge(*free_before(name))
                    for a, e, out, g in segs(name):
                        last = mm(out, ones[:, :], a_K.rearrange("p a b -> p (a b)")
                                  .rearrange("p (n t) -> p n t", t=T)[:, n % 4, a:e], start=True, stop=True)
                    last.then_inc(pair_full[pair(name)], 1)
            pe.wait_ge(*slab_after(("gdn", 3)))
            token_rows("gg", slab(("gdn", 3)), 0, 512, 1)
            name = ("gcol", 0)
            pe.wait_ge(s_a_la, 1)
            pe.wait_ge(*free_before(name))
            for t in range(NT):
                for d in range(2):
                    c = 8 * t + 4 * d
                    last = mm(bank(name)[:, c:c + 4], tri[:, d, :], a_la[:, t, 4 * d:4 * d + 4],
                              start=True, stop=True)
            last.then_inc(pair_full[pair(name)], 1)
            pe.wait_ge(s_a_norm, 1)
            pe.wait_ge(s_a_silu, 24)
            for t in range(NT):
                name = ("rows", t)
                pe.wait_ge(*free_before(name))
                vT = a_o.rearrange("p a b -> p (a b)").rearrange("p (n t) -> p n t", t=T)
                for h in range(GH):
                    tr(bank(name)[:, P * h:P * h + P], a_qk[:, 4 + h, P * t:P * t + P])
                for h in range(GH):
                    last = tr(bank(name)[:, 512 + P * h:512 + P * h + P], vT[:, h, P * t:P * t + P])
                last.then_inc(pair_full[pair(name)], 1)
            pe.wait_ge(s_a_norm, 2)

            def eight(name, lhs, rhs):
                pe.wait_ge(*free_before(name))
                for dh in range(8):
                    last = mm(bank(name)[:, P * dh:P * dh + P], lhs(dh), rhs(dh), start=True, stop=True)
                last.then_inc(pair_full[pair(name)], 1)

            def cut(v, base):
                return lambda s: lambda dh: v[:, base + dh % 4, P * (FWD, BWD)[dh // 4][s]:P * (FWD, BWD)[dh // 4][s] + P]

            def four(name, g, lhs, rhs):
                pe.wait_ge(*free_before(name))
                for h in range(GH):
                    last = mm(bank(name)[:, P * h:P * h + P], lhs(4 * g + h), rhs(4 * g + h), start=True, stop=True)
                last.then_inc(pair_full[pair(name)], 1)

            def level(s, l):
                ct, XT = a_CT[(7 * s + l) % 3], a_XT[s % 2]
                if l == 0:
                    pe.wait_ge(s_a_ct0, s + 1)
                else:
                    pe.wait_ge(s_a_ct, 6 * s + l)
                for g in range(2):
                    if l == 0:
                        name = ("x0", s, g)
                        pe.wait_ge(*free_before(name))
                        for h in range(GH):
                            last = tr(bank(name)[:, P * h:P * h + P], ct[:, 4 * g + h, :])
                        last.then_inc(pair_full[pair(name)], 1)
                        continue
                    pe.wait_ge(*free_after(("x0", s, g) if l == 1 else ("dx", s, l - 1, g)))
                    four(("t1", s, l, g), g, lambda dh: ct[:, dh, :], lambda dh: a_X[:, dh, :])
                for g in range(2 if l else 0):
                    pe.wait_ge(*free_after(("t1", s, l, g)))
                    if l == 1:
                        pe.wait_ge(s_a_x0, 2 * s + g + 1)
                    else:
                        pe.wait_ge(*free_after(("dxt", s, l - 1, g)))
                    if l < 6:
                        four(("dx", s, l, g), g, lambda dh: XT[:, dh, :], lambda dh: a_T1[:, dh, :])
                    four(("dxt", s, l, g), g, lambda dh: a_T1[:, dh, :], lambda dh: XT[:, dh, :])

            kT, qT = cut(a_qk, 4), cut(a_qk, 0)
            for stage in gdn_order():
                kind, s = stage[:2]
                seg = min(s, 1)
                tile = lambda dh: (FWD, BWD)[dh // 4][s]
                name = (kind, s)
                if kind == "level":
                    level(s, stage[2])
                elif kind == "gb":
                    eight(name, lambda dh: a_la[:, tile(dh), dh:dh + 1].to_broadcast([P, P]), lambda dh: tri[:, dh // 4, :])
                elif kind == "bb":
                    eight(name, lambda dh: a_beta[:, tile(dh), dh:dh + 1].to_broadcast([P, P]), lambda dh: ident[:, :])
                elif kind == "kk":
                    eight(name, kT(s), kT(s))
                elif kind == "kq":
                    eight(name, kT(s), qT(s))
                elif kind == "ks":
                    if s == 0:
                        pe.wait_ge(s_a_state, 1)
                    else:
                        pe.wait_ge(*free_after(("ds", s - 1)))
                        pe.wait_ge(s_sg_in, 16)
                    eight(name, kT(s), lambda dh: a_S[:, seg, dh, :])
                elif kind == "u":
                    pe.wait_ge(s_a_rhs, s + 1)
                    for g in range(2):
                        pe.wait_ge(*free_after(("dxt", s, 6, g)))
                    eight(name, lambda dh: a_XT[s % 2][:, dh, :], lambda dh: a_R[:, dh, :])
                elif kind == "ds":
                    eight(name, lambda dh: a_Kd[s % 2][:, dh, :], lambda dh: a_U[:, dh, :])
                elif kind == "o":
                    pe.wait_ge(*free_after(("kq", s)))
                    pe.wait_ge(*free_after(("u", s)))
                    pe.wait_ge(*free_before(name))
                    for dh in range(8):
                        out = bank(name)[:, P * dh:P * dh + P]
                        mm(out, a_qe[s % 2][:, dh, :], a_S[:, seg, dh, :], start=True, stop=False)
                        last = mm(out, a_dec[s % 2][:, dh, :], a_U[:, dh, :], start=False, stop=True)
                    last.then_inc(pair_full[pair(name)], 1)
            pe.wait_ge(s_a_on, 3)
            for t in range(NT):
                name = ("gmix", t)
                pe.wait_ge(*free_before(name))
                for h in range(GH):
                    last = tr(bank(name)[:, P * h:P * h + P], a_o[:, t, P * h:P * h + P])
                last.then_inc(pair_full[pair(name)], 1)
            for t in range(NT):
                pe.wait_ge(*free_after(("gmix", t)))
                pe.wait_ge(*free_after(("hmix", t)))
            pe.wait_ge(s_c_mix, 4)
            for n in OUT_ORDER:
                if n % 4 == 0:
                    pe.wait_ge(*slab_after(("out", n // 4)))
                project(("out", n), slab(("out", n // 4)), slice(P * (n % 4), P * (n % 4) + P),
                        rhs=lambda k: mixA[:, k, :] if k < 4 else mixBC[:, k - 4, :])
            name = ("rms", 1)
            pe.wait_ge(*free_before(name))
            pe.wait_ge(s_sq_sum, 1)
            for a, b, out, g in segs(name):
                last = mm(out, ones[:, :], sq[:, OUT_ORDER[0], a:b], start=True, stop=True)
            last.then_inc(pair_full[pair(name)], 1)
            narrow("router", rw, 16)
            narrow_rows("router", m_lgT)
            def h2_rows(t):
                name = ("h2row", t)
                pe.wait_ge(*free_before(name))
                for k in range(KD):
                    last = tr(bank(name)[:, P * k:P * k + P], hT[:, k, P * t:P * t + P])
                last.then_inc(pair_full[pair(name)], 1)

            for t in range(3):
                h2_rows(t)
            name = ("pos", 0)
            sel = m_sel.rearrange("p t e -> p (t e)")
            pe.wait_ge(s_sel, 1)
            pe.wait_ge(*free_before(name))
            mm(bank(name)[:, 0:NE * NT], tri[:, 0, :], sel, start=True, stop=True)
            mm(bank(name)[:, 512:512 + NE * NT], ones[:, :], sel, start=True, stop=True).then_inc(pair_full[pair(name)], 1)
            for t in range(3, NT):
                h2_rows(t)
            for i in range(3):
                name = ("rowvec", i)
                pe.wait_ge(*free_before(name))
                for k in range(KD):
                    v = modT[:, 40 + k, i:i + 1] if i < 2 else vecA[:, 64 + k:65 + k]
                    last = mm(bank(name)[:, P * k:P * k + P], v.to_broadcast([P, P]), ident[:, :], start=True, stop=True)
                last.then_inc(pair_full[pair(name)], 1)
            for t in range(NT):
                name = ("xrow", t)
                pe.wait_ge(*free_before(name))
                for k in range(KD):
                    last = tr(bank(name)[:, P * k:P * k + P], xT[:, k, P * t:P * t + P])
                last.then_inc(pair_full[pair(name)], 1)
            name = ("slots", 0)
            pe.wait_ge(s_idrow, 16)
            pe.wait_ge(*free_before(name))
            tr(bank(name)[:, 0:NB], m_idrow[0:NB, :], NB).then_inc(pair_full[pair(name)], 1)

            def gathered(b):
                pe.wait_ge(s_xg[b % 2], 16 * (b // 2 + 1))
                if b:
                    pe.wait_ge(block_free[XG], b)
                for k in range(KD):
                    last = tr(ps[:, XG, P * k:P * k + P], m_xg[:, b % 2, P * k:P * k + P])
                last.then_inc(block_full[XG], 1)

            def gate_up(b):
                pe.wait_ge(block_free[XG], b + 1)
                if b:
                    pe.wait_ge(block_free[GU], b)
                for i in range(2):
                    pe.wait_ge(*slab_full_of(b, i))
                    for k in range(KD):
                        last = mm(ps[:, GU, 512 * i:512 * i + 512], m_xgT[:, b % 2, k, :], expert_slab(b, i)[:, k, :],
                                  start=(k == 0), stop=(k == KD - 1))
                last.then_inc(block_full[GU], 1)

            def hidden(b):
                pe.wait_ge(block_free[GU], b + 1)
                if b:
                    pe.wait_ge(block_free[HD], b)
                for f in range(4):
                    last = tr(ps[:, HD, P * f:P * f + P], m_hid[:, b % 2, P * f:P * f + P])
                last.then_inc(block_full[HD], 1)

            def down(b):
                pe.wait_ge(block_free[HD], b + 1)
                if b:
                    pe.wait_ge(block_free[DN], b)
                pe.wait_ge(*slab_full_of(b, 2))
                for n in range(2):
                    for f in range(4):
                        last = mm(ps[:, DN, 512 * n:512 * n + 512], m_hidT[:, b % 2, P * f:P * f + P],
                                  expert_slab(b, 2)[:, f, 512 * n:512 * n + 512], start=(f == 0), stop=(f == 3))
                last.then_inc(block_full[DN], 1)

            for name in PLAN[-4:]:
                pe.wait_ge(*free_after(name))
            gathered(0)
            for b in range(NE):
                gate_up(b)
                if b:
                    hidden(b - 1)
                if b + 1 < NE:
                    gathered(b + 1)
                if b:
                    down(b - 1)
            hidden(NE - 1)
            down(NE - 1)

            def over(b):
                gathered(b)
                gate_up(b)
                hidden(b)
                down(b)

            pe.wait_ge(s_table, 1)
            over_blocks(pe, over)

        @block.scalar
        def _(act):
            A = nc.scalar.activation
            ch = Chain(act, "act_chain")
            dma = act.dma_start

            def rowsof(v, n):
                return v.rearrange("(n p) -> n p", p=P)

            st = s_st_in
            dma(stA[0:48, :], rowsof(I["ada_b"][0], 48)).then_inc(st, 16)
            dma(stA[48:56, :], rowsof(I["norm1_w"][0], 8)).then_inc(st, 16)
            dma(stA[56:64, :], rowsof(I["norm2_w"][0], 8)).then_inc(st, 16)
            dma(stA[64:72, :], rowsof(I["final_norm_w"], 8)).then_inc(st, 16)
            dma(stA[72:80, :], rowsof(I["c"][0], 8)).then_inc(st, 16)
            dma(stA[80:88, :], rowsof(I["c_ctx"], 8)).then_inc(st, 16)
            dma(stB[0:48, :], I["gdn_conv_w"][0].rearrange("j (n p) -> (j n) p", p=P)).then_inc(st, 16)
            dma(stB[48:56, :], I["rg_conv_w"][0].rearrange("j (n p) -> (j n) p", p=P)).then_inc(st, 16)
            dma(stB[56:58, :], rowsof(I["rg_conv_b"][0], 2)).then_inc(st, 16)
            dma(stB[58:66, :], I["rg_gate_b"][0].rearrange("d g (n p) -> (d g n) p", p=P)).then_inc(st, 16)
            dma(stB[66:70, :], I["rg_lambda"][0].rearrange("d (n p) -> (d n) p", p=P)).then_inc(st, 16)
            dma(stB[70:74, :], I["state_rglru"][0, 0].rearrange("d (n p) -> (d n) p", p=P)).then_inc(st, 16)
            dma(stB[74:78, :], I["hg_lb_logits"][0].rearrange("d (n p) -> (d n) p", p=P)).then_inc(st, 16)
            dma(stB[78:79, :], I["gdn_norm_w"]).then_inc(st, 16)
            for i in range(2):
                dma(stB[79:80, 64 * i:64 * i + 64], I["hg_norm_w"]).then_inc(st, 16)
            act.wait_ge(*free_after(("stage", 0)))
            A(cs[:, :, 1], vecA[:, 72:80], ACT.Silu).then_inc(s_cs, 1)
            A(cs[:, :, 0], vecA[:, 80:88], ACT.Silu).then_inc(s_cs, 1)

            def modulation(i):
                act.wait_ge(*full_after(("ada", i)))
                A(slab(("ada", i))[0:2, 0, :], bank(("ada", i))[0:2, 0:512], ACT.Copy).then_inc(pair_free[pair(("ada", i))], 1)

            def modulate(n, scl, shift):
                for k in range(KD):
                    act.wait_ge(s_hraw, KD * n + k + 1)
                    for a, b, g in SEG:
                        A(hT[:, k, a:b], hT[:, k, a:b], ACT.Identity, scale=scl[:, k, g:g + 1],
                               bias=modT[:, shift + k, g:g + 1]).then_inc(s_h, 1)

            act.wait_ge(s_eps, 1)

            def silu_out(b):
                act.wait_ge(s_a_conv, b + 1)
                if b == 8:
                    act.wait_ge(*full_after(("ho", NT - 1)))
                vT = a_o.rearrange("p a b -> p (a b)").rearrange("p (n t) -> p n t", t=T)
                dst = a_qk[:, b, :] if b < 8 else vT[:, b - 8, :]
                for a, e, g in SEG:
                    A(dst[:, a:e], a_cv(b)[:, a + 2 * g:e + 2 * g], ACT.Silu).then_inc(s_a_silu, 1)

            def narrow(kind, v):
                name = (kind, 0)
                act.wait_ge(*full_after(name))
                for a, b, out, g in segs(name):
                    ins = A(v[0:16, a:b], out[0:16, :], ACT.Copy)
                    ch(ins) if g == 0 else ins.then_inc(pair_free[pair(name)], 1)

            def qkv(b):
                name = ("qkv", b)
                act.wait_ge(*full_after(name))
                if b >= 2:
                    act.wait_ge(s_a_conv, b - 1)
                for a, e, out, g in segs(name):
                    ins = A(a_pad(b)[:, 2 + a + 2 * g:2 + e + 2 * g], out, ACT.Copy)
                    ch(ins) if g == 0 else ins.then_inc(pair_free[pair(name)], 1)

            modulation(0)
            act.wait_ge(s_x_in, 32)
            act.wait_ge(s_eps, 1)
            r = small[:, 24:24 + NT]
            for t in range(NT):
                ch(A(xsq, xrow[:, t, :], ACT.Square, accum_out=small[:, 24 + t:25 + t]))
                ch.sync()
            ch(A(r, r, ACT.Ln, scale=1.0 / D, bias=small[:, 0:1]))
            ch.sync()
            A(r, r, ACT.Exp, scale=-0.5).then_inc(s_r0, 1)
            modulation(1)
            modulation(2)
            modulation(3)
            act.wait_ge(s_mod, 1)
            modulate(0, scl1, 0)
            sm = s_small_in
            dma(wab[:, :, :], win[:, :, O_AB:O_AB + 16]).then_inc(sm, 16)
            dma(rw[:, :, :], I["router_w"].rearrange("(k p) e -> p k e", p=P)).then_inc(sm, 16)
            dma(rbias[:, :], I["router_b"].partition_broadcast(P)).then_inc(sm, 16)
            dma(alog[:, :], I["gdn_a_log"][0].rearrange("d h -> (d h)").partition_broadcast(P)).then_inc(sm, 16)
            dma(dtb[:, :], I["gdn_dt_bias"][0].rearrange("d h -> (d h)").partition_broadcast(P)).then_inc(sm, 16)
            dma(stateB[:, 1, :, :, :].rearrange("p d q v -> p (d q) v"),
                I["state_hgrn"][0, 0].rearrange("d (q e) k v -> (e k) (d q) v", e=2)).then_inc(s_sb_in, 16)
            act.wait_ge(s_wg_zero, 1)
            for n in range(8):
                for i in range(2):
                    dma(c_wg[64 * i:64 * i + 64, n, 64 * i:64 * i + 64],
                        I["rg_gate_w"][0, n // 4, n // 2 % 2, 2 * (n % 2) + i]).then_inc(s_wg_in, 16)
            act.wait_ge(s_c_pad, 1)
            act.wait_ge(s_h, 16)
            for b in range(2):
                name = ("rgx", b)
                act.wait_ge(*full_after(name))
                lo, hi = bank(name)[:, 0:CTX], bank(name)[:, 512:1024]
                ch(A(c_x[:, b, 2:2 + CTX], lo, ACT.Copy))
                A(c_x[:, b, 4 + CTX:4 + T].rearrange("p (c r) -> p r c", r=ROWS),
                       hi.rearrange("p (r c) -> p r c", c=GRID_W), ACT.Copy).then_inc(pair_free[pair(name)], 1)
            for b in range(2):
                name = ("rgy", b)
                act.wait_ge(*full_after(name))
                lo, hi = bank(name)[:, 0:CTX], bank(name)[:, 512:1024]
                ch(A(c_yg[:, b, 0:CTX], lo, ACT.Gelu_apprx_tanh))
                A(c_yg[:, b, CTX:T].rearrange("p (c r) -> p r c", r=ROWS),
                       hi.rearrange("p (r c) -> p r c", c=GRID_W), ACT.Gelu_apprx_tanh).then_inc(pair_free[pair(name)], 1)
            for b in range(2):
                name = ("hq", b)
                act.wait_ge(*full_after(name))
                for a, e, out, g in segs(name):
                    ins = A(b_q[:, b, a:e], out, ACT.Copy)
                    ch(ins) if g == 0 else ins.then_inc(pair_free[pair(name)], 1)
            for n in range(2):
                name = ("hi", n)
                act.wait_ge(*full_after(name))
                A(b_v[:, 4 * n:min(NT, 4 * n + 4), :], bank(name)[:, 0:256 * (4 if n == 0 else 1)]
                       .rearrange("p (t c) -> p t c", c=256), ACT.Copy).then_inc(pair_free[pair(name)], 1)
            act.wait_ge(s_c_lam, 1)
            ch(A(small[:, 8:12], small[:, 4:8], ACT.Exp))
            ch.sync()
            ch(A(small[:, 44:48], small[:, 44:48], ACT.Exp))
            A(small[:, 8:12], small[:, 8:12], ACT.Ln, bias=small[:, 1:2]).then_inc(s_c_ln, 1)
            for n in range(2):
                name = ("hgate", n)
                act.wait_ge(*full_after(name))
                A(b_g[:, 4 * n:min(NT, 4 * n + 4), :], bank(name)[:, 0:256 * (4 if n == 0 else 1)]
                       .rearrange("p (t c) -> p t c", c=256), ACT.Silu).then_inc(pair_free[pair(name)], 1)
            act.wait_ge(s_z_stored, 32)
            for n in range(8):
                name = ("rgg", n)
                act.wait_ge(*full_after(name))
                for a, b, out, g in segs(name):
                    ins = A(c_g[:, n // 4, n // 2 % 2, n % 2, a:b], out, ACT.Sigmoid, bias=vb[:, 58 + n:59 + n])
                    ch(ins) if g == 0 else ins.then_inc(pair_free[pair(name)], 1)
            for n in (0, 1, 4, 5):
                act.wait_ge(*free_after(("rgg", n)))
            ch.sync()
            act.wait_ge(s_c_nc8, 1)
            for db in range(4):
                A(c_a[:, db, :], c_g[:, db // 2, 0, db % 2, :], ACT.Exp, scale=small[:, 12 + db:13 + db]).then_inc(s_c_a, 1)
            for db in range(4):
                A(c_t[:, db, :], c_g[:, db // 2, 0, db % 2, :], ACT.Tanh, scale=small[:, 12 + db:13 + db]).then_inc(s_c_a, 1)
            act.wait_ge(s_c_y, 1)
            A(c_t[:, :, :], c_h[:, :, :], ACT.Sqrt).then_inc(s_c_sqrt, 1)
            act.wait_ge(s_c_fin, 1)
            dma(O["new_rg"][0, 0].rearrange("d (n p) -> p (d n)", p=P), small[:, 20:24],
                allow_slow_non_contiguous=True).then_inc(s_state_stored, 16)
            act.wait_ge(s_c_done, 1)
            for n in range(4):
                name = ("hf", n)
                act.wait_ge(*full_after(name))
                for a, e, out, g in segs(name):
                    ch(A(b_f[:, n, a:e], out, ACT.Sigmoid))
                    ins = A(b_k[:, n, a:e], out, ACT.Sigmoid, scale=-1.0)
                    ch(ins) if g == 0 else ins.then_inc(pair_free[pair(name)], 1)
            act.wait_ge(s_b_m, 1)
            ch(A(b_f[:, :, :], b_f[:, :, :], ACT.Ln))
            A(b_Z[0][:, :, :], b_Z[0][:, :, :], ACT.Ln, scale=1.0 / LNSPLIT).then_inc(s_b_ln, 1)
            modulation(4)
            modulation(5)
            for l in range(7):
                act.wait_ge(s_b_d, l + 1)
                A(b_f[:, :, :], b_f[:, :, :], ACT.Exp).then_inc(s_b_e, 1)
                if l:
                    modulation(5 + l)
            act.wait_ge(s_b_z, 7)
            A(b_f[:, :, :], b_b[:, :, :], ACT.Exp).then_inc(s_b_e, 1)
            act.wait_ge(s_b_d, 8)
            A(b_Z[1][:, :, :], b_Z[1][:, :, :], ACT.Exp).then_inc(s_b_e, 1)
            act.wait_ge(s_a_pad, 1)
            qkv(0)
            act.wait_ge(s_b_kd, 1)
            b_kdr = b_k.rearrange("p a t -> p (a t)").rearrange("p (t c) -> p t c", t=NT)
            for t in range(NT):
                act.wait_ge(*full_after(("kdt", t)))
                A(b_kdr[:, t, :], bank(("kdt", t))[:, 0:512], ACT.Copy).then_inc(pair_free[pair(("kdt", t))], 1)
            act.wait_ge(s_a_pad, 2)
            for b in range(1, 6):
                qkv(b)
                silu_out(b - 1)
                if b == 2:
                    act.wait_ge(*free_after(("hs", 0)))
                    dma(O["new_hgrn"][0, 0].rearrange("d (q e) k v -> (e k) (d q) v", e=2),
                        stateB[:, 0, :, :, :].rearrange("p d q v -> p (d q) v")).then_inc(s_state_stored, 16)
            act.wait_ge(s_b_oall, 1)
            A(b_osq, b_o[:, :, :].rearrange("p a t -> p (a t)"), ACT.Square).then_inc(s_b_sq, 1)
            silu_out(5)
            act.wait_ge(s_b_ss, 1)
            A(small[:, 24:44], small[:, 24:44], ACT.Sqrt, scale=1.0 / HK, bias=small[:, 0:1]).then_inc(s_b_r, 1)
            qkv(6)
            qkv(7)
            silu_out(6)
            for t in range(NT):
                act.wait_ge(*full_after(("hmix", t)))
                A(mixBC[:, 0:2, P * t:P * t + P], bank(("hmix", t))[:, 0:256].rearrange("p (a t) -> p a t", a=2),
                       ACT.Copy, scale=vb[:, 79:80]).then_inc(pair_free[pair(("hmix", t))], 1)
            sqs = a_K.rearrange("p a b -> p (a b)").rearrange("p (n t) -> p n t", t=T)
            narrow("ab", a_abT)
            act.wait_ge(s_a_pad, 3)
            for b in range(8, 12):
                qkv(b)
                silu_out(b - 1)
                if b == 8:
                    act.wait_ge(*full_after(("abT", 0)))
                    act.wait_ge(s_a_silu, 16)
                for n in (2 * b - 16, 2 * b - 15):
                    if n >= 4:
                        act.wait_ge(*full_after(("ss", n - 4)))
                    A(sqs[:, n % 4, :], a_qk[:, n, :], ACT.Square).then_inc(s_a_sq, 1)
            silu_out(11)
            for n in range(8):
                act.wait_ge(*free_after(("ss", n)))
            for h in (slice(4, 8), slice(0, 4)):
                ch(A(a_rn[:, h, :], a_rn[:, h, :], ACT.Ln, bias=small[:, 0:1]))
            ch.sync()
            for h in (slice(4, 8), slice(0, 4)):
                A(a_rn[:, h, :], a_rn[:, h, :], ACT.Exp, scale=-0.5).then_inc(s_a_rn, 1)
            act.wait_ge(s_a_z, 1)
            ch(A(a_w[:, :, :], a_w[:, :, :], ACT.Exp))
            ch(A(a_nea[:, :], alog[:, :], ACT.Exp))
            ch.sync()
            A(a_w[:, :, :], a_w[:, :, :], ACT.Ln, bias=small[:, 1:2]).then_inc(s_a_ln, 1)
            ch(A(a_beta[:, :, :], a_beta[:, :, :], ACT.Sigmoid))
            for t in range(NT):
                act.wait_ge(*full_after(("gg", t)))
                A(a_g[:, t, :], bank(("gg", t))[:, 0:512], ACT.Silu).then_inc(pair_free[pair(("gg", t))], 1)
            act.wait_ge(*free_after(("gcol", 0)))
            ch.sync()
            A(a_beg[:, :, :], a_gc[:, :, :], ACT.Exp).then_inc(s_a_eg, 1)
            for t in range(0, NT, 2):
                act.wait_ge(*full_after(("rows", t)))
                ch(A(a_K[:, t, :], bank(("rows", t))[:, 0:512], ACT.Copy))
                A(a_V[:, t, :], bank(("rows", t))[:, 512:1024], ACT.Copy).then_inc(pair_free[pair(("rows", t))], 1)
            def squares(part):
                act.wait_ge(s_a_oall, part + 1)
                for at in O_PARTS[part]:
                    A(a_K[:, at, :], a_o[:, at, :], ACT.Square).then_inc(s_a_osq, 1)

            def norms(part):
                act.wait_ge(s_a_oss, part + 1)
                for at in O_PARTS[part]:
                    A(a_rt[:, at, :], a_rt[:, at, :], ACT.Sqrt, scale=1.0 / P, bias=small[:, 0:1]).then_inc(s_a_orn, 1)

            half_heads = lambda v: v.rearrange("p (a b) -> p a b", a=GH)
            for stage in gdn_order():
                kind, s = stage[:2]
                name = (kind, s)
                if kind == "exp":
                    name = ("gb", s)
                    if s >= 2:
                        act.wait_ge(*full_after(("o", s - 2)))
                    act.wait_ge(*full_after(name))
                    act.wait_ge(s_a_d, s + 1)
                    A(a_dec[s % 2][:, :, :], a_dec[s % 2][:, :, :], ACT.Exp).then_inc(s_a_dec, 1)
                    A(a_qe[s % 2][:, :, :], bank(name).rearrange("p (a b) -> p a b", a=8), ACT.Exp).then_inc(pair_free[pair(name)], 1)
                elif kind == "level" and stage[2]:
                    for g in range(2):
                        name = ("t1", s, stage[2], g)
                        act.wait_ge(*full_after(name))
                        if stage[2] == 1 and s:
                            act.wait_ge(*full_after(("dxt", s - 1, 6, g)))
                        A(a_T1[:, 4 * g:4 * g + 4, :], half_heads(bank(name)[:, 0:512]), ACT.Copy).then_inc(pair_free[pair(name)], 1)
                elif kind == "u":
                    act.wait_ge(*full_after(name))
                    if s:
                        act.wait_ge(*full_after(("ds", s - 1)))
                    A(a_U[:, :, :], bank(name).rearrange("p (a b) -> p a b", a=8), ACT.Copy).then_inc(pair_free[pair(name)], 1)
                elif kind == "ds" and s == NT - 2:
                    squares(0)
                elif kind == "ds" and s == 0:
                    act.wait_ge(*free_after(name))
                    dma(O["new_gdn"][0, 0].rearrange("d h k v -> k (d h) v"), a_S[:, 0, :, :]).then_inc(s_state_stored, 16)
            norms(0)
            squares(1)
            norms(1)
            for t in range(NT):
                act.wait_ge(*full_after(("gmix", t)))
                A(mixA[:, :, P * t:P * t + P], bank(("gmix", t))[:, 0:512].rearrange("p (a t) -> p a t", a=4),
                       ACT.Copy, scale=vb[:, 78:79]).then_inc(pair_free[pair(("gmix", t))], 1)

            def x1_ready(n):
                if n == 0:
                    act.wait_ge(s_state_stored, 48)
                act.wait_ge(*free_after(("out", OUT_ORDER[n])))

            for n, k in enumerate(OUT_ORDER):
                x1_ready(n)
                A(sq[:, k, :], xT[:, k, :], ACT.Square).then_inc(s_sq, 1)
            name = ("rms", 1)
            act.wait_ge(*full_after(name))
            for a, b, out, g in segs(name):
                ins = A(rb[:, a:b], out, ACT.Ln, scale=1.0 / D, bias=small[:, 0:1])
                ch(ins) if g == 0 else ins.then_inc(pair_free[pair(name)], 1)
            act.wait_ge(*free_after(name))
            ch.sync()
            A(rb[:, :], rb[:, :], ACT.Exp, scale=-0.5).then_inc(s_rb, 1)
            modulate(1, scl2, 24)
            narrow("router", m_lgT)
            act.wait_ge(s_r_max, 1)
            A(m_p[:, :, :], m_p[:, :, :], ACT.Exp).then_inc(s_r_exp, 1)
            for t in range(NT):
                name = ("h2row", t)
                act.wait_ge(*full_after(name))
                A(m_h2[:, t, :], bank(name), ACT.Copy).then_inc(pair_free[pair(name)], 1)
                act.wait_ge(*free_after(name))
                dma(h2_dram[P * t:P * t + P, :], m_h2[:, t, :]).then_inc(s_h2_stored, 16)
            for i in range(3):
                name = ("rowvec", i)
                act.wait_ge(*full_after(name))
                A(m_gt[i] if i < 2 else m_fw, bank(name), ACT.Copy).then_inc(pair_free[pair(name)], 1)
            for t in range(NT):
                name = ("xrow", t)
                act.wait_ge(*full_after(name))
                A(m_xr(t), bank(name).rearrange("p (a b) -> p a b", a=KD), ACT.Copy).then_inc(pair_free[pair(name)], 1)
            act.wait_ge(s_z_stored, 32)

            def silu_gate(b):
                act.wait_ge(block_full[GU], b + 1)
                if b >= 2:
                    act.wait_ge(s_hid, b - 1)
                A(m_sg[:, b % 2, :], ps[:, GU, 0:512], ACT.Silu).then_inc(s_m_sg, 1)

            def block_out(b):
                act.wait_ge(block_full[HD], b + 1)
                if b >= 2:
                    act.wait_ge(block_full[DN], b - 1)
                A(m_hidT[:, b % 2, :], ps[:, HD, 0:512], ACT.Copy).then_inc(block_free[HD], 1)
                act.wait_ge(block_full[DN], b + 1)
                if b >= 2:
                    act.wait_ge(s_ys_stored[b % 2], 16 * (b // 2))
                A(m_dn[:, b % 2, :], ps[:, DN, :], ACT.Copy).then_inc(block_free[DN], 1)
                act.wait_ge(block_free[DN], b + 1)
                dma(ys_dram[P * b:P * b + P, :], m_dn[:, b % 2, :]).then_inc(s_ys_stored[b % 2], 16)

            for b in range(NE):
                silu_gate(b)
                if b:
                    block_out(b - 1)
            block_out(NE - 1)

            def over(b):
                silu_gate(b)
                block_out(b)

            act.wait_ge(s_table, 1)
            over_blocks(act, over)
            act.wait_ge(s_h2_stored, 16 * NT)

            def final_rms(t):
                act.wait_ge(s_x2, t + 1)
                r = small[:, 24 + t:25 + t]
                ch(A(m_sq, m_x2[:, t, :], ACT.Square, accum_out=r))
                ch.sync()
                A(r, r, ACT.Sqrt, scale=1.0 / D, bias=small[:, 0:1]).then_inc(s_x2rs, 1)

            for t in range(NT):
                act.wait_ge(s_y_in[t], 32)
                A(m_y[:, t, :], m_y[:, t, :], ACT.Copy, scale=gw[:, 0, t:t + 1]).then_inc(s_yA, 1)
                if t:
                    final_rms(t - 1)
            final_rms(NT - 1)

        @block.gpsimd
        def _(pool):
            ch = Chain(pool, "pool_chain")
            ch(nc.gpsimd.memset(ident[:, :], 0.0))
            ch.sync()
            nc.gpsimd.affine_select(out=ident[:, :], in_=ident[:, :], compare_op=ALU.not_equal, fill=1.0,
                                         base=0, pattern=[[-1, P]], channel_multiplier=1).then_inc(s_ident, 1)
            ch(nc.gpsimd.memset(ones[:, :], 1.0))
            ch.sync()
            for d, sign in ((0, 1), (1, -1)):
                ch(nc.gpsimd.affine_select(out=tri[:, d, :], in_=ones[:, :], compare_op=ALU.is_ge, fill=0.0,
                                           base=0, pattern=[[sign, P]], channel_multiplier=-sign))
            ch(nc.gpsimd.iota(vi[:, 0, :], pattern=[[1, P]], base=0, channel_multiplier=0))
            nc.gpsimd.iota(vi[:, 1, :], pattern=[[0, P]], base=0, channel_multiplier=1).then_inc(s_iota, 1)
            nc.gpsimd.memset(c_wg[:, :, :], 0.0).then_inc(s_wg_zero, 1)
            ch(nc.gpsimd.iota(numi[:, 0:16], pattern=[[1, 16]], base=0, channel_multiplier=0))
            ch.sync()
            nc.gpsimd.iota(numi[:, 16:16 + NT], pattern=[[P, NT]], base=0, channel_multiplier=1).then_inc(s_numi, 1)
            nc.gpsimd.memset(z_rows[:, :], 0.0).then_inc(s_z_rows, 1)
            pool.wait_ge(*full_after(("xt", NT - 1)))
            pool.wait_ge(s_r0, 1)
            nc.gpsimd.memset(c_x[:, :, :], 0.0).then_inc(s_c_pad, 1)
            pool.wait_ge(s_z_rows, 1)
            pool.wait_ge(*full_after(("ada", 3)))
            pool.dma_start(tok_dram.rearrange("(b p) o -> b (p o)", p=P), z_rows[0:NB, 0:P]).then_inc(s_z_stored, 16)
            pool.dma_start(ys_dram[NE * P:NB * P, :].rearrange("(b p) d -> p b d", p=P),
                           wide(z_rows[:, :], 1, MAX_OVER)).then_inc(s_z_stored, 16)
            pool.wait_ge(s_b_kd, 1)
            nc.gpsimd.memset(a_pad(0), 0.0).then_inc(s_a_pad, 1)
            pool.wait_ge(*full_after(("kdt", NT - 1)))
            nc.gpsimd.memset(a_pad(1), 0.0).then_inc(s_a_pad, 1)
            pool.wait_ge(*full_after(("hmix", NT - 1)))
            nc.gpsimd.memset(a_pad(8), 0.0).then_inc(s_a_pad, 1)
            nc.gpsimd.memset(a_S[:, 0, :, :], 0.0).then_inc(s_a_state, 1)
            pool.dma_start(a_S[:, 1, :, :], I["state_gdn"][0, 0].rearrange("d h k v -> k (d h) v")).then_inc(s_sg_in, 16)
            for s in range(NT):
                pool.wait_ge(*free_after(("kk", s)))
                for l in range(1, 7):
                    n = 7 * s + l
                    if l == 3:
                        for g in range(2):
                            pool.wait_ge(*full_after(("x0", s, g)))
                        pool.wait_ge(s_a_x0, 2 * s + 2)
                    elif n >= 3:
                        pool.wait_ge(*full_after(("t1", (n - 3) // 7, (n - 3) % 7, 1)))
                    for d in range(2):
                        ins = nc.gpsimd.tensor_tensor(out=a_CT[n % 3][:, 4 * d:4 * d + 4, :], in0=a_AT[:, 4 * d:4 * d + 4, :],
                                                      in1=wide(lmask[:, d, l, :], 1, 4), op=MULT)
                        ch(ins) if d == 0 else ins.then_inc(s_a_ct, 1)
            scatter = bass.IndirectOffsetOnAxis
            pool.wait_ge(s_z_stored, 32)
            pool.wait_ge(s_slot, 1)
            for t in range(NT):
                for c in range(2):
                    pool.indirect_dma_start(out=tok_dram, out_offset=scatter(ap=slot[:, c, t:t + 1], axis=0),
                                            in_=num[:, 16 + t:17 + t], in_offset=None).then_inc(s_scattered, 16)
            pool.wait_ge(s_scattered, 16 * 2 * NT)
            pool.dma_start(m_idrow[0:NB, :], tok_dram.rearrange("(b p) o -> b (p o)", p=P)).then_inc(s_idrow, 16)
            pool.wait_ge(s_h2_stored, 16 * NT)
            pool.wait_ge(*free_after(("slots", 0)))

            def gather(b):
                if b >= 2:
                    pool.wait_ge(block_full[XG], b - 1)
                pool.indirect_dma_start(out=m_xg[:, b % 2, :], out_offset=None, in_=h2_dram,
                                        in_offset=scatter(ap=slot_tok[:, b:b + 1], axis=0)).then_inc(s_xg[b % 2], 16)

            def stored(b):
                pool.wait_ge(s_ys_stored[b % 2], 16 * (b // 2 + 1))

            for b in range(NE):
                gather(b)
            pool.wait_ge(s_table, 1)
            over_blocks(pool, gather)
            stored(NE - 2)
            stored(NE - 1)
            over_blocks(pool, stored)
            for t in range(NT):
                for c, dst in ((0, m_y), (1, m_yB)):
                    pool.indirect_dma_start(out=dst[:, t, :], out_offset=None, in_=ys_dram,
                                            in_offset=scatter(ap=slot[:, c, t:t + 1], axis=0)).then_inc(s_y_in[t], 16)

        @block.vector
        def _(dve):
            ch = Chain(dve, "dve_chain")
            V = nc.vector
            TT, TS, STT = V.tensor_tensor, V.tensor_scalar, V.scalar_tensor_tensor

            def link(ins):
                ch(ins)
                ch.sync()

            ch(V.memset(small[:, 0:1], EPS))
            V.memset(small[:, 1:2], 1.0).then_inc(s_eps, 1)
            ch(V.memset(stateB[:, 0, :, :, :], 0.0))
            dve.wait_ge(s_numi, 1)
            V.tensor_copy(num[:, 0:16 + NT], numi[:, 0:16 + NT]).then_inc(s_num, 1)
            dve.wait_ge(*full_after(("stage", 0)))
            ch(V.tensor_copy(vecA[:, :], bank(("stage", 0))[:, 0:88]))
            V.tensor_copy(vecB[:, :], bank(("stage", 0))[:, 512:592]).then_inc(pair_free[pair(("stage", 0))], 1)
            def modulation(i):
                name = ("adaT", i)
                dve.wait_ge(*full_after(name))
                TT(out=modT[:, 4 * i:4 * i + 4, :], in0=bank(name)[:, 0:8].rearrange("p (a b) -> p a b", b=2),
                   in1=wide(vecA[:, 4 * i:4 * i + 4], 2, 2), op=ADD).then_inc(pair_free[pair(name)], 1)

            def scale_x(n):
                if n == 0:
                    name = ("rms", 0)
                    dve.wait_ge(*full_after(name))
                    V.tensor_copy(rb[:, :], bank(name)[:, 0:T]).then_inc(pair_free[pair(name)], 1)
                    dve.wait_ge(*free_after(name))
                else:
                    dve.wait_ge(s_rb, 1)
                for k in range(KD):
                    TT(out=hT[:, k, :], in0=xT[:, k, :], in1=rb[:, :], op=MULT).then_inc(s_hraw, 1)

            dve.wait_ge(*free_after(("stage", 0)))
            for name in START:
                if name[0] == "xt":
                    dve.wait_ge(*full_after(name))
                    V.tensor_copy(xT[:, :, P * name[1]:P * name[1] + P],
                                  bank(name).rearrange("p (a b) -> p a b", a=KD)).then_inc(pair_free[pair(name)], 1)
                elif name[0] == "adaT":
                    modulation(name[1])
                elif name[0] == "rms":
                    for t in range(NT):
                        dve.wait_ge(*free_after(("xt", t)))
                    scale_x(0)
            ch(STT(out=small[:, 4:8], in0=vb[:, 66:70], scalar=-1.0, in1=vb[:, 66:70], op0=MULT, op1=MIN))
            ch(TT(out=small[:, 44:48], in0=vb[:, 74:78], in1=vb[:, 74:78], op=SUB))
            TS(small[:, 16:20], vb[:, 66:70], -1.0, 0.0, MULT, MAX).then_inc(s_c_lam, 1)
            for i in range(4):
                dve.wait_ge(*free_after(("adaT", i)))
            STT(out=scl1[:, :, :], in0=modT[:, 8:16, :], scalar=1.0, in1=wide(vecA[:, 48:56], 2, 2), op0=ADD, op1=MULT).then_inc(s_mod, 1)

            for b in range(2):
                dve.wait_ge(*free_after(("rgx", b)))
                link(TS(c_u[:, b, :], c_x[:, b, 0:CONVW], vb[:, 48 + b:49 + b], vb[:, 56 + b:57 + b], MULT, ADD))
                for j in range(1, 4):
                    ins = STT(out=c_u[:, b, :], in0=c_x[:, b, j:j + CONVW], scalar=vb[:, 48 + 2 * j + b:49 + 2 * j + b],
                              in1=c_u[:, b, :], op0=MULT, op1=ADD)
                    link(ins) if j < 3 else ins.then_inc(s_conv_c, 1)
            dve.wait_ge(s_iota, 1)
            link(TT(out=vi[:, 0, :], in0=vi[:, 0, :], in1=vi[:, 1, :], op=ALU.bitwise_xor))
            link(V.tensor_copy(vf[:, 0, :], vi[:, 0, :]))
            for l, w in enumerate(LEVELS):
                link(TS(vf[:, 1, :], vf[:, 0, :], float(w), None, ALU.is_ge))
                link(STT(out=vf[:, 1, :], in0=vf[:, 0, :], scalar=float(2 * w), in1=vf[:, 1, :], op0=ALU.is_lt, op1=MULT))
                for d in range(2):
                    link(TT(out=lmask[:, d, l, :], in0=vf[:, 1, :], in1=tri[:, d, :], op=MULT))
            dve.wait_ge(s_conv_c, 2)
            dve.wait_ge(s_c_ln, 1)
            link(TT(out=small[:, 8:12], in0=small[:, 8:12], in1=small[:, 16:20], op=ADD))
            TS(small[:, 12:16], small[:, 8:12], -RG_C, None, MULT).then_inc(s_c_nc8, 1)
            link(V.reciprocal(small[:, 48:52], small[:, 44:48]))
            link(TT(out=small[:, 48:52], in0=small[:, 48:52], in1=small[:, 44:48], op=MULT))
            link(TT(out=small[:, 48:52], in0=small[:, 48:52], in1=small[:, 48:52], op=SUB))
            link(TS(small[:, 52:56], small[:, 48:52], -1.0, 1.0, MULT, ADD))
            dve.wait_ge(s_c_a, 8)
            link(TT(out=c_h[:, :, :], in0=c_a[:, :, :], in1=c_a[:, :, :], op=MULT))
            link(STT(out=c_h[:, :, :], in0=c_h[:, :, :], scalar=1.0, in1=c_t[:, :, :], op0=ADD, op1=MULT))
            TS(c_h[:, :, :], c_h[:, :, :], -1.0, 0.0, MULT, MAX).then_inc(s_c_y, 1)
            for d in range(2):
                for a, e, g in SEG:
                    ch(TT(out=c_g[:, d, 1, :, a:e], in0=c_g[:, d, 1, :, a:e], in1=c_u[:, :, a + 2 * g:e + 2 * g], op=MULT))
            ch.sync()
            dve.wait_ge(s_c_sqrt, 1)
            for d in range(2):
                ch(TT(out=c_t[:, 2 * d:2 * d + 2, :], in0=c_t[:, 2 * d:2 * d + 2, :], in1=c_g[:, d, 1, :, :], op=MULT))
            ch.sync()
            for db in range(4):
                for a, e, g in SEG:
                    way = slice(None, None, -1) if db // 2 else slice(None)
                    ch(V.tensor_tensor_scan(c_h[:, db, a:e][:, way], c_a[:, db, a:e][:, way], c_t[:, db, a:e][:, way],
                                            vb[:, 70 + db:71 + db] if g else 0.0, MULT, ADD))
            ch.sync()
            ch(V.tensor_copy(small[:, 20:22], c_h[:, 0:2, CTX - 1]))
            V.tensor_copy(small[:, 22:24], c_h[:, 2:4, 0]).then_inc(s_c_fin, 1)
            ch.sync()
            dve.wait_ge(s_c_fin, 1)
            link(TT(out=c_h[:, 0:2, :], in0=c_h[:, 0:2, :], in1=c_h[:, 2:4, :], op=ADD))
            for b in range(2):
                TT(out=mixBC[:, 2 + b, 0:CTX], in0=c_h[:, b, 0:CTX], in1=c_yg[:, b, 0:CTX], op=MULT).then_inc(s_c_mix, 1)
                ins = TT(out=mixBC[:, 2 + b, CTX:T].rearrange("p (r c) -> p c r", c=GRID_W),
                         in0=c_h[:, b, CTX:T].rearrange("p (c r) -> p c r", r=ROWS),
                         in1=c_yg[:, b, CTX:T].rearrange("p (c r) -> p c r", r=ROWS), op=MULT)
                ins.then_inc(s_c_mix, 1)
            dve.wait_ge(s_c_mix, 4)
            dve.wait_ge(s_z_stored, 32)
            V.memset(b_o[:, :, :], 0.0).then_inc(s_c_done, 1)
            dve.wait_ge(*free_after(("hf", 3)))
            for dp in range(4):
                ch(TS(b_f[:, dp, :], b_f[:, dp, :], small[:, 52 + dp:53 + dp], small[:, 48 + dp:49 + dp], MULT, ADD))
                ins = TS(b_k[:, dp, :], b_k[:, dp, :], small[:, 52 + dp:53 + dp], None, MULT)
                ch(ins) if dp < 3 else ins.then_inc(s_b_k, 1)
            dve.wait_ge(s_b_k, 1)
            ch.sync()
            link(TS(b_Z[0][:, :, :], b_f[:, :, :], F_MIN, LNSPLIT, MAX, MIN))
            TS(b_f[:, :, :], b_f[:, :, :], LNSPLIT, None, MAX).then_inc(s_b_m, 1)
            dve.wait_ge(s_b_ln, 1)
            link(TT(out=b_f[:, :, :], in0=b_f[:, :, :], in1=b_Z[0][:, :, :], op=ADD))
            for dp in range(4):
                way = slice(None, None, -1) if dp // 2 else slice(None)
                for t in range(NT):
                    ch(V.tensor_tensor_scan(b_b[:, dp, P * t:P * t + P][:, way], ones[:, :],
                                            b_f[:, dp, P * t:P * t + P][:, way], 0.0, MULT, ADD))
            ch.sync()

            def blocks(v, d, w):
                v = v[:, 2 * d:2 * d + 2, :] if v.shape[1] == 4 else v
                return v.rearrange("p a t -> p (a t)").rearrange("p (n w) -> p n w", w=w)

            def level_out(L):
                if L == 0:
                    modulation(4)
                for t in range(NT):
                    name = ("lev", L, t)
                    dve.wait_ge(*full_after(name))
                    src = bank(name).rearrange("p (e d q i) -> p e d q i", e=2, d=2, q=2)
                    dst = b_at[:, t, :, :].rearrange("p (e d q) i -> p e d q i", e=2, d=2)
                    if L == 0:
                        TT(out=b_at[:, t, :, :], in0=bank(name).rearrange("p (a i) -> p a i", a=8),
                                in1=wide(ident[:, :], 1, 8), op=MULT).then_inc(pair_free[pair(name)], 1)
                    else:
                        dve.wait_ge(*free_after(("lev", L - 1, t)))
                        msk = wide(lmask[:, :, L - 1, :].bitcast(I32), 2, 2)
                        ch(V.copy_predicated(dst[:, 0], msk, src[:, 0]))
                        V.copy_predicated(dst[:, 1], msk, src[:, 1]).then_inc(pair_free[pair(name)], 1)
                if L:
                    modulation(4 + L)

            for l, s in enumerate(LEVELS):
                w, n = 2 * s, 2 * T // (2 * s)
                L = l + 1
                for d in range(2):
                    b, E = blocks(b_b, d, w), blocks(b_f, d, w)
                    mid = b[:, :, s - 1:s] if d == 0 else b[:, :, s:s + 1]
                    mid = mid.to_broadcast([P, n, s])
                    lo, hi = b[:, :, 0:s], b[:, :, s:w]
                    ch(TT(out=E[:, :, 0:s], in0=mid if d == 0 else lo, in1=lo if d == 0 else mid, op=SUB))
                    ins = TT(out=E[:, :, s:w], in0=hi if d == 0 else mid, in1=mid if d == 0 else hi, op=SUB)
                    ch(ins) if d == 0 else ins.then_inc(s_b_d, 1)
                if l:
                    level_out(l - 1)
                dve.wait_ge(s_b_e, L)
                if L >= 3:
                    dve.wait_ge(*full_after(("lev", L - 2, NT - 1)))
                for d in range(2):
                    E, Z, q, k = (blocks(v, d, w) for v in (b_f, b_Z[L % 2], b_q, b_k))
                    left, right = (k, q) if d == 0 else (q, k)
                    ch(TT(out=Z[:, :, 0:s], in0=left[:, :, 0:s], in1=E[:, :, 0:s], op=MULT))
                    ins = TT(out=Z[:, :, s:w], in0=right[:, :, s:w], in1=E[:, :, s:w], op=MULT)
                    ch(ins) if d == 0 else ins.then_inc(s_b_z, 1)
                ch.sync()
                dve.wait_ge(s_b_z, L)
            level_out(6)
            level_out(7)
            for i in range(8, 12):
                dve.wait_ge(*free_after(("adaT", i)))
            ch(STT(out=scl2[:, :, :], in0=modT[:, 32:40, :], scalar=1.0, in1=wide(vecA[:, 56:64], 2, 2), op0=ADD, op1=MULT))
            dve.wait_ge(s_b_e, 8)
            for d in range(2):
                ch(TT(out=b_Z[0][:, 2 * d:2 * d + 2, :], in0=b_q[:, :, :], in1=b_f[:, 2 * d:2 * d + 2, :], op=MULT))
            ends = b_f.rearrange("p q (t c) -> p t q c", c=P)
            ch(V.tensor_copy(b_end[:, :, 0:2], ends[:, :, 0:2, P - 1]))
            ch(V.tensor_copy(b_end[:, 0:1, 2:4], ends[:, 0:1, 2:4, 0]))
            ch(V.tensor_copy(b_end[:, 1:NT, 2:4], ends[:, 1:NT, 2:4, 0][:, ::-1]))
            for d in range(2):
                b, Z = blocks(b_b, d, P), blocks(b_Z[1], d, P)
                end = (b[:, :, P - 1:P] if d == 0 else b[:, :, 0:1]).to_broadcast([P, 2 * NT, P])
                ins = TT(out=Z, in0=end, in1=b, op=SUB)
                ch(ins) if d == 0 else ins.then_inc(s_b_d, 1)
            ch.sync()
            dve.wait_ge(s_b_e, 9)
            TT(out=b_Z[1][:, :, :], in0=b_Z[1][:, :, :], in1=b_k[:, :, :], op=MULT).then_inc(s_b_kd, 1)
            dve.wait_ge(s_sb_in, 16)
            V.memset(small[:, 57:58], 0.0).then_inc(s_b_state, 1)
            ch.sync()

            def conv(b):
                dve.wait_ge(*free_after(("qkv", b)))
                if b >= 2:
                    dve.wait_ge(s_a_silu, 2 * (b - 1))
                cv = a_cv(b)
                link(TS(cv, a_pad(b)[:, 0:CONVW], vb[:, b:b + 1], None, MULT))
                for j in range(1, 4):
                    ins = STT(out=cv, in0=a_pad(b)[:, j:j + CONVW], scalar=vb[:, 12 * j + b:12 * j + b + 1],
                              in1=cv, op0=MULT, op1=ADD)
                    link(ins) if j < 3 else ins.then_inc(s_a_conv, 1)

            for s in range(NT):
                name = ("ho", s)
                dve.wait_ge(*full_after(name))
                for d in range(2):
                    o = b_o[:, (FWD, BWD)[d][s], :].rearrange("p (q e v) -> p e q v", q=2, e=2)
                    src = bank(name).rearrange("p (e x) -> p e x", e=2)[:, :, P * d:P * d + P]
                    ins = TT(out=o, in0=src.rearrange("p e (q v) -> p e q v", q=2), in1=o, op=ADD)
                    if d == 0:
                        link(ins)
                    else:
                        ins.then_inc(pair_free[pair(name)], 1)
                name = ("hs", s)
                dve.wait_ge(*full_after(name))
                S = stateB[:, min(s, 1), :, :, :].rearrange("p d q v -> p (d q) v")
                link(TT(out=S, in0=S, in1=wide(b_end[:, s, :], 2, HK), op=MULT))
                src = bank(name)[:, 0:512].rearrange("p (c v) -> p c v", c=4)
                ch(TT(out=S[0:64], in0=src[0:64, :, 0:64], in1=S[0:64], op=ADD))
                TT(out=S[64:128], in0=src[64:128, :, 64:128], in1=S[64:128], op=ADD).then_inc(pair_free[pair(name)], 1)
                dve.wait_ge(*free_after(name))
                dve.wait_ge(*free_after(("ho", s)))
                ch.sync()
                if s < NT - 1:
                    conv(s)
            V.memset(small[:, 58:59], 0.0).then_inc(s_b_oall, 1)
            conv(4)
            dve.wait_ge(s_b_sq, 1)
            V.tensor_reduce(small[:, 24:44], b_osq
                                 .rearrange("p (n v) -> p n v", v=HK), AX.X, ADD).then_inc(s_b_ss, 1)
            conv(5)
            dve.wait_ge(s_b_r, 1)
            link(V.reciprocal(small[:, 24:44], small[:, 24:44]))
            o = b_o.rearrange("p t c -> p (t c)").rearrange("p (n v) -> p n v", v=HK)
            link(TT(out=o, in0=o, in1=wide(small[:, 24:44], 2, HK), op=MULT))
            TT(out=b_o[:, :, :], in0=b_o[:, :, :], in1=b_g[:, :, :], op=MULT).then_inc(s_b_on, 1)
            for b in range(6, 8):
                conv(b)
            for b in range(8, 12):
                conv(b)
                if b == 8:
                    name = ("abT", 0)
                    dve.wait_ge(*full_after(name))
                    dve.wait_ge(s_small_in, 16 * 5)
                    ab = bank(name)[:, 0:16 * NT].rearrange("p (t c) -> p t c", c=16)
                    ch(TT(out=a_z[:, :, :], in0=ab[:, :, 0:8], in1=wide(dtb[:, :], 1, NT), op=ADD))
                    V.tensor_copy(a_beta[:, :, :], ab[:, :, 8:16]).then_inc(pair_free[pair(name)], 1)
                    dve.wait_ge(*free_after(name))
                    ch.sync()
                    link(STT(out=a_w[:, :, :], in0=a_z[:, :, :], scalar=-1.0, in1=a_z[:, :, :], op0=MULT, op1=MIN))
                    TS(a_z[:, :, :], a_z[:, :, :], 0.0, None, MAX).then_inc(s_a_z, 1)
                for n in (2 * b - 16, 2 * b - 15):
                    name = ("ss", n)
                    dve.wait_ge(*full_after(name))
                    if n == 0:
                        dve.wait_ge(s_a_silu, 16)
                    for a, e, out, g in segs(name):
                        ins = V.tensor_copy(a_rn[:, n, a:e], out)
                        ch(ins) if g == 0 else ins.then_inc(pair_free[pair(name)], 1)
            dve.wait_ge(s_a_rn, 1)
            TT(out=a_qk[:, 4:8, :], in0=a_qk[:, 4:8, :], in1=a_rn[:, 4:8, :], op=MULT).then_inc(s_a_norm, 1)
            dve.wait_ge(s_a_ln, 1)
            dve.wait_ge(s_a_z, 1)
            link(TT(out=a_w[:, :, :], in0=a_w[:, :, :], in1=a_z[:, :, :], op=ADD))
            STT(out=a_la[:, :, :], in0=a_w[:, :, :], scalar=-1.0, in1=wide(a_nea[:, :], 1, NT), op0=MULT, op1=MULT).then_inc(s_a_la, 1)
            dve.wait_ge(s_a_rn, 2)
            STT(out=a_qk[:, 0:4, :], in0=a_qk[:, 0:4, :], scalar=float(P) ** -0.5, in1=a_rn[:, 0:4, :], op0=MULT, op1=MULT).then_inc(s_a_norm, 1)
            name = ("gcol", 0)
            dve.wait_ge(*full_after(name))
            V.tensor_copy(a_gc[:, :, :], bank(name)[:, 0:8 * NT].rearrange("p (t c) -> p t c", c=8)).then_inc(pair_free[pair(name)], 1)
            for t in range(1, NT, 2):
                name = ("rows", t)
                dve.wait_ge(*full_after(name))
                ch(V.tensor_copy(a_K[:, t, :], bank(name)[:, 0:512]))
                V.tensor_copy(a_V[:, t, :], bank(name)[:, 512:1024]).then_inc(pair_free[pair(name)], 1)
            dve.wait_ge(s_a_eg, 1)
            link(TT(out=a_beg[:, :, :], in0=a_beg[:, :, :], in1=a_beta[:, :, :], op=MULT))
            for dst, src in ((s_beta, a_beta), (s_gc, a_gc), (s_beg, a_beg)):
                ch(V.tensor_copy(dst[:, :, 0:4], src[:, :, 0:4]))
                ch(V.tensor_copy(dst[:, 0:1, 4:8], src[:, 0:1, 4:8]))
                ch(V.tensor_copy(dst[:, 1:NT, 4:8], src[:, 1:NT, 4:8][:, ::-1]))
            ch.sync()
            dve.wait_ge(*free_after(("rows", NT - 1)))
            ch(V.memset(a_o[:, :, :], 0.0))
            eight = lambda v: v.rearrange("p (a b) -> p a b", a=8)
            fours_of = lambda v: v.rearrange("p (a b) -> p a b", a=GH)

            def decays(s):
                name = ("gb", s)
                dec = a_dec[s % 2]
                dve.wait_ge(*full_after(name))
                if s >= 2:
                    dve.wait_ge(*full_after(("ds", s - 2)))
                link(TT(out=dec, in0=eight(bank(name)), in1=wide(s_gc[:, s, :], 2, P), op=SUB))
                TS(dec, dec, 0.0, None, MIN).then_inc(s_a_d, 1)

            def decayed(s, tile):
                name = ("gb", s)
                dec, qe, Kd = a_dec[s % 2], a_qe[s % 2], a_Kd[s % 2]
                dve.wait_ge(s_a_dec, s + 1)
                dve.wait_ge(*free_after(name))
                for d in range(2):
                    last = P - 1 if d == 0 else 0
                    h = slice(4 * d, 4 * d + 4)
                    ch(TT(out=Kd[:, h, :], in0=a_K[:, tile(d), :].rearrange("p (h c) -> p h c", h=4),
                          in1=dec[:, h, last:last + 1].to_broadcast([P, 4, P]), op=MULT))
                    ch(V.tensor_copy(a_ge[:, s, h], qe[:, h, last]))
                ch.sync()
                for d in range(2):
                    h = slice(4 * d, 4 * d + 4)
                    ch(TT(out=qe[:, h, :], in0=qe[:, h, :], in1=a_qk[:, 0:4, P * tile(d):P * tile(d) + P], op=MULT))
                    ch(TT(out=dec[:, h, :], in0=dec[:, h, :], in1=wide(tri[:, d, :], 1, 4), op=MULT))
                ch.sync()

            def start(s, g):
                h = slice(4 * g, 4 * g + 4)
                if s >= 2 and g == 0:
                    dve.wait_ge(*full_after(("u", s - 2)))
                TT(out=a_XT[s % 2][:, h, :], in0=wide(ident[:, :], 1, 4), in1=a_CT[7 * s % 3][:, h, :], op=SUB).then_inc(s_a_x0, 1)
                name = ("x0", s, g)
                dve.wait_ge(*full_after(name))
                if s:
                    dve.wait_ge(*full_after(("t1", s - 1, 6, g)))
                TT(out=a_X[:, h, :], in0=wide(ident[:, :], 1, 4), in1=fours_of(bank(name)[:, 0:512]), op=SUB).then_inc(pair_free[pair(name)], 1)

            def level(s, l, g):
                h = slice(4 * g, 4 * g + 4)
                if l < 6:
                    name = ("dx", s, l, g)
                    dve.wait_ge(*full_after(name))
                    dve.wait_ge(*free_after(("dx", s, l - 1, g) if l > 1 else ("x0", s, g)))
                    TT(out=a_X[:, h, :], in0=a_X[:, h, :], in1=fours_of(bank(name)[:, 0:512]), op=SUB).then_inc(pair_free[pair(name)], 1)
                name = ("dxt", s, l, g)
                dve.wait_ge(*full_after(name))
                if l > 1:
                    dve.wait_ge(*free_after(("dxt", s, l - 1, g)))
                else:
                    dve.wait_ge(s_a_x0, 2 * s + g + 1)
                XT = a_XT[s % 2][:, h, :]
                TT(out=XT, in0=XT, in1=fours_of(bank(name)[:, 0:512]), op=SUB).then_inc(pair_free[pair(name)], 1)

            def o_sums(part):
                dve.wait_ge(s_a_osq, (2, 3)[part])
                for n, at in enumerate(O_PARTS[part]):
                    ins = V.tensor_reduce(a_rt[:, at, :], a_K[:, at, :].rearrange("p t (h v) -> p t h v", h=4), AX.X, ADD)
                    ch(ins) if n + 1 < len(O_PARTS[part]) else ins.then_inc(s_a_oss, 1)

            def o_scale(part):
                dve.wait_ge(s_a_orn, (2, 3)[part])
                for at in O_PARTS[part]:
                    r = a_rt[:, at, :]
                    o = a_o[:, at, :]
                    heads = o.rearrange("p t (h v) -> p t h v", h=4)
                    link(V.reciprocal(r, r))
                    link(TT(out=heads, in0=heads, in1=wide(r, 3, P), op=MULT))
                    TT(out=o, in0=o, in1=a_g[:, at, :], op=MULT).then_inc(s_a_on, 1)

            for stage in gdn_order():
                kind, s = stage[:2]
                name = (kind, s)
                tile = lambda d, s=s: (FWD, BWD)[d][s]
                if kind == "gb":
                    decays(s)
                elif kind == "exp":
                    decayed(s, tile)
                elif kind == "bb":
                    dve.wait_ge(*full_after(name))
                    if s:
                        dve.wait_ge(s_a_ct, 6 * s)
                        dve.wait_ge(s_a_ct0, s)
                    TT(out=a_AT[:, :, :], in0=eight(bank(name)), in1=a_dec[s % 2], op=MULT).then_inc(pair_free[pair(name)], 1)
                elif kind == "kk":
                    dve.wait_ge(*full_after(name))
                    dve.wait_ge(*free_after(("bb", s)))
                    TT(out=a_AT[:, :, :], in0=eight(bank(name)), in1=a_AT[:, :, :], op=MULT).then_inc(pair_free[pair(name)], 1)
                    dve.wait_ge(*free_after(name))
                    if s:
                        dve.wait_ge(*full_after(("t1", s - 1, 4, 1)))
                    for d in range(2):
                        ins = TT(out=a_CT[7 * s % 3][:, 4 * d:4 * d + 4, :], in0=a_AT[:, 4 * d:4 * d + 4, :],
                                 in1=wide(lmask[:, d, 0, :], 1, 4), op=MULT)
                        ch(ins) if d == 0 else ins.then_inc(s_a_ct0, 1)
                elif kind == "kq":
                    dve.wait_ge(*full_after(name))
                    TT(out=a_dec[s % 2], in0=eight(bank(name)), in1=a_dec[s % 2], op=MULT).then_inc(pair_free[pair(name)], 1)
                elif kind == "level":
                    l = stage[2]
                    if l == 0:
                        dve.wait_ge(s_a_ct0, s + 1)
                        ch.sync()
                    for g in range(2):
                        level(s, l, g) if l else start(s, g)
                elif kind == "ks":
                    for d in range(2):
                        h = slice(4 * d, 4 * d + 4)
                        if s and d == 0:
                            dve.wait_ge(*full_after(("ds", s - 1)))
                        ch(TT(out=a_R[:, h, :], in0=a_V[:, tile(d), :].rearrange("p (h c) -> p h c", h=4),
                              in1=wide(s_beta[:, s, h], 2, P), op=MULT))
                    dve.wait_ge(*full_after(name))
                    TT(out=a_U[:, :, :], in0=eight(bank(name)), in1=wide(s_beg[:, s, :], 2, P), op=MULT).then_inc(pair_free[pair(name)], 1)
                    ch.sync()
                    dve.wait_ge(*free_after(name))
                    TT(out=a_R[:, :, :], in0=a_R[:, :, :], in1=a_U[:, :, :], op=SUB).then_inc(s_a_rhs, 1)
                    if s == NT - 1:
                        o_sums(0)
                elif kind == "o":
                    dve.wait_ge(*full_after(name))
                    for d in range(2):
                        o = a_o[:, tile(d), :]
                        ins = TT(out=o, in0=bank(name)[:, 512 * d:512 * d + 512], in1=o, op=ADD)
                        if d == 0:
                            link(ins)
                        else:
                            ins.then_inc(pair_free[pair(name)], 1)
                elif kind == "ds":
                    dve.wait_ge(*full_after(name))
                    S = a_S[:, min(s, 1), :, :]
                    if s == 1:
                        dve.wait_ge(s_sg_in, 16)
                    if s == 0:
                        dve.wait_ge(s_a_state, 1)
                    link(TT(out=S, in0=S, in1=wide(a_ge[:, s, :], 2, P), op=MULT))
                    TT(out=S, in0=S, in1=eight(bank(name)), op=ADD).then_inc(pair_free[pair(name)], 1)
                    dve.wait_ge(*free_after(name))
                    dve.wait_ge(*free_after(("o", s)))
                    if s == NT - 2:
                        V.memset(small[:, 59:60], 0.0).then_inc(s_a_oall, 1)
            dve.wait_ge(*free_after(("o", NT - 1)))
            V.memset(small[:, 59:60], 0.0).then_inc(s_a_oall, 1)
            o_sums(1)
            o_scale(0)
            o_scale(1)
            def add_squares(i):
                total = sq[:, OUT_ORDER[0], :]
                dve.wait_ge(s_sq, i + 1)
                ins = TT(out=total, in0=total, in1=sq[:, OUT_ORDER[i], :], op=ADD)
                link(ins) if i < KD - 1 else ins.then_inc(s_sq_sum, 1)

            for i, n in enumerate(OUT_ORDER):
                name = ("out", n)
                dve.wait_ge(*full_after(name))
                for a, e, out, g in segs(name):
                    ins = STT(out=xT[:, n, a:e], in0=out, scalar=modT[:, 16 + n, g:g + 1], in1=xT[:, n, a:e],
                              op0=MULT, op1=ADD)
                    ch(ins) if g == 0 else ins.then_inc(pair_free[pair(name)], 1)
                if i >= 2:
                    add_squares(i - 1)
            add_squares(KD - 1)
            for n in range(KD):
                dve.wait_ge(*free_after(("out", n)))
            scale_x(1)
            name = ("routerT", 0)
            dve.wait_ge(*full_after(name))
            link(TT(out=m_p[:, :, :], in0=bank(name)[:, 0:NT * NE].rearrange("p (t e) -> p t e", e=NE),
                    in1=wide(rbias[:, :], 1, NT), op=ADD))
            link(V.tensor_reduce(m_col[:, 0:NT], m_p[:, :, :], AX.X, MAX))
            V.memset(small[:, 60:61], 0.0).then_inc(pair_free[pair(name)], 1)
            TT(out=m_p[:, :, :], in0=m_p[:, :, :], in1=wide(m_col[:, 0:NT], 2, NE), op=SUB).then_inc(s_r_max, 1)
            dve.wait_ge(s_r_exp, 1)
            link(V.tensor_reduce(m_col[:, 0:NT], m_p[:, :, :], AX.X, ADD))
            link(V.reciprocal(m_col[:, 8:8 + NT], m_col[:, 0:NT]))
            link(TT(out=m_p[:, :, :], in0=m_p[:, :, :], in1=wide(m_col[:, 8:8 + NT], 2, NE), op=MULT))

            def rank4(values, rank, cmp, cmp2):
                n = values.shape[1]
                other, own = wide(values, 2, 4), wide(values, 3, 4)
                ch(TT(out=cmp, in0=other, in1=own, op=ALU.is_gt))
                link(TT(out=cmp2, in0=other, in1=own, op=ALU.is_equal))
                link(TT(out=cmp2, in0=cmp2, in1=wide(m_left, 1, n), op=MULT))
                link(TT(out=cmp, in0=cmp, in1=cmp2, op=ADD))
                link(V.tensor_reduce(rank, cmp, AX.X, ADD))

            ch(V.memset(m_more[:, :, 1:NT], 1.0))
            ch(V.memset(m_more[:, :, 0:1], 0.0))
            dve.wait_ge(s_num, 1)
            link(TT(out=m_left, in0=wide(num[:, 0:4], 1, 4), in1=wide(num[:, 0:4], 2, 4), op=ALU.is_lt))
            fours = lambda v: v.rearrange("p t e -> p (t e)").rearrange("p (n e) -> p n e", e=4)
            rank4(fours(m_p), fours(m_rank), m_r4[0], m_r4[1])
            link(STT(out=m_gate[:, :, :], in0=m_rank[:, :, :], scalar=2.0, in1=m_p[:, :, :], op0=ALU.is_lt, op1=MULT))
            link(V.tensor_reduce(m_gs.rearrange("p t g -> p (t g)"), fours(m_gate), AX.X, ADD))
            dve.wait_ge(*free_after(("routerT", 0)))
            rank4(m_gs, m_gr, m_r4[0][:, 0:NT], m_r4[1][:, 0:NT])
            link(TS(m_gr[:, :, :], m_gr[:, :, :], 1.0, None, ALU.is_lt))
            link(TT(out=fours(m_gate), in0=fours(m_gate), in1=wide(m_gr.rearrange("p t g -> p (t g)"), 2, 4), op=MULT))
            STT(out=fours(m_sel), in0=fours(m_rank), scalar=2.0, in1=wide(m_gr.rearrange("p t g -> p (t g)"), 2, 4),
                op0=ALU.is_lt, op1=MULT).then_inc(s_sel, 1)
            dve.wait_ge(s_sel, 1)
            link(V.tensor_reduce(m_col[:, 0:NT], m_gate[:, :, :], AX.X, ADD))
            link(V.reciprocal(m_col[:, 8:8 + NT], m_col[:, 0:NT]))
            link(TT(out=m_gate[:, :, :], in0=m_gate[:, :, :], in1=wide(m_col[:, 8:8 + NT], 2, NE), op=MULT))
            name = ("pos", 0)
            dve.wait_ge(*full_after(name))
            ch(V.tensor_copy(m_tot[:, :, :], bank(name)[:, 512:512 + NT * NE].rearrange("p (t e) -> p e t", e=NE)))
            V.tensor_copy(m_t1[:, :, :], bank(name)[:, 0:NT * NE].rearrange("p (t e) -> p t e", e=NE)).then_inc(pair_free[pair(name)], 1)
            dve.wait_ge(*free_after(name))
            ch.sync()
            flat = lambda v: v.rearrange("p e t -> p (e t)")
            link(V.tensor_tensor_scan(flat(m_run), flat(m_more), flat(m_tot), 0.0, MULT, ADD))
            ch(V.tensor_copy(m_no[:, 0, :], m_run[:, :, NT - 1]))
            link(TT(out=m_t1[:, 1:NT, :], in0=m_t1[:, 1:NT, :],
                    in1=m_run[:, :, 0:NT - 1].rearrange("p e t -> p t e"), op=ADD))
            link(STT(out=m_c4[:, :, :], in0=wide(m_no[:, 0, :], 2, 4), scalar=1.0 / P,
                     in1=wide(num[:, 1:5], 1, NE), op0=MULT, op1=ALU.is_gt))
            link(V.tensor_reduce(m_no[:, 1, :], m_c4[:, :, :], AX.X, ADD))
            link(V.tensor_tensor_scan(m_no[:, 2, :], ones[:, 0:NE], m_no[:, 1, :], 0.0, MULT, ADD))
            link(TT(out=m_no[:, 3, :], in0=m_no[:, 2, :], in1=m_no[:, 1, :], op=SUB))
            link(TT(out=m_no[:, 3, :], in0=m_no[:, 3, :], in1=num[:, 0:NE], op=SUB))
            link(TS(m_no[:, 3, :], m_no[:, 3, :], float(NE - 1), float(P), ADD, MULT))
            link(STT(out=m_cg[:, :, :], in0=m_t1[:, :, :], scalar=float(P), in1=wide(m_no[:, 3, :], 1, NT),
                     op0=ALU.is_gt, op1=MULT))
            link(TT(out=m_t1[:, :, :], in0=m_t1[:, :, :], in1=m_cg[:, :, :], op=ADD))
            link(STT(out=m_t1[:, :, :], in0=wide(num[:, 0:NE], 1, NT), scalar=float(P), in1=m_t1[:, :, :], op0=MULT, op1=ADD))
            link(TT(out=m_t1[:, :, :], in0=m_t1[:, :, :], in1=m_sel[:, :, :], op=MULT))
            link(V.tensor_reduce(m_ab[:, 1, :], m_t1[:, :, :], AX.X, MAX))
            link(V.tensor_reduce(m_ab[:, 0, :], m_t1[:, :, :], AX.X, ADD))
            link(TT(out=m_ab[:, 0, :], in0=m_ab[:, 0, :], in1=m_ab[:, 1, :], op=SUB))
            TS(slot[:, :, :], m_ab[:, :, :], -1.0, None, ADD).then_inc(s_slot, 1)
            link(TT(out=m_cmp[:, :, :], in0=wide(m_no[:, 2, :], 1, MAX_OVER), in1=wide(num[:, 0:MAX_OVER], 2, NE), op=ALU.is_le))
            link(V.tensor_reduce(m_of[:, 0:MAX_OVER], m_cmp[:, :, :], AX.X, ADD))
            ch(V.tensor_copy(m_of[:, MAX_OVER:MAX_OVER + 1], m_no[:, 2, NE - 1:NE]))
            ch.sync()
            TS(table[:, 0:MAX_OVER + 1], m_of[:, 0:MAX_OVER + 1], float(NE - 1), None, MIN).then_inc(s_table, 1)
            for c in range(2):
                link(TT(out=m_cg[:, :, :], in0=m_t1[:, :, :], in1=wide(m_ab[:, c, :], 2, NE), op=ALU.is_equal))
                link(TT(out=m_cg[:, :, :], in0=m_cg[:, :, :], in1=m_gate[:, :, :], op=MULT))
                link(V.tensor_reduce(gw[:, c, :], m_cg[:, :, :], AX.X, ADD))
            name = ("slots", 0)
            dve.wait_ge(*full_after(name))
            V.tensor_copy(slot_tok[:, :], bank(name)[:, 0:NB]).then_inc(pair_free[pair(name)], 1)

            def transposed(b):
                dve.wait_ge(block_full[XG], b + 1)
                if b >= 2:
                    dve.wait_ge(block_full[GU], b - 1)
                V.tensor_copy(m_xgT[:, b % 2, :, :], ps[:, XG, :].rearrange("p (a b) -> p a b", a=KD)).then_inc(block_free[XG], 1)

            def hidden(b):
                dve.wait_ge(s_m_sg, b + 1)
                if b >= 2:
                    dve.wait_ge(block_full[HD], b - 1)
                TT(out=m_hid[:, b % 2, :], in0=ps[:, GU, 512:1024], in1=m_sg[:, b % 2, :], op=MULT).then_inc(s_hid, 1)
                dve.wait_ge(s_hid, b + 1)
                V.memset(small[:, 60:61], 0.0).then_inc(block_free[GU], 1)

            transposed(0)
            for b in range(NE):
                hidden(b)
                if b + 1 < NE:
                    transposed(b + 1)

            def over(b):
                transposed(b)
                hidden(b)

            dve.wait_ge(s_table, 1)
            over_blocks(dve, over)

            def final_norm(t):
                dve.wait_ge(s_x2, t + 1)
                dve.wait_ge(s_x2rs, t + 1)
                link(V.reciprocal(small[:, 24 + t:25 + t], small[:, 24 + t:25 + t]))
                STT(out=m_out[:, t, :], in0=m_x2[:, t, :], scalar=small[:, 24 + t:25 + t], in1=m_fw,
                    op0=MULT, op1=MULT).then_inc(s_out, 1)

            for t in range(NT):
                dve.wait_ge(s_yA, t + 1)
                dve.wait_ge(s_y_in[t], 32)
                link(STT(out=m_y[:, t, :], in0=m_yB[:, t, :], scalar=gw[:, 1, t:t + 1], in1=m_y[:, t, :],
                         op0=MULT, op1=ADD))
                link(TT(out=m_y[:, t, :], in0=m_y[:, t, :], in1=m_gt[min(t, 1)], op=MULT))
                if t == 0:
                    for u in range(NT):
                        dve.wait_ge(*free_after(("xrow", u)))
                TT(out=m_x2[:, t, :].rearrange("p (a b) -> p a b", a=KD), in0=m_y[:, t, :].rearrange("p (a b) -> p a b", a=KD),
                   in1=m_xr(t), op=ADD).then_inc(s_x2, 1)
                if t:
                    final_norm(t - 1)
            final_norm(NT - 1)


def build(nc, inputs):
    arrays, I = {}, {}
    for name, a in inputs.items():
        a = np.ascontiguousarray(a)
        arrays[f"in_{name}"] = a
        I[name] = nc.dram_tensor(f"in_{name}", a.shape, mybir.dt.from_np(a.dtype), kind="ExternalInput").ap()
    O = {}
    for name, shape in OUTS.items():
        O[name] = nc.dram_tensor(f"out_{name}", shape, F32, kind="ExternalOutput").ap()
    layer_program(nc, I, O)
    return arrays


OUTS = {"y_prompt": (1, CTX, D), "y_sample": (1, LAT, D), "new_gdn": (1, 1, 2, GH, P, P),
        "new_hgrn": (1, 1, 2, HH, HK, HK), "new_rg": (1, 1, 2, 256)}


def kernel(**inputs):
    import concourse.bacc as _bacc
    from concourse.bass_utils import run_bass_kernel_spmd as _run

    nc = _bacc.Bacc("TRN2", target_bir_lowering=False, num_devices=1)
    arrays = build(nc, inputs)
    r = _run(nc, [arrays], core_ids=[0])
    return tuple(r.results[0][f"out_{name}"] for name in OUTS)
```
